# Optimizing a Trainium2 kernel written in Bass

```python
import math
import jax
import jax.numpy as jnp
from jax import lax
import numpy as np
import jax, jax.numpy as jnp

D_MODEL = 1024
BATCH = 1
SEQ = 512
DEPTH = 2

GRID_W = 64
CTX_LEN = 256
N_MIXERS = 2
RMS_EPS = 1e-6

RW_HEAD = 64
RW_WIDTH = D_MODEL
RW_HEADS = RW_WIDTH // RW_HEAD
W_LORA = 64
A_LORA = 64
RW_IN_COLS = 4 * RW_WIDTH + 2 * (W_LORA + A_LORA)
RW_MIX_COLS = 3 * RW_WIDTH + 2 * (W_LORA + A_LORA)
GN_EPS = 64e-5

DA_HEADS = 8
DA_HEAD = 64
DA_VHEAD = 2 * DA_HEAD
DA_QW = DA_HEADS * 2 * DA_HEAD
DA_VW = DA_HEADS * DA_VHEAD
DA_GW = DA_VW
DA_IN_COLS = 2 * DA_QW + DA_VW + DA_GW
SUBLN_EPS = 1e-5
ROPE_THETA = 10000.0
ROPE_FREQS = DA_HEAD // 4
Q_BLOCK = 128

N_A = (DEPTH + 1) // 2
N_B = DEPTH // 2


def rms_norm(x, g, eps=RMS_EPS):
    xf = x.astype(jnp.float32)
    y = xf * lax.rsqrt(jnp.mean(xf * xf, axis=-1, keepdims=True) + eps)
    return (y * g.astype(jnp.float32)).astype(x.dtype)

def centred_token_shift(u, mu):
    prev = jnp.pad(u[:, :-1], ((0, 0), (1, 0), (0, 0)))
    nxt = jnp.pad(u[:, 1:], ((0, 0), (0, 1), (0, 0)))
    return u + mu * (0.5 * (prev + nxt) - u)

def rwkv7_streams(h, w_in, mu, w0, w2, a0, a2, k_k, k_a):
    B, T, _ = h.shape
    C = RW_WIDTH
    heads = lambda t: t.reshape(t.shape[:-1] + (RW_HEADS, RW_HEAD))
    proj = (h @ w_in).astype(jnp.float32)
    g = proj[..., 3 * C:4 * C]
    mixed = centred_token_shift(
        jnp.concatenate([proj[..., :3 * C], proj[..., 4 * C:]], axis=-1), mu.astype(jnp.float32))
    r, k, v = mixed[..., :C], mixed[..., C:2 * C], mixed[..., 2 * C:3 * C]
    lw = mixed[..., 3 * C:3 * C + 2 * W_LORA].reshape(B, T, 2, W_LORA)
    la = mixed[..., 3 * C + 2 * W_LORA:].reshape(B, T, 2, A_LORA)
    w_raw = w0 + jnp.einsum("btdr,drc->btdc", jnp.tanh(lw), w2)
    decay = jnp.exp(-jnp.exp(-jax.nn.softplus(-w_raw) - 0.5))
    a = jax.nn.sigmoid(a0 + jnp.einsum("btdr,drc->btdc", la, a2))
    kk = heads(k * k_k)
    kk = kk * lax.rsqrt(jnp.sum(kk * kk, axis=-1, keepdims=True) + 1e-12)
    kd = k[:, :, None, :] * (1.0 + (a - 1.0) * k_a)
    return heads(r), heads(v), kk, heads(decay), heads(a), heads(kd), g

def wkv_scan(r, w, k, v, kk, a, s0, reverse):
    xs = tuple(jnp.moveaxis(t, 1, 0) for t in (r, w, k, v, kk, a))

    def step(S, inp):
        r_t, w_t, k_t, v_t, kk_t, a_t = inp
        sa = jnp.einsum("bhvk,bhk->bhv", S, kk_t)
        S = (S * w_t[:, :, None, :]
             - sa[..., None] * (kk_t * a_t)[:, :, None, :]
             + v_t[..., None] * k_t[:, :, None, :])
        return S, jnp.einsum("bhvk,bhk->bhv", S, r_t)

    s_fin, o = lax.scan(step, s0, xs, reverse=reverse)
    return jnp.moveaxis(o, 0, 1), s_fin

def scan_direction(streams, d, s0, reverse):
    r, v, kk, decay, a, kd, _ = streams
    return wkv_scan(r, decay[:, :, d], kd[:, :, d], v, kk, a[:, :, d], s0, reverse)

def rwkv7_readout(o, streams, r_k, gn_g, gn_b, w_out, out_dtype):
    r, v, _, _, _, kd, g = streams
    B, T = o.shape[:2]
    mean = jnp.mean(o, axis=-1, keepdims=True)
    var = jnp.mean(jnp.square(o - mean), axis=-1, keepdims=True)
    y = ((o - mean) * lax.rsqrt(var + GN_EPS)).reshape(B, T, RW_WIDTH) * gn_g + gn_b
    bonus = jnp.sum(jnp.sum(r[:, :, None] * kd * r_k, axis=-1, keepdims=True) * v[:, :, None], axis=2)
    y = (y + bonus.reshape(B, T, RW_WIDTH)) * jax.nn.silu(g)
    return y.astype(out_dtype) @ w_out

def rwkv7_mixer(h, hc, w_in, mu, w0, w2, a0, a2, k_k, k_a, r_k, gn_g, gn_b, w_out, ctx_out):
    lat = rwkv7_streams(h, w_in, mu, w0, w2, a0, a2, k_k, k_a)
    con = rwkv7_streams(hc, w_in, mu, w0, w2, a0, a2, k_k, k_a)
    s0 = jnp.zeros((h.shape[0], RW_HEADS, RW_HEAD, RW_HEAD), jnp.float32)
    oc_f, sc_f = scan_direction(con, 0, s0, False)
    oc_b, sc_b = scan_direction(con, 1, s0, True)
    ol_f, _ = scan_direction(lat, 0, sc_f, False)
    ol_b, _ = scan_direction(lat, 1, sc_b, True)
    y = rwkv7_readout(ol_f + ol_b, lat, r_k, gn_g, gn_b, w_out, h.dtype)
    yc = rwkv7_readout(oc_f + oc_b, con, r_k, gn_g, gn_b, w_out, hc.dtype) if ctx_out else None
    return y, yc

def axial_rope_tables(rows):
    row_ids = jnp.repeat(jnp.arange(rows), GRID_W).astype(jnp.float32)
    col_ids = jnp.tile(jnp.arange(GRID_W), rows).astype(jnp.float32)
    inv_freq = ROPE_THETA ** (-jnp.arange(ROPE_FREQS, dtype=jnp.float32) / ROPE_FREQS)
    ang = jnp.stack([row_ids[:, None] * inv_freq, col_ids[:, None] * inv_freq], axis=1)
    return jnp.cos(ang), jnp.sin(ang)

def apply_axial_rope(x, cos, sin):
    xr = x.reshape(x.shape[:-1] + (2, 2, ROPE_FREQS))
    x1, x2 = xr[..., 0, :], xr[..., 1, :]
    c = cos[None, :, None, None].astype(x.dtype)
    s = sin[None, :, None, None].astype(x.dtype)
    out = jnp.stack([x1 * c - x2 * s, x2 * c + x1 * s], axis=-2)
    return out.reshape(x.shape)

def diff_attention_blocks(q, k_all, v_all, lam):
    B, T = q.shape[:2]
    nb = T // Q_BLOCK
    qb = jnp.moveaxis(q.reshape((B, nb, Q_BLOCK) + q.shape[2:]), 1, 0)
    scale = DA_HEAD ** -0.5

    def block(q_blk):
        s = jnp.einsum("bqhcd,bkhcd->bchqk", q_blk, k_all).astype(jnp.float32) * scale
        p = jax.nn.softmax(s, axis=-1)
        attn = p[:, 0] - lam * p[:, 1]
        return jnp.einsum("bhqk,bkhe->bqhe", attn.astype(v_all.dtype), v_all)

    o = lax.map(block, qb)
    return jnp.moveaxis(o, 0, 1).reshape(B, T, DA_HEADS, DA_VHEAD)

def diff_finish(o, g, subln, lam_init, w_out):
    B, T = o.shape[:2]
    y = rms_norm(o, subln, SUBLN_EPS) * (1.0 - lam_init)
    return (y.reshape(B, T, DA_VW) * jax.nn.silu(g)) @ w_out

def diff_mixer(h, hc, layer_idx, w_in, qn, kn, lam_vecs, subln, w_out, cos, sin, ctx_out):
    B, T, _ = h.shape
    Lc = hc.shape[1]
    lam_init = 0.8 - 0.6 * math.exp(-0.3 * layer_idx)
    lv = lam_vecs.astype(jnp.float32)
    lam = jnp.exp(jnp.sum(lv[0] * lv[1])) - jnp.exp(jnp.sum(lv[2] * lv[3])) + lam_init
    proj = h @ w_in
    q = apply_axial_rope(rms_norm(proj[..., :DA_QW].reshape(B, T, DA_HEADS, 2, DA_HEAD), qn), cos, sin)
    k = apply_axial_rope(rms_norm(proj[..., DA_QW:2 * DA_QW].reshape(B, T, DA_HEADS, 2, DA_HEAD), kn), cos, sin)
    v = proj[..., 2 * DA_QW:2 * DA_QW + DA_VW].reshape(B, T, DA_HEADS, DA_VHEAD)
    g = proj[..., 2 * DA_QW + DA_VW:]
    if ctx_out:
        pc = hc @ w_in
        kvc = pc[..., DA_QW:2 * DA_QW + DA_VW]
    else:
        kvc = hc @ w_in[:, DA_QW:2 * DA_QW + DA_VW]
    kc = rms_norm(kvc[..., :DA_QW].reshape(B, Lc, DA_HEADS, 2, DA_HEAD), kn)
    vc = kvc[..., DA_QW:].reshape(B, Lc, DA_HEADS, DA_VHEAD)
    k_all = jnp.concatenate([kc, k], axis=1)
    v_all = jnp.concatenate([vc, v], axis=1)
    y = diff_finish(diff_attention_blocks(q, k_all, v_all, lam), g, subln, lam_init, w_out)
    yc = None
    if ctx_out:
        qc = rms_norm(pc[..., :DA_QW].reshape(B, Lc, DA_HEADS, 2, DA_HEAD), qn)
        yc = diff_finish(diff_attention_blocks(qc, kc, vc, lam), pc[..., 2 * DA_QW + DA_VW:],
                         subln, lam_init, w_out)
    return y, yc

def first_inputs(seed: int = 0) -> dict:
    key = jax.random.key(seed)
    ks = jax.random.split(key, 26)
    f32 = jnp.float32
    nrm = lambda k, shape, s: jax.random.normal(k, shape, f32) * s
    D = D_MODEL
    return {
        "x": nrm(ks[0], (BATCH, SEQ, D), 1.0),
        "c": nrm(ks[1], (BATCH, D), 1.0),
        "ctx": nrm(ks[2], (BATCH, CTX_LEN, D), 1.0),
        "c_ctx": nrm(ks[3], (D,), 1.0),
        "ada_w": nrm(ks[4], (DEPTH, D, 3 * D), 0.5 * D ** -0.5),
        "ada_b": nrm(ks[5], (DEPTH, 3 * D), 0.02),
        "norm_g": 1.0 + nrm(ks[6], (DEPTH, D), 0.02),
        "rw_in": nrm(ks[7], (N_A, D, RW_IN_COLS), D ** -0.5),
        "rw_mu": jax.random.uniform(ks[8], (N_A, RW_MIX_COLS), f32),
        "rw_w0": jax.random.uniform(ks[9], (N_A, 2, RW_WIDTH), f32, minval=-6.0, maxval=-1.0),
        "rw_w2": nrm(ks[10], (N_A, 2, W_LORA, RW_WIDTH), 0.1 * W_LORA ** -0.5),
        "rw_a0": nrm(ks[11], (N_A, 2, RW_WIDTH), 0.1),
        "rw_a2": nrm(ks[12], (N_A, 2, A_LORA, RW_WIDTH), 0.1 * A_LORA ** -0.5),
        "rw_kk": 0.85 + nrm(ks[13], (N_A, RW_WIDTH), 0.05),
        "rw_ka": 1.0 + nrm(ks[14], (N_A, RW_WIDTH), 0.05),
        "rw_rk": nrm(ks[15], (N_A, RW_HEADS, RW_HEAD), 0.1),
        "rw_gn_g": 1.0 + nrm(ks[16], (N_A, RW_WIDTH), 0.02),
        "rw_gn_b": nrm(ks[17], (N_A, RW_WIDTH), 0.02),
        "rw_out": nrm(ks[18], (N_A, RW_WIDTH, D), RW_WIDTH ** -0.5),
        "da_in": nrm(ks[19], (N_B, D, DA_IN_COLS), D ** -0.5),
        "da_qn": 1.0 + nrm(ks[20], (N_B, DA_HEAD), 0.02),
        "da_kn": 1.0 + nrm(ks[21], (N_B, DA_HEAD), 0.02),
        "da_lam": nrm(ks[22], (N_B, 4, DA_HEAD), 0.1),
        "da_subln": 1.0 + nrm(ks[23], (N_B, DA_VHEAD), 0.02),
        "da_out": nrm(ks[24], (N_B, DA_VW, D), DA_VW ** -0.5),
    }

def first_block(x, c, ctx, c_ctx, ada_w, ada_b, norm_g, rw_in, rw_mu, rw_w0, rw_w2, rw_a0, rw_a2,
              rw_kk, rw_ka, rw_rk, rw_gn_g, rw_gn_b, rw_out, da_in, da_qn, da_kn, da_lam,
              da_subln, da_out):
    n_lat = x.shape[1]
    rows = n_lat // GRID_W
    cos, sin = axial_rope_tables(rows)
    xc = ctx
    for i in range(DEPTH):
        last = i == DEPTH - 1
        j = i // N_MIXERS
        mod = jax.nn.silu(c) @ ada_w[i] + ada_b[i]
        shift, scale, gate = jnp.split(mod[:, None, :], 3, axis=-1)
        modc = jax.nn.silu(c_ctx) @ ada_w[i] + ada_b[i]
        shift_c, scale_c, gate_c = jnp.split(modc, 3)
        h = rms_norm(x, norm_g[i]) * (1.0 + scale) + shift
        hc = rms_norm(xc, norm_g[i]) * (1.0 + scale_c) + shift_c
        if i % N_MIXERS == 0:
            y, yc = rwkv7_mixer(h, hc, rw_in[j], rw_mu[j], rw_w0[j], rw_w2[j], rw_a0[j], rw_a2[j],
                                rw_kk[j], rw_ka[j], rw_rk[j], rw_gn_g[j], rw_gn_b[j], rw_out[j],
                                not last)
        else:
            y, yc = diff_mixer(h, hc, i, da_in[j], da_qn[j], da_kn[j], da_lam[j], da_subln[j],
                               da_out[j], cos, sin, not last)
        x = x + gate * y
        if not last:
            xc = xc + gate_c * yc
    return x


HEAD_DIM = 64
N_HEADS_MOBA = 6
N_HEADS_DIL = 6
N_HEADS_MEM = 4
D_MOBA = N_HEADS_MOBA * HEAD_DIM
D_DIL = N_HEADS_DIL * HEAD_DIM
D_MEM = N_HEADS_MEM * HEAD_DIM
D_MIX = D_MOBA + D_DIL + D_MEM
D_IN = 4 * D_MOBA + 4 * D_DIL + 2 * D_MEM
N_MEM = 256
MOBA_BLOCK = 256
MOBA_TOPK = 3
MOBA_Q_CHUNK = 32
DIL_PATTERNS = ((128, 1), (512, 4), (2048, 16))
EPS = 1e-6


def rms_norm_2(x, g):
    xf = x.astype(jnp.float32)
    y = xf * lax.rsqrt(jnp.mean(xf * xf, axis=-1, keepdims=True) + EPS)
    return (y * g.astype(jnp.float32)).astype(x.dtype)

def rope(x):
    T = x.shape[2]
    half = HEAD_DIM // 2
    inv = ROPE_THETA ** (-jnp.arange(half, dtype=jnp.float32) / half)
    ang = jnp.arange(T, dtype=jnp.float32)[:, None] * inv[None, :]
    cos, sin = jnp.cos(ang), jnp.sin(ang)
    x1 = x[..., :half].astype(jnp.float32)
    x2 = x[..., half:].astype(jnp.float32)
    out = jnp.concatenate([x1 * cos - x2 * sin, x2 * cos + x1 * sin], axis=-1)
    return out.astype(x.dtype)

def to_heads(t, n):
    B, T, _ = t.shape
    return t.reshape(B, T, n, HEAD_DIM).transpose(0, 2, 1, 3)

def from_heads(t):
    B, H, T, dh = t.shape
    return t.transpose(0, 2, 1, 3).reshape(B, T, H * dh)

def moba_attention(q, k, v):
    B, H, T, dh = q.shape
    nb = -(-T // MOBA_BLOCK)
    Tp = nb * MOBA_BLOCK
    pad = ((0, 0), (0, 0), (0, Tp - T), (0, 0))
    q, k, v = jnp.pad(q, pad), jnp.pad(k, pad), jnp.pad(v, pad)
    kb = k.reshape(B, H, nb, MOBA_BLOCK, dh)
    vb = v.reshape(B, H, nb, MOBA_BLOCK, dh)
    k_mean = jnp.mean(kb.astype(jnp.float32), axis=3)
    topk = min(MOBA_TOPK, nb - 1)
    n_chunks = Tp // MOBA_Q_CHUNK
    q_chunks = q.reshape(B, H, n_chunks, MOBA_Q_CHUNK, dh).transpose(2, 0, 1, 3, 4)
    b_ix = jnp.arange(B)[:, None, None, None]
    h_ix = jnp.arange(H)[None, :, None, None]
    scale = dh ** -0.5

    def one_chunk(args):
        ci, qc = args
        start = ci * MOBA_Q_CHUNK
        c = start // MOBA_BLOCK
        q_pos = start + jnp.arange(MOBA_Q_CHUNK)
        k_pos = c * MOBA_BLOCK + jnp.arange(MOBA_BLOCK)
        own_k = lax.dynamic_index_in_dim(kb, c, axis=2, keepdims=False)
        own_v = lax.dynamic_index_in_dim(vb, c, axis=2, keepdims=False)
        s_own = jnp.einsum('bhqd,bhkd->bhqk', qc, own_k).astype(jnp.float32) * scale
        s_own = jnp.where(k_pos[None, :] <= q_pos[:, None], s_own, -jnp.inf)
        if topk == 0:
            p = jax.nn.softmax(s_own, axis=-1).astype(vb.dtype)
            return jnp.einsum('bhqk,bhkd->bhqd', p, own_v)
        gate = jnp.einsum('bhqd,bhnd->bhqn', qc.astype(jnp.float32), k_mean)
        gate = jnp.where(jnp.arange(nb) < c, gate, -jnp.inf)
        _, idx = lax.top_k(gate, topk)
        valid = idx < c
        sel_k = kb[b_ix, h_ix, idx]
        sel_v = vb[b_ix, h_ix, idx]
        s_sel = jnp.einsum('bhqd,bhqnkd->bhqnk', qc, sel_k).astype(jnp.float32) * scale
        s_sel = jnp.where(valid[..., None], s_sel, -jnp.inf)
        s_sel = s_sel.reshape(B, H, MOBA_Q_CHUNK, topk * MOBA_BLOCK)
        p = jax.nn.softmax(jnp.concatenate([s_own, s_sel], axis=-1), axis=-1).astype(vb.dtype)
        p_own = p[..., :MOBA_BLOCK]
        p_sel = p[..., MOBA_BLOCK:].reshape(B, H, MOBA_Q_CHUNK, topk, MOBA_BLOCK)
        return (jnp.einsum('bhqk,bhkd->bhqd', p_own, own_v)
                + jnp.einsum('bhqnk,bhqnkd->bhqd', p_sel, sel_v))

    out = lax.map(one_chunk, (jnp.arange(n_chunks, dtype=jnp.int32), q_chunks))
    return out.transpose(1, 2, 0, 3, 4).reshape(B, H, Tp, dh)[:, :, :T]

def dilated_attention(q, k, v):
    B, H, T, dh = q.shape
    scale = dh ** -0.5
    outs, lses = [], []
    for window, dil in DIL_PATTERNS:
        W = window // dil
        n = -(-T // (W * dil))
        L = n * W * dil
        pad = ((0, 0), (0, 0), (0, L - T), (0, 0))

        def split(t):
            return jnp.pad(t, pad).reshape(B, H, n, W, dil, dh).transpose(0, 1, 4, 2, 3, 5)

        qs, ks, vs = split(q), split(k), split(v)
        prev = ((0, 0), (0, 0), (0, 0), (1, 0), (0, 0), (0, 0))
        k_cat = jnp.concatenate([jnp.pad(ks, prev)[:, :, :, :-1], ks], axis=4)
        v_cat = jnp.concatenate([jnp.pad(vs, prev)[:, :, :, :-1], vs], axis=4)
        s = jnp.einsum('bhrnqd,bhrnkd->bhrnqk', qs, k_cat).astype(jnp.float32) * scale
        i = jnp.arange(W)[:, None]
        j = jnp.arange(2 * W)[None, :]
        band = (j >= i) & (j <= i + W)
        first = (jnp.arange(n)[:, None, None] > 0) | (j[None] >= W)
        s = jnp.where(band[None] & first, s, -jnp.inf)
        lse = jax.nn.logsumexp(s, axis=-1)
        p = jnp.exp(s - lse[..., None]).astype(v.dtype)
        o = jnp.einsum('bhrnqk,bhrnkd->bhrnqd', p, v_cat)
        outs.append(o.transpose(0, 1, 3, 4, 2, 5).reshape(B, H, L, dh)[:, :, :T])
        lses.append(lse.transpose(0, 1, 3, 4, 2).reshape(B, H, L)[:, :, :T])
    w = jax.nn.softmax(jnp.stack(lses, axis=0), axis=0)
    o_all = jnp.stack(outs, axis=0).astype(jnp.float32)
    return jnp.einsum('pbht,pbhtd->bhtd', w, o_all).astype(q.dtype)

def memory_attention(q, k, v):
    s = jnp.einsum('bhqd,bhkd->bhqk', q, k).astype(jnp.float32) * (HEAD_DIM ** -0.5)
    p = jax.nn.softmax(s, axis=-1).astype(v.dtype)
    return jnp.einsum('bhqk,bhkd->bhqd', p, v)

def hybrid_layer(x, mem, norm_g, w_in, w_out, mem_norm_g, w_mem_kv, qk_g):
    h = rms_norm_2(x, norm_g)
    proj = jnp.einsum('btd,de->bte', h, w_in)
    sizes = [D_MOBA] * 4 + [D_DIL] * 4 + [D_MEM] * 2
    cuts = [int(c) for c in np.cumsum(sizes)[:-1]]
    a_q, a_k, a_v, a_g, b_q, b_k, b_v, b_g, m_q, m_g = jnp.split(proj, cuts, axis=-1)

    qa = rope(rms_norm_2(to_heads(a_q, N_HEADS_MOBA), qk_g[0]))
    ka = rope(rms_norm_2(to_heads(a_k, N_HEADS_MOBA), qk_g[1]))
    oa = from_heads(moba_attention(qa, ka, to_heads(a_v, N_HEADS_MOBA)))

    qb = rope(rms_norm_2(to_heads(b_q, N_HEADS_DIL), qk_g[2]))
    kb = rope(rms_norm_2(to_heads(b_k, N_HEADS_DIL), qk_g[3]))
    ob = from_heads(dilated_attention(qb, kb, to_heads(b_v, N_HEADS_DIL)))

    mkv = jnp.einsum('bmd,de->bme', rms_norm_2(mem, mem_norm_g), w_mem_kv)
    m_k, m_v = jnp.split(mkv, 2, axis=-1)
    qm = rms_norm_2(to_heads(m_q, N_HEADS_MEM), qk_g[4])
    km = rms_norm_2(to_heads(m_k, N_HEADS_MEM), qk_g[5])
    om = from_heads(memory_attention(qm, km, to_heads(m_v, N_HEADS_MEM)))

    y = jnp.concatenate([oa * jax.nn.silu(a_g), ob * jax.nn.silu(b_g), om * jax.nn.silu(m_g)], axis=-1)
    return x + jnp.einsum('bte,ed->btd', y, w_out)

def second_inputs(seed: int = 0) -> dict:
    key = jax.random.key(seed)
    ks = jax.random.split(key, 10)
    f32 = jnp.float32
    x = jax.random.normal(ks[0], (BATCH, SEQ, D_MODEL), f32)
    mem = jax.random.normal(ks[1], (BATCH, N_MEM, D_MODEL), f32)
    norm_g = 1.0 + 0.02 * jax.random.normal(ks[2], (DEPTH, D_MODEL), f32)
    w_in = jax.random.normal(ks[3], (DEPTH, D_MODEL, D_IN), f32) * D_MODEL ** -0.5
    w_out = jax.random.normal(ks[4], (DEPTH, D_MIX, D_MODEL), f32) * (D_MIX ** -0.5) / math.sqrt(2 * DEPTH)
    mem_norm_g = 1.0 + 0.02 * jax.random.normal(ks[5], (DEPTH, D_MODEL), f32)
    w_mem_kv = jax.random.normal(ks[6], (DEPTH, D_MODEL, 2 * D_MEM), f32) * D_MODEL ** -0.5
    qk_g = 1.0 + 0.02 * jax.random.normal(ks[7], (DEPTH, 6, HEAD_DIM), f32)
    return {"x": x, "mem": mem, "norm_g": norm_g, "w_in": w_in, "w_out": w_out,
            "mem_norm_g": mem_norm_g, "w_mem_kv": w_mem_kv, "qk_g": qk_g}

def second_block(x, mem, norm_g, w_in, w_out, mem_norm_g, w_mem_kv, qk_g):
    for layer in range(DEPTH):
        x = hybrid_layer(x, mem, norm_g[layer], w_in[layer], w_out[layer],
                         mem_norm_g[layer], w_mem_kv[layer], qk_g[layer])
    return x


def setup_inputs(seed=0):
    out = dict(first_inputs(seed))
    for name, value in second_inputs(seed + 1).items():
        if name != "x":
            out[name + "_2"] = value
    return out


def reference(
    x, c, ctx, c_ctx, ada_w, ada_b, norm_g, rw_in, rw_mu, rw_w0, rw_w2, rw_a0, rw_a2, rw_kk,
    rw_ka, rw_rk, rw_gn_g, rw_gn_b, rw_out, da_in, da_qn, da_kn, da_lam, da_subln, da_out,
    mem_2, norm_g_2, w_in_2, w_out_2, mem_norm_g_2, w_mem_kv_2, qk_g_2,
):
    x = first_block(
        x, c, ctx, c_ctx, ada_w, ada_b, norm_g, rw_in, rw_mu, rw_w0, rw_w2, rw_a0, rw_a2, rw_kk,
        rw_ka, rw_rk, rw_gn_g, rw_gn_b, rw_out, da_in, da_qn, da_kn, da_lam, da_subln, da_out,
    )
    return second_block(
        x, mem_2, norm_g_2, w_in_2, w_out_2, mem_norm_g_2, w_mem_kv_2, qk_g_2,
    )


_drawn_inputs = setup_inputs


def setup_inputs(seed=0):
    import zlib

    import numpy as np

    out = dict(_drawn_inputs(seed))
    spreads = {}
    factors = {'norm_g': 6.221,
     'rw_w2': 8.0,
     'rw_a0': 7.242,
     'rw_a2': 7.408,
     'rw_gn_g': 45.395,
     'rw_gn_b': 42.481,
     'da_qn': 8.0,
     'da_kn': 8.0,
     'da_lam': 8.0,
     'da_subln': 64.0,
     'mem_2': 2.775,
     'norm_g_2': 8.0,
     'mem_norm_g_2': 25.204,
     'qk_g_2': 8.0}
    for name, (base, spread) in spreads.items():
        noise = np.random.default_rng([zlib.crc32(name.encode()), seed]).standard_normal(out[name].shape)
        drawn = base * np.exp(spread * noise) if base else spread * noise
        out[name] = jnp.asarray(drawn.astype(out[name].dtype))
    for name, factor in factors.items():
        out[name] = (out[name] * factor).astype(out[name].dtype)
    return out
```

```python
from contextlib import ExitStack
import math

import numpy as np

import concourse.bass as bass
from concourse import mybir

ALU = mybir.AluOpType
ACT = mybir.ActivationFunctionType
F32 = mybir.dt.float32
AX = mybir.AxisListType

NCTX, NLAT, NT = 256, 512, 768
NEG = -1.0e30
DECAY = math.exp(-0.5)
LAM_INIT = 0.8 - 0.6 * math.exp(-0.3)
NSLOT = 4

PCOLS = {}
_n = 0
for _name, _w in (("cs", 16), ("ada_b", 48), ("norm_g", 16), ("mu", 26), ("kk", 8), ("ka", 8), ("rk", 8),
                  ("gn_g", 8), ("gn_b", 8), ("a0", 16), ("qn", 1), ("kn", 1), ("subln", 1), ("ng2", 16),
                  ("mng2", 16), ("qkg", 12), ("lam", 256)):
    PCOLS[_name] = (_n, _w)
    _n += _w
NPAR = _n

CCOLS = {}
_n = 0
for _name, _w in (("ident", 128), ("ones", 128), ("blk", 128), ("eps", 8)):
    CCOLS[_name] = (_n, _w)
    _n += _w
NCON = _n
RCOLS = {"tri": (0, 512), "msk": (512, 512), "lvl": (1024, 2 * 6 * 128)}
NRC = 1024 + 1536
ACOLS = {"rot1": (0, 128), "rot2": (128, 128), "cos1": (256, 768), "sin1": (1024, 768)}
NAC = 1792
BCOLS = {"rot2": (0, 128), "cos2": (128, 512), "sin2": (640, 512), "mw1": (1152, 512), "mw2": (1664, 512)}
NBC = 2176


def constants():
    f = np.float32
    con = np.zeros((128, NCON), f)
    con[:, 0:128] = np.eye(128)
    con[:, 128:256] = 1.0
    i = np.arange(128)
    con[:, 256:384] = (i[:, None] // 64 == i[None] // 64)
    con[:, 384:392] = np.array([1e-6, 1e-5, 64e-5, 1e-12, 0, 0, 0, 0])[None]
    rc = np.zeros((128, NRC), f)
    j, t = i[:, None], i[None, :]
    same = (j // 64) == (t // 64)
    for d in range(2):
        incl = same & ((j <= t) if d == 0 else (j >= t))
        strict = same & ((j < t) if d == 0 else (j > t))
        rc[:, 256 * d:256 * d + 128] = -DECAY * incl
        rc[:, 256 * d + 128:256 * d + 256] = -DECAY * strict
        rc[:, 512 + 256 * d:512 + 256 * d + 128] = strict
        rc[:, 512 + 256 * d + 128:512 + 256 * d + 256] = incl
        for l in range(6):
            s = 1 << l
            b = (j // (2 * s)) == (t // (2 * s))
            jo, to = (j // s) % 2, (t // s) % 2
            m = b & ((jo == 0) & (to == 1) if d == 0 else (jo == 1) & (to == 0))
            rc[:, 1024 + (6 * d + l) * 128:1024 + (6 * d + l + 1) * 128] = m
    ac = np.zeros((128, NAC), f)
    inv = (np.float32(10000.0) ** (-np.arange(16, dtype=f) / f(16))).astype(f)
    tok = np.arange(512)
    rows, cols = (tok // 64).astype(f), (tok % 64).astype(f)
    ac[:, 256:1024] = 1.0
    for p in range(128):
        c = p % 64
        ax, half, fr = c // 32, (c // 16) % 2, c % 16
        ang = ((rows if ax == 0 else cols) * inv[fr]).astype(f)
        ac[p, 256 + 256:256 + 768] = np.cos(ang)
        ac[p, 1024 + 256:1024 + 768] = np.sin(ang)
        partner = p + 16 if half == 0 else p - 16
        ac[partner, p] = -1.0 if half == 0 else 1.0
    bc = np.zeros((128, NBC), f)
    inv = (np.float32(10000.0) ** (-np.arange(32, dtype=f) / f(32))).astype(f)
    for p in range(128):
        c = p % 64
        half, fr = c // 32, c % 32
        ang = (tok.astype(f) * inv[fr]).astype(f)
        bc[p, 128:640] = np.cos(ang)
        bc[p, 640:1152] = np.sin(ang)
        partner = p + 32 if half == 0 else p - 32
        bc[partner, p] = -1.0 if half == 0 else 1.0
    u = np.arange(512)
    dist = i[:, None] - (u[None] - 384)
    bc[:, 1152:1664] = np.where(dist >= 0, 0.0, NEG)
    mult = (dist <= 128).astype(f) + (dist % 4 == 0) + (dist % 16 == 0)
    ok = (dist >= 0) & (mult > 0)
    bc[:, 1664:2176] = np.where(ok, 8.0 * np.log(np.maximum(mult, 1.0)), NEG)
    return con, rc, ac, bc


class Prog:

    def __init__(self, nc, ctx):
        self.nc, self.ctx = nc, ctx
        self.q = {e: [] for e in ("pe", "act", "dve", "pool", "sp")}
        self.sem = {e: ctx.enter_context(nc.semaphore("s_" + e)) for e in self.q}
        self.n = {e: 0 for e in self.q}
        self.seen = {e: {} for e in self.q}
        self.slots = {}

    def wait(self, e, *toks):
        for t in toks:
            if t is None:
                continue
            if isinstance(t, list):
                self.wait(e, *t)
                continue
            s, v = t
            if self.seen[e].get(id(s), 0) < v:
                self.seen[e][id(s)] = v
                self.q[e].append(lambda eng, s=s, v=v: eng.wait_ge(s, v))

    def op(self, e, fn, *toks):
        self.wait(e, *toks)
        self.n[e] += 1
        s = self.sem[e]
        self.q[e].append(lambda eng: fn(eng).then_inc(s, 1))
        return (s, self.n[e])

    def quiet(self, e, fn, *toks):
        self.wait(e, *toks)
        self.q[e].append(fn)

    def dma(self, slot, dst, src, *toks, e="sp"):
        self.wait(e, *toks)
        if slot not in self.slots:
            self.slots[slot] = [self.ctx.enter_context(self.nc.semaphore("d_" + slot)), 0]
        r = self.slots[slot]
        r[1] += 16
        self.q[e].append(lambda eng, s=r[0]: eng.dma_start(dst, src).then_inc(s, 16))
        return (r[0], r[1])

    def last(self, e):
        return (self.sem[e], self.n[e]) if self.n[e] else None

    def play(self, e, eng):
        for f in self.q[e]:
            f(eng)


def build(nc, T):
    with ExitStack() as ctx:
        P = Prog(nc, ctx)
        body(nc, ctx, P, T)
        block = ctx.enter_context(nc.Block())

        @block.sync
        def _(e):
            P.play("sp", e)

        @block.gpsimd
        def _(e):
            P.play("pool", e)

        @block.scalar
        def _(e):
            P.play("act", e)

        @block.vector
        def _(e):
            P.play("dve", e)

        @block.tensor
        def _(e):
            P.play("pe", e)


def body(nc, ctx, P, T):
    def sb(c, name, cols):
        return c.enter_context(nc.sbuf_tensor(name, [128] + list(cols), F32))

    def pe(fn, *t):
        return P.op("pe", fn, *t)

    def act(out, in_, f, *t, scale=1.0, bias=0.0, accum=None):
        if accum is None:
            return P.op("act", lambda e: e.activation(out, in_, f, bias=bias, scale=scale), *t)
        return P.op("act", lambda e: e.activation(out, in_, f, bias=bias, scale=scale, accum_out=accum), *t)

    def copy(e, out, in_, *t):
        if e == "act":
            return P.op("act", lambda g: g.activation(out, in_, ACT.Copy), *t)
        return P.op(e, lambda g: g.tensor_copy(out, in_), *t)

    def tt(e, out, a, b, o, *t):
        return P.op(e, lambda g: g.tensor_tensor(out, a, b, o), *t)

    def ts(e, out, a, s1, s2, o0, o1, *t):
        if o1 is None:
            return P.op(e, lambda g: g.tensor_scalar(out, a, s1, None, o0), *t)
        return P.op(e, lambda g: g.tensor_scalar(out, a, s1, s2, o0, o1), *t)

    def stt(out, a, s, b, o0, o1, *t):
        return P.op("dve", lambda g: g.scalar_tensor_tensor(out=out, in0=a, scalar=s, in1=b, op0=o0, op1=o1), *t)

    psum = ctx.enter_context(nc.psum_tensor("ps", [128, 8, 512], F32))
    bank_free = [[] for _ in range(8)]
    turn = [0]

    def bank():
        i = turn[0] % 8
        turn[0] += 1
        return i

    def bank2():
        turn[0] += turn[0] % 2
        i = turn[0] % 8
        turn[0] += 2
        return i

    def mms(lst, *toks, skip=False):
        P.wait("pe", *toks)
        for k, (o, l, r, st, sp_) in enumerate(lst):
            f = lambda e, o=o, l=l, r=r, st=st, sp_=sp_: e.matmul(o, l, r, start=st, stop=sp_, skip_group_check=skip)
            if k == len(lst) - 1:
                return P.op("pe", f)
            P.quiet("pe", f)

    con = sb(ctx, "con", [NCON])
    par = sb(ctx, "par", [NPAR])
    t_con = P.dma("con", con[:, :], T["con"])
    t_par = P.dma("par", par[:, :], T["par"])
    P.t_in = [t_con, t_par]

    def C(name, a=0, n=None):
        o, w = CCOLS[name]
        return con[:, o + a:o + (w if n is None else a + n)]

    def Q(name, a=0, n=None):
        o, w = PCOLS[name]
        return par[:, o + a:o + (w if n is None else a + n)]

    ident, ones, blk = C("ident"), C("ones"), C("blk")
    EPS = {v: C("eps", k, 1) for k, v in enumerate((1e-6, 1e-5, 64e-5, 1e-12))}

    def transposes(lst, *toks):
        P.wait("pe", *toks)
        for k, (o, i) in enumerate(lst):
            f = lambda e, o=o, i=i: e.transpose(o, i, ident)
            if k == len(lst) - 1:
                return P.op("pe", f)
            P.quiet("pe", f)

    wring = sb(ctx, "wring", [NSLOT, 8, 128])
    wfree = [None] * NSLOT
    wn = [0]

    def wload(src):
        i = wn[0] % NSLOT
        wn[0] += 1
        return i, P.dma(f"w{i}", wring[:, i, :, :], src, wfree[i])

    xres = T["x1"]
    sm = sb(ctx, "sm", [160])
    modc = sb(ctx, "modc", [24, 2])
    s0 = sb(ctx, "s0", [8, 2])
    AB = sb(ctx, "AB", [8, 2])
    t_cs = act(s0[:, :, :], Q("cs").rearrange("p (k s) -> p k s", s=2), ACT.Silu, t_par)

    def silu_tok():
        return t_cs

    def modulation(layer, *toks):
        last = None
        i = bank()
        t = None
        for m in range(24):
            w, tw = wload(T["ada"][layer, m])
            t = mms([(psum[:, i, 2 * m:2 * m + 2], wring[:, w, k, :], s0[:, k, :], k == 0, k == 7)
                     for k in range(8)], tw, t_cs, bank_free[i] if m == 0 else None, t_con)
            wfree[w] = t
        ab = Q("ada_b", 24 * layer, 24).unsqueeze(2).to_broadcast([128, 24, 2])
        t1 = tt("dve", modc[:, :, :], psum[:, i, 0:48].rearrange("p (m s) -> p m s", s=2), ab, ALU.add,
                t, t_par, *toks)
        bank_free[i] = [t1]
        t2 = ts("dve", AB[:, :, :], modc[:, 8:16, :], 1.0, None, ALU.add, None, t1)
        g = Q("norm_g", 8 * layer, 8).unsqueeze(2).to_broadcast([128, 8, 2])
        t3 = tt("dve", AB[:, :, :], AB[:, :, :], g, ALU.mult, t2)
        return t3

    def rstd(src_sq, widths, R, lhs, eps, n, t_sq, *free):
        out = []
        for (a, b) in widths:
            i = bank()
            t = mms([(psum[:, i, 0:b - a], lhs, s[:, a:b], k == 0, k == len(src_sq) - 1)
                     for k, s in enumerate(src_sq)], t_sq, bank_free[i], t_con)
            t = act(R[:, a:b], psum[:, i, 0:b - a], ACT.Ln, t, *free, scale=1.0 / n, bias=EPS[eps])
            bank_free[i] = [t]
            out.append(act(R[:, a:b], R[:, a:b], ACT.Exp, t, scale=-0.5))
        return out

    def spans(W):
        return [(0, 256), (256, 768)] if W == 768 else ([(0, 512)] if W == 512 else [(0, 256)])

    def normed(c, xT, W, hT, A, B, t_x, t_ab, tag, streams, *free):
        R = sb(c, "R" + tag, [W])
        tq = act(hT[:, :, :], xT[:, :, :], ACT.Square, t_x, *free)
        tr = rstd([hT[:, k, :] for k in range(8)], spans(W), R, ones, 1e-6, 1024.0, tq)
        t_pe = P.last("pe")
        last = []
        for k in range(8):
            for a, b, s in streams:
                t = stt(hT[:, k, a:b], xT[:, k, a:b], A(k, s), R[:, a:b], ALU.mult, ALU.mult, tr, t_ab, t_pe)
                if B is not None:
                    t = act(hT[:, k, a:b], hT[:, k, a:b], ACT.Identity, t, bias=B(k, s))
            last.append(t)
        return last

    def proj_cm(wsrc, hT, W, t_h, K=8):
        w, tw = wload(wsrc)
        res = []
        t = None
        for a, b in spans(W):
            i = bank()
            t = mms([(psum[:, i, 0:b - a], wring[:, w, k, :], hT[:, k, a:b], k == 0, k == K - 1) for k in range(K)],
                    tw, t_h, bank_free[i])
            res.append((i, a, b))
        wfree[w] = t
        return res, t

    def proj_tm(wsrc, hT, W, t_h, dst, e, *free):
        w, tw = wload(wsrc)
        t = None
        outs = []
        for n0 in range(0, W // 128, 4):
            n1 = min(W // 128, n0 + 4)
            i = bank()
            P.wait("pe", bank_free[i])
            for n in range(n0, n1):
                t = mms([(psum[:, i, 128 * (n - n0):128 * (n - n0) + 128], hT[:, k, 128 * n:128 * n + 128],
                          wring[:, w, k, :], k == 0, k == 7) for k in range(8)], tw, t_h)
            tc = copy(e, dst[:, n0:n1, :], psum[:, i, 0:128 * (n1 - n0)].rearrange("p (n c) -> p n c", c=128), t, *free)
            bank_free[i] = [tc]
            outs.append(tc)
        wfree[w] = t
        return outs

    def barrier():
        toks = [P.last(e) for e in ("pe", "act", "dve", "pool")]
        for e in P.q:
            P.wait(e, *toks)

    c0 = ExitStack()
    hT = sb(c0, "hT", [8, NT])
    kit = Kit()
    kit.sb = sb
    kit.act = act
    kit.copy = copy
    kit.tt = tt
    kit.ts = ts
    kit.stt = stt
    kit.mms = mms
    kit.psum = psum
    kit.bank = bank
    kit.bank2 = bank2
    kit.bank_free = bank_free
    kit.wload = wload
    kit.wfree = wfree
    kit.wring = wring
    kit.C = C
    kit.Q = Q
    kit.ident = ident
    kit.ones = ones
    kit.blk = blk
    kit.hT = hT
    kit.modc = modc
    kit.AB = AB
    kit.transposes = transposes
    kit.rstd = rstd
    kit.spans = spans
    kit.proj_cm = proj_cm
    kit.proj_tm = proj_tm
    kit.barrier = barrier
    kit.t_con = t_con
    kit.t_par = t_par
    kit.modulation = modulation
    kit.normed = normed
    kit.sm = sm
    kit.ctx = ctx
    time_mix(nc, P, T, kit)
    c0.close()
    diff_layer(nc, P, T, kit)
    second_block(nc, P, T, kit)


class Kit:
    pass


def time_mix(nc, P, T, g_):
    sb, act, copy, tt, ts, stt, mms, psum = g_.sb, g_.act, g_.copy, g_.tt, g_.ts, g_.stt, g_.mms, g_.psum
    bank, bank_free, wload, wfree, wring, C, Q = g_.bank, g_.bank_free, g_.wload, g_.wfree, g_.wring, g_.C, g_.Q
    ident, blk, hT, modc, AB = g_.ident, g_.blk, g_.hT, g_.modc, g_.AB
    transposes, rstd, spans, proj_cm, barrier = g_.transposes, g_.rstd, g_.spans, g_.proj_cm, g_.barrier
    t_con, t_par = g_.t_con, g_.t_par

    t_ab = g_.modulation(0)
    cx = ExitStack()
    xT = sb(cx, "xT0", [8, NT])
    t_x = P.dma("x", xT[:, :, :], T["x"])
    A = lambda k, s: AB[:, k, s:s + 1]
    B = lambda k, s: modc[:, k, s:s + 1]
    t_h = g_.normed(cx, xT, NT, hT, A, B, t_x, t_ab, "0", [(0, 256, 1), (256, 768, 0)])
    t_h = t_h + [P.last("act"), P.last("dve")]
    barrier()
    cx.close()

    c = ExitStack()
    rc = sb(c, "rc", [NRC])
    t_rc = P.dma("rc", rc[:, :], T["rc"], P.last("dve"), P.last("act"))
    TRI = lambda d: rc[:, 256 * d:256 * d + 256]
    MSK = lambda d: rc[:, 512 + 256 * d:512 + 256 * d + 256]
    LVL = lambda d, l: rc[:, 1024 + (6 * d + l) * 128:1024 + (6 * d + l + 1) * 128]
    tl = sb(c, "tl", [NT])
    la = sb(c, "la", [NT])
    kT = sb(c, "kT", [2, NT])
    rT = sb(c, "rT", [2, NT])
    vT = sb(c, "vT", [2, NT])
    kkT = sb(c, "kkT", [2, NT])
    bT = sb(c, "bT", [2, 2, NT])
    kdT = sb(c, "kdT", [2, 2, NT])
    sg = sb(c, "sg", [2, 6, 256])
    oT = sb(c, "oT", [2, NT])
    lw2 = sb(c, "lw2", [4, 256])
    w0b = sb(c, "w0b", [2, 256])
    omu = sb(c, "omu", [2, 26])
    tr = sb(c, "tr", [2, 4608])
    S = sb(c, "S", [2, 2, 2, 128])

    keep = sb(c, "keep", [2, 2816])
    K_ = {}
    for d in range(2):
        o = 0
        for nm, w in (("P", 256), ("rho", 256), ("Lb", 512), ("Lk", 512), ("kt", 256), ("bt", 256), ("vt", 256),
                      ("W1", 256), ("W2", 256)):
            K_[nm, d] = keep[:, d, o:o + w]
            o += w
    Ut = sb(c, "Ut", [2, 256])
    t_mu1 = ts("dve", omu[:, 0, :], Q("mu"), -1.0, 1.0, ALU.mult, ALU.add, t_par)
    t_mu2 = ts("dve", omu[:, 1, :], Q("mu"), 0.5, None, ALU.mult, None)
    t_z = P.op("dve", lambda e: e.memset(S[:, :, :, :, :], 0.0))
    pad = [tr[:, i, 0:771] for i in range(2)]
    um = [tr[:, i, 1024:1024 + 769] for i in range(2)]
    ss = [tr[:, i, 2048:2048 + 769] for i in range(2)]
    nmix = [0]
    st = {"padfree": [None, None], "zero": [None, None]}

    def zero_pads():
        for i in range(2):
            for cc in (0, 257, 770):
                t = P.op("pool", lambda e, i=i, cc=cc: e.memset(pad[i][:, cc:cc + 1], 0.0), P.last("pe"), P.last("dve"), P.last("act"))
            st["zero"][i] = t

    def mix(wsrc, mucol, dst, f=None):
        i = nmix[0] % 2
        nmix[0] += 1
        res, t = proj_cm(wsrc, hT, NT, t_h)
        for (b, a, e_) in res:
            o = 1 if a == 0 else 2
            tp = copy("act", pad[i][:, a + o:e_ + o], psum[:, b, 0:e_ - a], t, st["zero"][i], st["padfree"][i])
            bank_free[b] = [tp]
        tu = act(um[i], pad[i][:, 1:770], ACT.Copy, tp, t_mu1, scale=omu[:, 0, mucol:mucol + 1])
        t1 = tt("dve", ss[i], pad[i][:, 0:769], pad[i][:, 2:771], ALU.add, tp)
        last = None
        for a, e_, o in ((0, 256, 0), (256, 768, 1)):
            last = stt(dst[:, a:e_], ss[i][:, a + o:e_ + o], omu[:, 1, mucol:mucol + 1], um[i][:, a + o:e_ + o],
                       ALU.mult, ALU.add, t1, tu, t_mu2)
        st["padfree"][i] = last
        return last

    zero_pads()
    t_lw = mix(T["rw_in"][32], 24, tl)
    t_tl = act(tl[:, :], tl[:, :], ACT.Tanh, t_lw)
    t_la = mix(T["rw_in"][33], 25, la)

    F_ = [0, 1, 2, 3, 4, 5]
    B_ = [1, 0, 5, 4, 3, 2]
    t_y = []
    hl = [(j, p) for j in range(2) for p in range(2)]
    t_end = None
    for g in range(4):
        tw2 = P.dma("lw2", lw2[:, :, :], T["lw2"][g], t_end)
        tw0 = P.dma("w0b", w0b[:, :, :], T["w0b"][g], t_end)
        if g:
            barrier()
            zero_pads()
        tk = [mix(T["rw_in"][8 + 2 * g + p], 8 + 2 * g + p, kT[:, p, :]) for p in range(2)]
        sq = kdT[:, 0, :, :]
        for p in range(2):
            col = Q("kk", 2 * g + p, 1)
            t = ts("dve", kkT[:, p, :], kT[:, p, :], col, None, ALU.mult, None, tk[p])
            tq = act(sq[:, p, :], kkT[:, p, :], ACT.Square, t)
            t = rstd([sq[:, p, :]], spans(NT), kdT[:, 1, p, :], blk, 1e-12, 1.0, tq)
            t_kk = tt("dve", kkT[:, p, :], kkT[:, p, :], kdT[:, 1, p, :], ALU.mult, t)
        trr = [mix(T["rw_in"][2 * g + p], 2 * g + p, rT[:, p, :]) for p in range(2)]
        tv = [mix(T["rw_in"][16 + 2 * g + p], 16 + 2 * g + p, vT[:, p, :]) for p in range(2)]
        for d in range(2):
            for p in range(2):
                for a, b in spans(NT):
                    i = bank()
                    t = mms([(psum[:, i, 0:b - a], lw2[:, 2 + d, 128 * p:128 * p + 128], la[:, a:b], True, True)],
                            tw2, t_la, bank_free[i])
                    ta = act(bT[:, d, p, a:b], psum[:, i, 0:b - a], ACT.Sigmoid, t,
                             bias=Q("a0", 8 * d + 2 * g + p, 1))
                    bank_free[i] = [ta]
            for n in range(0, 6, 2):
                i = bank()
                P.wait("pe", bank_free[i])
                for q in range(2):
                    t = mms([(psum[:, i, 256 * q:256 * q + 256], tl[:, 128 * (n + q):128 * (n + q) + 128],
                              lw2[:, d, :], True, True)], tw2, t_tl)
                t = tt("dve", sg[:, d, n:n + 2, :], psum[:, i, :].rearrange("p (q c) -> p q c", q=2),
                       w0b[:, d, :].unsqueeze(1).to_broadcast([128, 2, 256]), ALU.add, t, tw0)
                bank_free[i] = [t]
                t_sg = act(sg[:, d, n:n + 2, :], sg[:, d, n:n + 2, :], ACT.Sigmoid, t)
            for p in range(2):
                t = ts("dve", kdT[:, d, p, :], bT[:, d, p, :], -1.0, Q("ka", 2 * g + p, 1), ALU.add, ALU.mult,
                       ta, t_kk)
                t_kd = stt(kdT[:, d, p, :], kdT[:, d, p, :], 1.0, kT[:, p, :], ALU.add, ALU.mult, t)
                t_b = stt(bT[:, d, p, :], bT[:, d, p, :], -1.0, kkT[:, p, :], ALU.mult, ALU.mult, ta)
        t_str = [t_kd, t_b, P.last("dve"), P.last("act"), P.last("pe")]
        t_chain = {0: None, 1: None}
        s_cur = {0: 0, 1: 0}
        t_s = {}
        if g:
            t_z = P.op("dve", lambda e: e.memset(S[:, :, :, :, :], 0.0), P.last("pe"))
        t_s = {0: t_z, 1: t_z}
        t_o = []
        P.wait("pool", *t_str)
        for m in range(6):
            tile = (F_[m], B_[m])
            x = {}
            pw = [P.last("pe"), P.last("dve"), P.last("act"), P.last("pool")]
            for d in range(2):
                tok = slice(128 * tile[d], 128 * tile[d] + 128)
                o = [0]

                def cut(w):
                    o[0] += w
                    return tr[:, d, o[0] - w:o[0]]

                Pinv, AL = cut(256), cut(256)
                AR = cut(512).rearrange("p (q s t) -> p q s t", q=2, s=2)
                be, ka = cut(256), cut(256)
                LA, LK = cut(512), None
                NTb = cut(512)
                D, E, Y = cut(512), cut(512), cut(512)
                at = Pinv
                Y0 = AL
                b2 = lambda ap: ap.rearrange("p (q t) -> p q t", q=2)
                i = bank()
                t = mms([(psum[:, i, 256 * p:256 * p + 256], sg[:, d, tile[d], 128 * p:128 * p + 128], TRI(d),
                          True, True) for p in range(2)], t_sg, t_rc, bank_free[i])
                cum = psum[:, i, :].rearrange("p (q s t) -> p q s t", q=2, s=2)
                t1 = act(b2(K_["P", d]), cum[:, :, 0, :], ACT.Exp, t, *pw)
                t2 = act(b2(Pinv), cum[:, :, 0, :], ACT.Exp, scale=-1.0)
                t3 = act(b2(AL), cum[:, :, 1, :], ACT.Exp)
                bank_free[i] = [t3]
                ta1 = tt("dve", AR[:, :, 1, :], b2(K_["P", d]), rT[:, :, tok], ALU.mult, t1, *pw)
                ta2 = tt("dve", AR[:, :, 0, :], b2(AL), kkT[:, :, tok], ALU.mult, t3)
                tb = tt("pool", b2(be), b2(Pinv), bT[:, d, :, tok], ALU.mult, t2, *pw)
                tk_ = tt("pool", b2(ka), b2(Pinv), kdT[:, d, :, tok], ALU.mult)
                tro = copy("pool", b2(K_["rho", d]), AR[:, :, 1, :], ta1)
                i = bank()
                t = transposes([(psum[:, i, 128 * p:128 * p + 128], b2(be)[:, p, :]) for p in range(2)] +
                               [(psum[:, i, 256 + 128 * p:384 + 128 * p], b2(ka)[:, p, :]) for p in range(2)],
                               tb, tk_, bank_free[i])
                t4 = copy("act", K_["bt", d], psum[:, i, 0:256], t)
                t5 = copy("act", K_["kt", d], psum[:, i, 256:512])
                bank_free[i] = [t5]
                i = bank()
                t = transposes([(psum[:, i, 128 * p:128 * p + 128], AR[:, p, 0, :]) for p in range(2)] +
                               [(psum[:, i, 256 + 128 * p:384 + 128 * p], vT[:, p, tok]) for p in range(2)],
                               ta2, bank_free[i])
                t6 = copy("act", at, psum[:, i, 0:256], t, tk_)
                t7 = copy("act", K_["vt", d], psum[:, i, 256:512])
                bank_free[i] = [t7]
                msk = MSK(d).rearrange("p (s t) -> p s t", s=2)
                LKt = Y.rearrange("p (h t) -> p h t", h=4)
                for (src, which) in ((be, 0), (ka, 1)):
                    for j in range(2):
                        i = bank()
                        t = mms([(psum[:, i, 256 * p:256 * p + 256], b2(src)[64 * j:64 * j + 64, p, :],
                                  AR[64 * j:64 * j + 64, p, :, :], True, True) for p in range(2)],
                                ta1, ta2, bank_free[i])
                        pv = psum[:, i, :].rearrange("p (q s t) -> p q s t", q=2, s=2)
                        strict = (LA if which == 0 else Y).rearrange("p (h t) -> p h t", h=4)[:, 2 * j:2 * j + 2, :]
                        incl = K_["Lb" if which == 0 else "Lk", d].rearrange("p (h t) -> p h t", h=4)[:, 2 * j:2 * j + 2, :]
                        t = tt("dve", strict, pv[:, :, 0, :], msk[:, 0, :].unsqueeze(1).to_broadcast([128, 2, 128]),
                               ALU.mult, t)
                        t_L = tt("dve", incl, pv[:, :, 1, :], msk[:, 1, :].unsqueeze(1).to_broadcast([128, 2, 128]),
                                 ALU.mult)
                        bank_free[i] = [t_L]
                        if which == 0:
                            t_LA = t_L
                i = bank()
                t = mms([(psum[:, i, 64 * (2 * p + j):64 * (2 * p + j) + 64], Y[:, 128 * (2 * j + p):128 * (2 * j + p) + 128],
                          K_["vt", d][:, 64 * (2 * p + j):64 * (2 * p + j) + 64], True, True) for j, p in hl],
                        t_L, t7, bank_free[i])
                t_y0 = copy("dve", Y0, psum[:, i, 0:256], t)
                bank_free[i] = [t_y0]
                v4 = lambda ap: ap.rearrange("p (h t) -> p h t", h=4)
                lv = lambda l: LVL(d, l).unsqueeze(1).to_broadcast([128, 4, 128])
                idb = ident.unsqueeze(1).to_broadcast([128, 4, 128])
                t = tt("dve", v4(E), v4(LA), lv(0), ALU.mult, t_LA)
                t_e = tt("dve", v4(E), v4(E), idb, ALU.add, t)
                i = bank()
                t = transposes([(psum[:, i, 128 * h:128 * h + 128], E[:, 128 * h:128 * h + 128]) for h in range(4)],
                               t_e, bank_free[i])
                t_d = copy("act", D, psum[:, i, :], t)
                bank_free[i] = [t_d]
                t_n = tt("pool", v4(NTb), v4(LA), lv(1), ALU.mult, t_LA)
                x[d] = dict(D=D, E=E, Y=Y, LA=LA, NTb=NTb, t_e=t_e, t_d=t_d, t_n=t_n, at=at, Y0=Y0, t_y0=t_y0,
                            v4=v4, lv=lv, t6=t6, tok=tok)
            hs = lambda ap, h: ap[:, 128 * h:128 * h + 128]
            for l in range(1, 6):
                for d in range(2):
                    X = x[d]
                    i = bank()
                    t = mms([(psum[:, i, 128 * h:128 * h + 128], hs(X["NTb"], h), hs(X["D"], h), True, True)
                             for h in range(4)], X["t_n"], X["t_d"], bank_free[i])
                    ty = copy("act", X["Y"], psum[:, i, :], t)
                    bank_free[i] = [ty]
                    if l < 5:
                        X["t_n"] = tt("pool", X["v4"](X["NTb"]), X["v4"](X["LA"]), LVL(d, l + 1).unsqueeze(1).to_broadcast([128, 4, 128]), ALU.mult, t)
                    X["ty"] = ty
                for d in range(2):
                    X = x[d]
                    i = bank()
                    te = mms([(psum[:, i, 128 * h:128 * h + 128], hs(X["Y"], h), hs(X["E"], h), True, True)
                              for h in range(4)], X["ty"], X["t_e"], bank_free[i])
                    if l < 5:
                        i2 = bank()
                        td = mms([(psum[:, i2, 128 * h:128 * h + 128], hs(X["E"], h), hs(X["Y"], h), True, True)
                                  for h in range(4)], bank_free[i2])
                        X["t_d"] = tt("dve", X["D"], X["D"], psum[:, i2, :], ALU.add, td)
                        bank_free[i2] = [X["t_d"]]
                        te = td
                    X["t_e"] = tt("dve", X["E"], X["E"], psum[:, i, :], ALU.add, te)
                    bank_free[i] = [X["t_e"]]
            for d in range(2):
                X = x[d]
                i = bank()
                t = mms([(psum[:, i, 64 * (2 * p + j):64 * (2 * p + j) + 64], hs(X["E"], 2 * j + p),
                          X["Y0"][:, 64 * (2 * p + j):64 * (2 * p + j) + 64], True, True) for j, p in hl],
                        X["t_e"], X["t_y0"], bank_free[i])
                X["t_w2"] = copy("dve", K_["W2", d], psum[:, i, 0:256], t)
                bank_free[i] = [X["t_w2"]]
                i = bank()
                t = mms([(psum[64 * j:64 * j + 64, i, 128 * p:128 * p + 128],
                          X["at"][:, 64 * (2 * p + j):64 * (2 * p + j) + 64], hs(X["E"], 2 * j + p), True, True)
                         for j, p in hl], X["t6"], bank_free[i])
                X["t_w1"] = copy("act", K_["W1", d], psum[:, i, 0:256], t)
                bank_free[i] = [X["t_w1"]]
            sstart = {}
            for s in range(2):
                half = (s, 1 - s)
                iu = bank()
                P.wait("pe", bank_free[iu])
                for d in range(2):
                    r0 = 64 * half[d]
                    sc = s_cur[d]
                    sstart[d, half[d]] = sc
                    w1 = K_["W1", d].rearrange("p (q t) -> p q t", q=2)
                    t_u = mms([(psum[r0:r0 + 64, iu, 128 * p:128 * p + 128], w1[:, p, r0:r0 + 64], S[:, d, sc, p, :],
                                True, True) for p in range(2)], x[d]["t_w1"], t_s[d])
                for d in range(2):
                    r0 = 64 * half[d]
                    x[d]["t_u"] = tt("dve", Ut[r0:r0 + 64, d, :], psum[r0:r0 + 64, iu, 0:256],
                                     K_["W2", d][r0:r0 + 64, :], ALU.add, t_u, x[d]["t_w2"])
                bank_free[iu] = [x[1]["t_u"]]
                for d in range(2):
                    r0 = 64 * half[d]
                    sc = s_cur[d]
                    sn = 1 - sc
                    i = bank()
                    lst = []
                    for p in range(2):
                        o_ = psum[:, i, 128 * p:128 * p + 128]
                        cs = slice(128 * p, 128 * p + 128)
                        lst += [(o_, K_["kt", d][r0:r0 + 64, cs], K_["vt", d][r0:r0 + 64, cs], True, False),
                                (o_, K_["bt", d][r0:r0 + 64, cs], Ut[r0:r0 + 64, d, cs], False, True)]
                    ts_ = mms(lst, x[d]["t_u"], bank_free[i])
                    pend = r0 + 63 if d == 0 else r0
                    pc = K_["P", d].rearrange("p (q t) -> p q t", q=2)[:, :, pend:pend + 1]
                    if s == 1:
                        pass
                    for j in range(2):
                        q0 = 64 * j
                        src = psum[q0:q0 + 64, i, 0:256].rearrange("p (q v) -> p q v", q=2)[:, :, q0:q0 + 64]
                        so = S[q0:q0 + 64, d, sc, :, q0:q0 + 64]
                        sd = S[q0:q0 + 64, d, sn, :, q0:q0 + 64]
                        t = tt("dve", sd, src, so, ALU.add, ts_, t_s[d], x[d].get("t_os"))
                        t_n2 = tt("dve", sd, sd, pc[q0:q0 + 64].to_broadcast([64, 2, 64]), ALU.mult, t)
                    bank_free[i] = [t]
                    t_s[d] = t_n2
                    if s == 0:
                        x[d]["io"] = bank()
                    io = x[d]["io"]
                    lst = []
                    for p in range(2):
                        lst.append((psum[:, io, 256 * s + 64 * p:256 * s + 64 * p + 64], S[:, d, sc, p, :],
                                    K_["rho", d].rearrange("p (q t) -> p q t", q=2)[:, p, r0:r0 + 64], True, True))
                    x[d]["t_os"] = mms(lst, tro, bank_free[io] if s == 0 else None)
                    s_cur[d] = sn
            for d in range(2):
                X = x[d]
                i = bank()
                lst = []
                for j, p in hl:
                    o_ = psum[64 * j:64 * j + 64, i, 128 * p:128 * p + 128]
                    cs = slice(64 * (2 * p + j), 64 * (2 * p + j) + 64)
                    lst += [(o_, K_["vt", d][:, cs], hs(K_["Lk", d], 2 * j + p), True, False),
                            (o_, Ut[:, d, cs], hs(K_["Lb", d], 2 * j + p), False, True)]
                t = mms(lst, X["t_u"], bank_free[i])
                first = (tile[d] == 0 and d == 0) or (tile[d] == 1 and d == 1) or (tile[d] in (2, 3) and d == 0) \
                    or (tile[d] in (4, 5) and d == 1)
                od = oT[:, :, X["tok"]]
                src = psum[:, i, 0:256].rearrange("p (q t) -> p q t", q=2)
                if first:
                    t1 = copy("dve", od, src, t, t_end)
                else:
                    t1 = tt("dve", od, od, src, ALU.add, t, P.last("dve"))
                bank_free[i] = [t1]
                io = X["io"]
                for s in range(2):
                    hf = s if d == 0 else 1 - s
                    o2 = oT[:, :, 128 * tile[d] + 64 * hf:128 * tile[d] + 64 * hf + 64]
                    t1 = tt("dve", o2, o2, psum[:, io, 256 * s:256 * s + 128].rearrange("p (q t) -> p q t", q=2),
                            ALU.add, t1, X["t_os"])
                bank_free[io] = [t1]
                t_o.append(t1)
        P.wait("act", *[P.last(e) for e in ("pe", "dve", "pool")])
        P.wait("dve", *[P.last(e) for e in ("pe", "act", "pool")])
        sq, rr, bon, gt = bT[:, 0], bT[:, 1], kkT, tr[:, :, 3072:3840]
        for p in range(2):
            gp = 2 * g + p
            for a, b in spans(NT):
                i = bank()
                t = mms([(psum[:, i, 0:b - a], blk, oT[:, p, a:b], True, True)], t_o, bank_free[i])
                t = stt(oT[:, p, a:b], psum[:, i, 0:b - a], -1.0 / 64, oT[:, p, a:b], ALU.mult, ALU.add, t)
                bank_free[i] = [t]
            tq = act(sq[:, p, :], oT[:, p, :], ACT.Square, t)
            t = rstd([sq[:, p, :]], spans(NT), rr[:, p, :], blk, 64e-5, 64.0, tq)
            t = tt("dve", oT[:, p, :], oT[:, p, :], rr[:, p, :], ALU.mult, t)
            t_n = ts("dve", oT[:, p, :], oT[:, p, :], Q("gn_g", gp, 1), Q("gn_b", gp, 1), ALU.mult, ALU.add, t)
            t = tt("dve", bon[:, p, :], kdT[:, 0, p, :], kdT[:, 1, p, :], ALU.add)
            tb = stt(bon[:, p, :], bon[:, p, :], Q("rk", gp, 1), rT[:, p, :], ALU.mult, ALU.mult, t)
            for a, b in spans(NT):
                i = bank()
                t = mms([(psum[:, i, 0:b - a], blk, bon[:, p, a:b], True, True)], tb, bank_free[i])
                t = tt("dve", kT[:, p, a:b], psum[:, i, 0:b - a], vT[:, p, a:b], ALU.mult, t)
                bank_free[i] = [t]
            t = tt("dve", oT[:, p, :], oT[:, p, :], kT[:, p, :], ALU.add, t, t_n)
            res, tg = proj_cm(T["rw_in"][24 + gp], hT, NT, t_h)
            for (i, a, b) in res:
                t2 = act(gt[:, p, a:b], psum[:, i, 0:b - a], ACT.Silu, tg)
                bank_free[i] = [t2]
            t = tt("dve", oT[:, p, :], oT[:, p, :], gt[:, p, :], ALU.mult, t, t2)
        t_end = P.dma("ysp", T["ysp"][:, 2 * g:2 * g + 2, :], oT[:, :, :], t)
        t_y.append(t_end)
        t_end = [t_end, P.last("pe"), P.last("act"), P.last("dve"), P.last("pool")]
    barrier()
    P.wait("act", t_y)
    P.wait("dve", t_y)
    P.wait("pool", t_y)
    c.close()
    c = ExitStack()
    yT = sb(c, "yT", [8, NT])
    xT = sb(c, "xTb", [8, NT])
    t_yl = P.dma("yl", yT[:, :, :], T["ysp"], t_y)
    t_xl = P.dma("xl", xT[:, :, :], T["x"])
    for k in range(8):
        res, t = proj_cm(T["rw_out"][k], yT, NT, t_yl)
        for (i, a, b) in res:
            s = 1 if a == 0 else 0
            tx = stt(xT[:, k, a:b], psum[:, i, 0:b - a], modc[:, 16 + k, s:s + 1], xT[:, k, a:b], ALU.mult, ALU.add,
                     t, t_xl)
            bank_free[i] = [tx]
    P.t_x1 = P.dma("xs", T["x1"], xT[:, :, :], tx)
    barrier()
    for e in P.q:
        P.wait(e, P.t_x1)
    c.close()
    return None


def heads_norm(g_, buf, W, gcol, R, sq, t, *free):
    tq = g_.act(sq[:, 0:W], buf[:, 0:W], ACT.Square, t, *free)
    tr = g_.rstd([sq], g_.spans(W), R, g_.blk, 1e-6, 64.0, tq)
    return g_.stt(buf[:, 0:W], buf[:, 0:W], gcol, R[:, 0:W], ALU.mult, ALU.mult, tr)


def rope(g_, P, buf, a0, a1, rot, cos, sin, tmp, t, *free):
    i = g_.bank()
    n = a1 - a0
    tm = g_.mms([(g_.psum[:, i, 0:n], rot, buf[:, a0:a1], True, True)], t, g_.bank_free[i])
    t1 = g_.tt("dve", tmp[:, 0:n], g_.psum[:, i, 0:n], sin, ALU.mult, tm, *free)
    g_.bank_free[i] = [t1]
    t2 = g_.tt("dve", buf[:, a0:a1], buf[:, a0:a1], cos, ALU.mult, tm)
    return g_.tt("dve", buf[:, a0:a1], buf[:, a0:a1], tmp[:, 0:n], ALU.add, t1, t2)


def diff_layer(nc, P, T, g_):
    sb, act, copy, tt, ts, stt, mms, psum = g_.sb, g_.act, g_.copy, g_.tt, g_.ts, g_.stt, g_.mms, g_.psum
    bank, bank2, bank_free, wload, wfree, wring, C, Q = g_.bank, g_.bank2, g_.bank_free, g_.wload, g_.wfree, g_.wring, g_.C, g_.Q
    modc, AB, barrier, proj_cm, proj_tm, transposes = g_.modc, g_.AB, g_.barrier, g_.proj_cm, g_.proj_tm, g_.transposes
    x2 = sb(g_.ctx, "x2", [8, 512])
    c = ExitStack()
    hT = sb(c, "hT1", [8, NT])
    yT = sb(c, "yT1", [8, 512])
    ac = sb(c, "ac", [NAC])
    t_ac = P.dma("ac", ac[:, :], T["ac"])
    t_ab = g_.modulation(1)
    cx = ExitStack()
    xT = sb(cx, "xT1", [8, NT])
    t_x = P.dma("x1l", xT[:, :, :], T["x1"], P.t_x1)
    A = lambda k, s: AB[:, k, s:s + 1]
    B = lambda k, s: modc[:, k, s:s + 1]
    t_h = g_.normed(cx, xT, NT, hT, A, B, t_x, t_ab, "1", [(0, 256, 1), (256, 768, 0)])
    t_h = t_h + [P.last("act"), P.last("dve")]
    barrier()
    cx.close()
    sm = g_.sm
    lv = Q("lam")
    t1 = tt("dve", sm[:, 0:64], lv[:, 0:64], lv[:, 64:128], ALU.mult, g_.t_par)
    t1 = P.op("dve", lambda e: e.reduce_sum(sm[:, 64:65], sm[:, 0:64], AX.X), t1)
    t2 = tt("dve", sm[:, 0:64], lv[:, 128:192], lv[:, 192:256], ALU.mult, t1)
    t2 = P.op("dve", lambda e: e.reduce_sum(sm[:, 65:66], sm[:, 0:64], AX.X), t2)
    t3 = act(sm[:, 64:66], sm[:, 64:66], ACT.Exp, t2)
    t3 = tt("dve", sm[:, 66:67], sm[:, 65:66], sm[:, 64:65], ALU.subtract, t3)
    t_lam = ts("dve", sm[:, 67:68], sm[:, 66:67], -LAM_INIT, None, ALU.add, None, t3)
    t_sl = ts("dve", sm[:, 68:69], Q("subln"), 1.0 - LAM_INIT, None, ALU.mult, None)
    nlam = sm[:, 67:68]
    subl = sm[:, 68:69]

    def two(name, cols):
        return [sb(c, f"{name}{i}", cols) for i in range(2)]

    qb, kb, vb, gb = two("qb", [512]), two("kb", [NT]), two("vb", [6, 128]), two("gb", [512])
    sq, R, tmp = sb(c, "sqa", [NT]), sb(c, "Ra", [NT]), sb(c, "tmpa", [512])
    p0, p1 = two("p0", [NT]), two("p1", [NT])
    aT = two("aT", [6, 512])
    st = two("st", [8])
    rot = ac[:, 0:128]
    cos, sin = ac[:, 256:1024], ac[:, 1024:1792]
    hl = hT[:, :, 256:768]
    fin = {0: None, 1: None}
    t_y = []
    npair = 0
    pfree = {0: None, 1: None}
    for h in range(8):
        b = h % 2
        q, k, v, gg = qb[b], kb[b], vb[b], gb[b]
        res, t = proj_cm(T["da_in"][h], hl, 512, t_h)
        tq = copy("act", q[:, :], psum[:, res[0][0], :], t, fin[b])
        bank_free[res[0][0]] = [tq]
        tq = heads_norm(g_, q, 512, Q("qn"), R, sq, tq, P.last("dve"), P.last("pe"))
        tq = rope(g_, P, q, 0, 512, rot, cos[:, 256:768], sin[:, 256:768], tmp, [tq, t_ac])
        res, t = proj_cm(T["da_in"][8 + h], hT, NT, t_h)
        for (i, a0, a1) in res:
            tk = copy("act", k[:, a0:a1], psum[:, i, 0:a1 - a0], t, fin[b])
            bank_free[i] = [tk]
        tk = heads_norm(g_, k, NT, Q("kn"), R, sq, tk, P.last("dve"), P.last("pe"))
        tk = rope(g_, P, k, 256, 768, rot, cos[:, 256:768], sin[:, 256:768], tmp, [tk, t_ac])
        tv = proj_tm(T["da_in"][16 + h], hT, NT, t_h, v, "act", fin[b])
        res, t = proj_cm(T["da_in"][24 + h], hl, 512, t_h)
        tg = act(gg[:, :], psum[:, res[0][0], :], ACT.Silu, t, fin[b])
        bank_free[res[0][0]] = [tg]
        t_at = []
        for qt in range(4):
            u = npair % 2
            npair += 1
            s_ = st[u]
            pr = (p0[u], p1[u])
            te = []
            for cc in range(2):
                i = bank2()
                t = mms([(psum[:, i + (a0 // 512), 0:a1 - a0], q[64 * cc:64 * cc + 64, 128 * qt:128 * qt + 128],
                          k[64 * cc:64 * cc + 64, a0:a1], True, True) for a0, a1 in ((0, 512), (512, 768))],
                        tq, tk, bank_free[i], bank_free[i + 1])
                sp_ = psum[:, i:i + 2, :].rearrange("p a n -> p (a n)")[:, 0:768]
                t = P.op("dve", lambda e, sp_=sp_, cc=cc, s_=s_: e.reduce_max(s_[:, cc:cc + 1], sp_, AX.X), t, pfree[u])
                t = ts("dve", s_[:, cc:cc + 1], s_[:, cc:cc + 1], -0.125, None, ALU.mult, None, t)
                t = act(pr[cc][:, :], sp_, ACT.Exp, t, pfree[u], scale=0.125, bias=s_[:, cc:cc + 1],
                        accum=s_[:, 2 + cc:3 + cc])
                bank_free[i] = [t]
                bank_free[i + 1] = [t]
                te.append(t)
            t = P.op("dve", lambda e, s_=s_: e.reciprocal(s_[:, 4:6], s_[:, 2:4]), te)
            t2 = ts("dve", s_[:, 5:6], s_[:, 5:6], nlam, None, ALU.mult, None, t, t_lam)
            ta = ts("dve", pr[1][:, :], pr[1][:, :], s_[:, 5:6], None, ALU.mult, None, t2)
            ta = stt(pr[0][:, :], pr[0][:, :], s_[:, 4:5], pr[1][:, :], ALU.mult, ALU.add, ta)
            for n0, n1 in ((0, 4), (4, 6)):
                i = bank()
                t = transposes([(psum[:, i, 128 * (n - n0):128 * (n - n0) + 128], pr[0][:, 128 * n:128 * n + 128])
                                for n in range(n0, n1)], ta, bank_free[i])
                t2 = copy("dve" if n0 else "act", aT[b][:, n0:n1, 128 * qt:128 * qt + 128],
                          psum[:, i, 0:128 * (n1 - n0)].rearrange("p (n c) -> p n c", c=128), t, fin[b])
                bank_free[i] = [t2]
                t_at.append(t2)
            pfree[u] = [t, ta]
        i = bank()
        t_pv = mms([(psum[:, i, :], v[:, n, :], aT[b][:, n, :], n == 0, n == 5) for n in range(6)],
                   t_at, tv, bank_free[i])
        t = copy("act", yT[:, h, :], psum[:, i, :], t_pv)
        bank_free[i] = [t]
        tq2 = act(sq[:, 0:512], yT[:, h, :], ACT.Square, t, P.last("pe"), P.last("dve"))
        tr = g_.rstd([sq], [(0, 512)], R, g_.ones, 1e-5, 128.0, tq2, P.last("dve"))
        t = stt(yT[:, h, :], yT[:, h, :], subl, R[:, 0:512], ALU.mult, ALU.mult, tr, t_sl)
        t = tt("dve", yT[:, h, :], yT[:, h, :], gg[:, :], ALU.mult, t, tg)
        fin[b] = [t_pv, t]
        t_y.append(t)
    barrier()
    t_xl = P.dma("x1m", x2[:, :, :], T["x1"][:, :, 256:768])
    for k in range(8):
        res, t = proj_cm(T["da_out"][k], yT, 512, t_y)
        i = res[0][0]
        tx = stt(x2[:, k, :], psum[:, i, :], modc[:, 16 + k, 0:1], x2[:, k, :], ALU.mult, ALU.add, t, t_xl)
        bank_free[i] = [tx]
    P.x2, P.t_x2 = x2, tx
    barrier()
    c.close()


def second_block(nc, P, T, g_):
    sb, act, copy, tt, ts, stt, mms, psum = g_.sb, g_.act, g_.copy, g_.tt, g_.ts, g_.stt, g_.mms, g_.psum
    bank, bank2, bank_free, wload, wfree, wring, C, Q = g_.bank, g_.bank2, g_.bank_free, g_.wload, g_.wfree, g_.wring, g_.C, g_.Q
    barrier, proj_cm, proj_tm, transposes = g_.barrier, g_.proj_cm, g_.proj_tm, g_.transposes
    x2, t_x = P.x2, P.t_x2
    c = g_.ctx
    bc = sb(c, "bc", [NBC])
    t_bc = P.dma("bc", bc[:, :], T["bc"])
    mem = sb(c, "mem", [8, 256])
    t_mem = P.dma("mem", mem[:, :, :], T["mem"])
    hT = sb(c, "hT2", [8, 512])
    hm = sb(c, "hm2", [8, 256])
    yT = sb(c, "yT2", [8, 512])

    def two(name, cols):
        return [sb(c, f"{name}{i}", cols) for i in range(2)]

    qb, kb, vb, gb = two("qc", [512]), two("kc", [512]), two("vc", [4, 128]), two("gc", [512])
    sq, R, tmp = sb(c, "sqc", [512]), sb(c, "Rc", [512]), sb(c, "tmpc", [512])
    pr = [sb(c, f"pc{i}", [512]) for i in range(3)]
    aT = [sb(c, f"aTc{i}", [4, 512]) for i in range(3)]
    st = [sb(c, f"stc{i}", [8]) for i in range(3)]
    rot, cos, sin = bc[:, 0:128], bc[:, 128:640], bc[:, 640:1152]
    fin = {0: None, 1: None}
    pfree = [None] * 3
    afree = [None] * 3
    n_p = n_a = 0
    for l in range(2):
        cl = ExitStack()
        A = lambda k, s: Q("ng2", 8 * l + k, 1)
        Am = lambda k, s: Q("mng2", 8 * l + k, 1)
        t_h = g_.normed(cl, x2, 512, hT, A, None, t_x, None, f"n{l}", [(0, 512, 0)], P.last("pe"))
        t_m = g_.normed(cl, mem, 256, hm, Am, None, t_mem, None, f"m{l}", [(0, 256, 0)], P.last("pe"))
        t_h = [P.last("dve"), P.last("act")]
        t_y = []
        for pi in range(8):
            kind = 0 if pi < 3 else (1 if pi < 6 else 2)
            b = pi % 2
            q, k, v, gg = qb[b], kb[b], vb[b], gb[b]
            if kind < 2:
                base = 12 * kind + (pi - 3 * kind)
                wq, wk, wv, wg = (T["w_in2"][l, base + 3 * z] for z in range(4))
                nk = 512
                src, th2 = hT, t_h
            else:
                r = pi - 6
                wq, wg = T["w_in2"][l, 24 + r], T["w_in2"][l, 26 + r]
                wk, wv = T["w_mkv"][l, r], T["w_mkv"][l, 2 + r]
                nk = 256
                src, th2 = hm, t_h
            res, t = proj_cm(wq, hT, 512, t_h)
            tq = copy("act", q[:, :], psum[:, res[0][0], :], t, fin[b])
            bank_free[res[0][0]] = [tq]
            tq = heads_norm(g_, q, 512, Q("qkg", 6 * l + 2 * kind, 1), R, sq, tq, P.last("dve"), P.last("pe"))
            if kind < 2:
                tq = rope(g_, P, q, 0, 512, rot, cos, sin, tmp, [tq, t_bc])
            res, t = proj_cm(wk, src, nk, th2)
            tk = copy("act", k[:, 0:nk], psum[:, res[0][0], 0:nk], t, fin[b])
            bank_free[res[0][0]] = [tk]
            tk = heads_norm(g_, k, nk, Q("qkg", 6 * l + 2 * kind + 1, 1), R, sq, tk, P.last("dve"), P.last("pe"))
            if kind < 2:
                tk = rope(g_, P, k, 0, 512, rot, cos, sin, tmp, [tk, t_bc])
            tv = proj_tm(wv, src, nk, th2, v, "act", fin[b])
            res, t = proj_cm(wg, hT, 512, t_h)
            tg = act(gg[:, :], psum[:, res[0][0], :], ACT.Silu, t, fin[b])
            bank_free[res[0][0]] = [tg]
            io = bank()
            tpv = []
            P.wait("pe", bank_free[io])
            for j in range(2):
                a_ = n_a % 3
                n_a += 1
                t_at = []
                for qt in range(4):
                    u = n_p % 3
                    n_p += 1
                    s_, pp = st[u], pr[u]
                    n = 128 * (qt + 1) if kind < 2 else 256
                    i = bank()
                    if i == io:
                        i = bank()
                    t = mms([(psum[:, i, 0:n], q[64 * j:64 * j + 64, 128 * qt:128 * qt + 128],
                              k[64 * j:64 * j + 64, 0:n], True, True)], tq, tk, bank_free[i])
                    if kind < 2:
                        o = (1152 if kind == 0 else 1664) + 384 - 128 * qt
                        t = P.op("dve", lambda e, pp=pp, n=n, i=i, o=o, s_=s_: e.tensor_tensor_reduce(
                            out=pp[:, 0:n], in0=psum[:, i, 0:n], in1=bc[:, o:o + n], scale=1.0, scalar=-3.0e38,
                            op0=ALU.add, op1=ALU.max, accum_out=s_[:, 0:1]), t, pfree[u], t_bc)
                        bank_free[i] = [t]
                        ein = pp[:, 0:n]
                    else:
                        t = P.op("dve", lambda e, n=n, i=i, s_=s_: e.reduce_max(s_[:, 0:1], psum[:, i, 0:n], AX.X),
                                 t, pfree[u])
                        ein = psum[:, i, 0:n]
                    t = ts("dve", s_[:, 1:2], s_[:, 0:1], -0.125, None, ALU.mult, None, t)
                    t = act(pp[:, 0:n], ein, ACT.Exp, t, scale=0.125, bias=s_[:, 1:2], accum=s_[:, 2:3])
                    if kind == 2:
                        bank_free[i] = [t]
                    t = P.op("dve", lambda e, s_=s_: e.reciprocal(s_[:, 3:4], s_[:, 2:3]), t)
                    ta = ts("dve", pp[:, 0:n], pp[:, 0:n], s_[:, 3:4], None, ALU.mult, None, t)
                    i = bank()
                    if i == io:
                        i = bank()
                    t = transposes([(psum[:, i, 128 * z:128 * z + 128], pp[:, 128 * z:128 * z + 128])
                                    for z in range(n // 128)], ta, bank_free[i])
                    pfree[u] = [t]
                    t2 = copy("act" if qt % 2 else "dve", aT[a_][:, 0:n // 128, 128 * qt:128 * qt + 128],
                              psum[:, i, 0:n].rearrange("p (n c) -> p n c", c=128), t, afree[a_])
                    bank_free[i] = [t2]
                    t_at.append(t2)
                nkt = 4 if kind < 2 else 2
                lst = []
                for z in range(nkt):
                    q0 = 128 * z if kind < 2 else 0
                    lst.append((psum[64 * j:64 * j + 64, io, q0:512], v[:, z, 64 * j:64 * j + 64],
                                aT[a_][:, z, q0:512], z == 0, z == nkt - 1))
                t = mms(lst, t_at, tv, skip=True)
                afree[a_] = [t]
                tpv.append(t)
            t = tt("dve", yT[:, pi, :], psum[:, io, :], gg[:, :], ALU.mult, tpv, tg)
            bank_free[io] = [t]
            fin[b] = [tpv[-1], t]
            t_y.append(t)
        for k in range(8):
            res, t = proj_cm(T["w_out2"][l, k], yT, 512, t_y)
            i = res[0][0]
            tx = tt("dve", x2[:, k, :], psum[:, i, :], x2[:, k, :], ALU.add, t)
            bank_free[i] = [tx]
        t_x = tx
        cl.close()
        P.wait("act", P.last("pe"), P.last("dve"))
        P.wait("dve", P.last("pe"), P.last("act"))
    t = P.dma("out", T["out"], x2[:, :, :], t_x)
    P.wait("sp", t)


def kernel(**inputs):
    import numpy as _np
    import concourse.bacc as _bacc
    from concourse import mybir as _mybir
    from concourse.bass_utils import run_bass_kernel_spmd as _run

    I = {k: _np.asarray(v) for k, v in inputs.items()}

    def cm(a):
        return a.T.reshape(8, 128, -1).transpose(1, 0, 2)

    def wb(w):
        n = w.shape[-1] // 128
        lead = w.shape[:-2]
        k = len(lead)
        a = w.reshape(*lead, 8, 128, n, 128)
        return _np.ascontiguousarray(a.transpose(*range(k), k + 2, k + 1, k, k + 3))

    def cols(v):
        return v.reshape(-1, 128).T

    con, rc, ac, bc = constants()
    par = _np.zeros((128, NPAR), _np.float32)

    def put(name, a):
        o, w = PCOLS[name]
        par[:, o:o + w] = a.reshape(128, w)

    put("cs", _np.stack([cols(I["c"][0]), cols(I["c_ctx"])], axis=2))
    put("ada_b", _np.concatenate([cols(I["ada_b"][l]) for l in range(2)], axis=1))
    put("norm_g", _np.concatenate([cols(I["norm_g"][l]) for l in range(2)], axis=1))
    put("mu", cols(I["rw_mu"][0]))
    put("kk", cols(I["rw_kk"][0]))
    put("ka", cols(I["rw_ka"][0]))
    put("rk", cols(I["rw_rk"][0].reshape(-1)))
    put("gn_g", cols(I["rw_gn_g"][0]))
    put("gn_b", cols(I["rw_gn_b"][0]))
    put("a0", _np.concatenate([cols(I["rw_a0"][0, d]) for d in range(2)], axis=1))
    two = lambda v: _np.tile(v, 2)[:, None]
    put("qn", two(I["da_qn"][0]))
    put("kn", two(I["da_kn"][0]))
    put("subln", I["da_subln"][0][:, None])
    put("ng2", _np.concatenate([cols(I["norm_g_2"][l]) for l in range(2)], axis=1))
    put("mng2", _np.concatenate([cols(I["mem_norm_g_2"][l]) for l in range(2)], axis=1))
    put("qkg", _np.concatenate([two(I["qk_g_2"][l, i]) for l in range(2) for i in range(6)], axis=1))
    put("lam", _np.broadcast_to(I["da_lam"][0].reshape(1, 256), (128, 256)))
    lw2 = _np.zeros((4, 128, 4, 256), _np.float32)
    w0b = _np.zeros((4, 128, 2, 256), _np.float32)
    for g in range(4):
        for d in range(2):
            lw2[g, 64 * d:64 * d + 64, d] = I["rw_w2"][0, d][:, 256 * g:256 * g + 256]
            lw2[g, 64 * d:64 * d + 64, 2 + d] = I["rw_a2"][0, d][:, 256 * g:256 * g + 256]
            w0b[g, :, d] = I["rw_w0"][0, d][None, 256 * g:256 * g + 256]
    w2 = I["w_in_2"]
    arrays = {
        "x": cm(_np.concatenate([I["ctx"][0], I["x"][0]], axis=0)),
        "mem": cm(I["mem_2"][0]),
        "con": con, "rc": rc, "ac": ac, "bc": bc, "par": par, "lw2": lw2, "w0b": w0b,
        "ada": wb(I["ada_w"]),
        "rw_in": wb(I["rw_in"][0]), "rw_out": wb(I["rw_out"][0]),
        "da_in": wb(I["da_in"][0]), "da_out": wb(I["da_out"][0]),
        "w_in2": wb(w2), "w_out2": wb(I["w_out_2"]), "w_mkv": wb(I["w_mem_kv_2"]),
    }
    nc = _bacc.Bacc("TRN2", target_bir_lowering=False, num_devices=1)
    T, feed = {}, {}
    for k, a in arrays.items():
        a = _np.ascontiguousarray(a)
        feed["in_" + k] = a
        T[k] = nc.dram_tensor("in_" + k, a.shape, _mybir.dt.float32, kind="ExternalInput").ap()
    T["ysp"] = nc.dram_tensor("ysp", (128, 8, 768), _mybir.dt.float32, kind="Internal").ap()
    T["x1"] = nc.dram_tensor("x1s", (128, 8, 768), _mybir.dt.float32, kind="Internal").ap()
    T["out"] = nc.dram_tensor("out_x", (128, 8, 512), _mybir.dt.float32, kind="ExternalOutput").ap()
    build(nc, T)
    r = _run(nc, [feed], core_ids=[0])
    o = r.results[0]["out_x"]
    return _np.ascontiguousarray(_np.asarray(o).transpose(2, 1, 0).reshape(1, 512, 1024))
```

```python
from contextlib import ExitStack
import math

import numpy as np

import concourse.bass as bass
from concourse import mybir

ALU = mybir.AluOpType
ACT = mybir.ActivationFunctionType
F32 = mybir.dt.float32
F32R = mybir.dt.float32r
AX = mybir.AxisListType

NCTX, NLAT, NT = 256, 512, 768
NEG = -1.0e30
DECAY = math.exp(-0.5)
LAM_INIT = 0.8 - 0.6 * math.exp(-0.3)
NSLOT = 4

PCOLS = {}
_n = 0
for _name, _w in (("cs", 16), ("ada_b", 48), ("norm_g", 16), ("mu", 26), ("kk", 8), ("ka", 8), ("rk", 8),
                  ("gn_g", 8), ("gn_b", 8), ("a0", 16), ("qn", 1), ("kn", 1), ("subln", 1), ("ng2", 16),
                  ("mng2", 16), ("qkg", 12), ("lam", 256)):
    PCOLS[_name] = (_n, _w)
    _n += _w
NPAR = _n

CCOLS = {}
_n = 0
for _name, _w in (("ident", 128), ("ones", 128), ("blk", 128), ("eps", 8)):
    CCOLS[_name] = (_n, _w)
    _n += _w
NCON = _n
RCOLS = {"tri": (0, 512), "msk": (512, 512), "lvl": (1024, 2 * 6 * 128)}
NRC = 1024 + 1536
ACOLS = {"rot1": (0, 128), "rot2": (128, 128), "cos1": (256, 768), "sin1": (1024, 768)}
NAC = 1792
BCOLS = {"rot2": (0, 128), "cos2": (128, 512), "sin2": (640, 512), "mw1": (1152, 512), "mw2": (1664, 512)}
NBC = 2176


def constants():
    f = np.float32
    con = np.zeros((128, NCON), f)
    con[:, 0:128] = np.eye(128)
    con[:, 128:256] = 1.0
    i = np.arange(128)
    con[:, 256:384] = (i[:, None] // 64 == i[None] // 64)
    con[:, 384:392] = np.array([1e-6, 1e-5, 64e-5, 1e-12, 0, 0, 0, 0])[None]
    rc = np.zeros((128, NRC), f)
    j, t = i[:, None], i[None, :]
    same = (j // 64) == (t // 64)
    for d in range(2):
        incl = same & ((j <= t) if d == 0 else (j >= t))
        strict = same & ((j < t) if d == 0 else (j > t))
        rc[:, 256 * d:256 * d + 128] = -DECAY * incl
        rc[:, 256 * d + 128:256 * d + 256] = -DECAY * strict
        rc[:, 512 + 256 * d:512 + 256 * d + 128] = strict
        rc[:, 512 + 256 * d + 128:512 + 256 * d + 256] = incl
        for l in range(6):
            s = 1 << l
            b = (j // (2 * s)) == (t // (2 * s))
            jo, to = (j // s) % 2, (t // s) % 2
            m = b & ((jo == 0) & (to == 1) if d == 0 else (jo == 1) & (to == 0))
            rc[:, 1024 + (6 * d + l) * 128:1024 + (6 * d + l + 1) * 128] = m
    ac = np.zeros((128, NAC), f)
    inv = (np.float32(10000.0) ** (-np.arange(16, dtype=f) / f(16))).astype(f)
    tok = np.arange(512)
    rows, cols = (tok // 64).astype(f), (tok % 64).astype(f)
    ac[:, 256:1024] = 1.0
    for p in range(128):
        c = p % 64
        ax, half, fr = c // 32, (c // 16) % 2, c % 16
        ang = ((rows if ax == 0 else cols) * inv[fr]).astype(f)
        ac[p, 256 + 256:256 + 768] = np.cos(ang)
        ac[p, 1024 + 256:1024 + 768] = np.sin(ang)
        partner = p + 16 if half == 0 else p - 16
        ac[partner, p] = -1.0 if half == 0 else 1.0
    bc = np.zeros((128, NBC), f)
    inv = (np.float32(10000.0) ** (-np.arange(32, dtype=f) / f(32))).astype(f)
    for p in range(128):
        c = p % 64
        half, fr = c // 32, c % 32
        ang = (tok.astype(f) * inv[fr]).astype(f)
        bc[p, 128:640] = np.cos(ang)
        bc[p, 640:1152] = np.sin(ang)
        partner = p + 32 if half == 0 else p - 32
        bc[partner, p] = -1.0 if half == 0 else 1.0
    u = np.arange(512)
    dist = i[:, None] - (u[None] - 384)
    bc[:, 1152:1664] = np.where(dist >= 0, 0.0, NEG)
    mult = (dist <= 128).astype(f) + (dist % 4 == 0) + (dist % 16 == 0)
    ok = (dist >= 0) & (mult > 0)
    bc[:, 1664:2176] = np.where(ok, 8.0 * np.log(np.maximum(mult, 1.0)), NEG)
    return con, rc, ac, bc


class Prog:

    def __init__(self, nc, ctx):
        self.nc, self.ctx = nc, ctx
        self.q = {e: [] for e in ("pe", "act", "dve", "pool", "sp")}
        self.sem = {e: ctx.enter_context(nc.semaphore("s_" + e)) for e in self.q}
        self.n = {e: 0 for e in self.q}
        self.seen = {e: {} for e in self.q}
        self.slots = {}

    def wait(self, e, *toks):
        for t in toks:
            if t is None:
                continue
            if isinstance(t, list):
                self.wait(e, *t)
                continue
            s, v = t
            if self.seen[e].get(id(s), 0) < v:
                self.seen[e][id(s)] = v
                self.q[e].append(lambda eng, s=s, v=v: eng.wait_ge(s, v))

    def op(self, e, fn, *toks):
        self.wait(e, *toks)
        self.n[e] += 1
        s = self.sem[e]
        self.q[e].append(lambda eng: fn(eng).then_inc(s, 1))
        return (s, self.n[e])

    def quiet(self, e, fn, *toks):
        self.wait(e, *toks)
        self.q[e].append(fn)

    def dma(self, slot, dst, src, *toks, e="sp"):
        self.wait(e, *toks)
        if slot not in self.slots:
            self.slots[slot] = [self.ctx.enter_context(self.nc.semaphore("d_" + slot)), 0]
        r = self.slots[slot]
        r[1] += 16
        self.q[e].append(lambda eng, s=r[0]: eng.dma_start(dst, src).then_inc(s, 16))
        return (r[0], r[1])

    def last(self, e):
        return (self.sem[e], self.n[e]) if self.n[e] else None

    def final(self, toks):
        best = {}
        for s, v in toks:
            best[id(s)] = max(best.get(id(s), (s, 0)), (s, v), key=lambda t: t[1])
        return list(best.values())

    def play(self, e, eng):
        for f in self.q[e]:
            f(eng)


def build(nc, T):
    with ExitStack() as ctx:
        P = Prog(nc, ctx)
        body(nc, ctx, P, T)
        block = ctx.enter_context(nc.Block())

        @block.sync
        def _(e):
            P.play("sp", e)

        @block.gpsimd
        def _(e):
            P.play("pool", e)

        @block.scalar
        def _(e):
            P.play("act", e)

        @block.vector
        def _(e):
            P.play("dve", e)

        @block.tensor
        def _(e):
            P.play("pe", e)


def body(nc, ctx, P, T):
    def sb(c, name, cols):
        return c.enter_context(nc.sbuf_tensor(name, [128] + list(cols), F32))

    def pe(fn, *t):
        return P.op("pe", fn, *t)

    tables = [""]

    def act(out, in_, f, *t, scale=1.0, bias=0.0, accum=None):
        want = {ACT.Exp: "el", ACT.Ln: "el", ACT.Silu: "silu", ACT.Sigmoid: "sig", ACT.Tanh: "tanh"}.get(f)
        if want and want != tables[0]:
            tables[0] = want
            if want == "el":
                P.quiet("act", lambda e: e.preload_act_table_set("natural_log_exp_and_others"))
        if accum is None:
            return P.op("act", lambda e: e.activation(out, in_, f, bias=bias, scale=scale), *t)
        return P.op("act", lambda e: e.activation(out, in_, f, bias=bias, scale=scale, accum_out=accum), *t)

    def copy(e, out, in_, *t):
        if e == "act":
            return P.op("act", lambda g: g.activation(out, in_, ACT.Copy), *t)
        return P.op(e, lambda g: g.tensor_copy(out, in_), *t)

    def tt(e, out, a, b, o, *t):
        return P.op(e, lambda g: g.tensor_tensor(out, a, b, o), *t)

    def ts(e, out, a, s1, s2, o0, o1, *t):
        if o1 is None:
            return P.op(e, lambda g: g.tensor_scalar(out, a, s1, None, o0), *t)
        return P.op(e, lambda g: g.tensor_scalar(out, a, s1, s2, o0, o1), *t)

    def stt(out, a, s, b, o0, o1, *t):
        return P.op("dve", lambda g: g.scalar_tensor_tensor(out=out, in0=a, scalar=s, in1=b, op0=o0, op1=o1), *t)

    psum = ctx.enter_context(nc.psum_tensor("ps", [128, 8, 512], F32))
    bank_free = Banks()
    bank, bank2 = bank_free.take, bank_free.take2

    def mms(lst, *toks, skip=False):
        P.wait("pe", *toks)
        for k, (o, l, r, st, sp_) in enumerate(lst):
            f = lambda e, o=o, l=l, r=r, st=st, sp_=sp_: e.matmul(o, l, r, start=st, stop=sp_, skip_group_check=skip)
            if k == len(lst) - 1:
                return P.op("pe", f)
            P.quiet("pe", f)

    con = sb(ctx, "con", [NCON])
    par = sb(ctx, "par", [NPAR])
    t_con = P.dma("con", con[:, :], T["con"])
    t_par = P.dma("par", par[:, :], T["par"])
    P.t_in = [t_con, t_par]

    def C(name, a=0, n=None):
        o, w = CCOLS[name]
        return con[:, o + a:o + (w if n is None else a + n)]

    def Q(name, a=0, n=None):
        o, w = PCOLS[name]
        return par[:, o + a:o + (w if n is None else a + n)]

    ident, ones, blk = C("ident"), C("ones"), C("blk")
    EPS = {v: C("eps", k, 1) for k, v in enumerate((1e-6, 1e-5, 64e-5, 1e-12))}

    def transposes(lst, *toks):
        P.wait("pe", *toks)
        for k, (o, i) in enumerate(lst):
            f = lambda e, o=o, i=i: e.transpose(o, i, ident)
            if k == len(lst) - 1:
                return P.op("pe", f)
            P.quiet("pe", f)

    class Ring:
        now = None

        def __init__(self, c, name, n):
            self.buf, self.name, self.n, self.k = sb(c, name, [n, 8, 128]), name, n, 0
            self.free = [[P.last(e) for e in ("pe", "act", "dve", "pool")]] * n
            Ring.now = self

        def load(self, src):
            i = self.k % self.n
            self.k += 1
            return i, P.dma(f"{self.name}{i}", self.buf[:, i, :, :], src, self.free[i])

    sm = sb(ctx, "sm", [160])
    modcs = sb(ctx, "modc", [2, 24, 2])
    s0 = sb(ctx, "s0", [8, 2])
    ABs = sb(ctx, "AB", [2, 8, 2])
    t_cs = act(s0[:, :, :], Q("cs").rearrange("p (k s) -> p k s", s=2), ACT.Silu, t_par)

    def modulation(layer, done):
        modc, AB = modcs[:, layer], ABs[:, layer]
        R = Ring.now
        i = bank()
        P.wait("pe", bank_free[i], t_cs, t_con)
        for m in range(24):
            w, tw = R.load(T["ada"][layer, m])
            t = mms([(psum[:, i, 2 * m:2 * m + 2], R.buf[:, w, k, :], s0[:, k, :], k == 0, k == 7)
                     for k in range(8)], tw)
            R.free[w] = t
            yield
        ab = Q("ada_b", 24 * layer, 24).unsqueeze(2).to_broadcast([128, 24, 2])
        t1 = tt("dve", modc, psum[:, i, 0:48].rearrange("p (m s) -> p m s", s=2), ab, ALU.add, t, t_par)
        bank_free[i] = [t1]
        t2 = ts("dve", AB, modc[:, 8:16, :], 1.0, None, ALU.add, None, t1)
        g = Q("norm_g", 8 * layer, 8).unsqueeze(2).to_broadcast([128, 8, 2])
        done[layer] = tt("dve", AB, AB, g, ALU.mult, t2)

    def rstd(src_sq, widths, R, lhs, eps, n, t_sq, *free, N=None):
        out = []
        for (a, b) in widths:
            i = bank()
            t = mms([(psum[:, i, 0:b - a], lhs, s[:, a:b], k == 0, k == len(src_sq) - 1)
                     for k, s in enumerate(src_sq)], t_sq, bank_free[i], t_con)
            t1 = act(R[:, a:b], psum[:, i, 0:b - a], ACT.Ln, t, *free, scale=1.0 / n, bias=EPS[eps])
            t2 = act(R[:, a:b], R[:, a:b], ACT.Exp, t1, scale=-0.5)
            M = (src_sq[0] if N is None else N)[:, a:b]
            t3 = ts("dve", M, psum[:, i, 0:b - a], 0.5 / n, 0.5 * eps, ALU.mult, ALU.add, t1)
            bank_free[i] = [t3]
            t4 = tt("pool", M, M, R[:, a:b], ALU.mult, t2, t3)
            t5 = tt("pool", M, M, R[:, a:b], ALU.mult, t4)
            out.append(P.op("dve", lambda e, M=M, r=R[:, a:b]: e.scalar_tensor_tensor(
                out=r, in0=M, scalar=1.5, in1=r, op0=ALU.subtract, op1=ALU.mult, reverse0=True), t5))
        return out

    def spans(W):
        return [(0, 256), (256, 768)] if W == 768 else ([(0, 512)] if W == 512 else [(0, 256)])

    def normed(c, xT, W, hT, A, B, t_x, t_ab, tag, streams, *free):
        R = sb(c, "R" + tag, [W])
        tq = act(hT[:, :, :], xT[:, :, :], ACT.Square, t_x, *free)
        Nw = sb(c, "Nw" + tag, [W])
        tr = rstd([hT[:, k, :] for k in range(8)], spans(W), R, ones, 1e-6, 1024.0, tq, N=Nw)
        t_pe = P.last("pe")
        last = []
        for k in range(8):
            for a, b, s in streams:
                t = stt(hT[:, k, a:b], xT[:, k, a:b], A(k, s), R[:, a:b], ALU.mult, ALU.mult, tr, t_ab, t_pe)
                if B is not None:
                    t = act(hT[:, k, a:b], hT[:, k, a:b], ACT.Identity, t, bias=B(k, s))
            last.append(t)
        return last

    def proj_cm(wsrc, hT, W, t_h, K=8):
        R = Ring.now
        w, tw = R.load(wsrc)
        res = []
        t = None
        for a, b in spans(W):
            i = bank()
            t = mms([(psum[:, i, 0:b - a], R.buf[:, w, k, :], hT[:, k, a:b], k == 0, k == K - 1) for k in range(K)],
                    tw, t_h, bank_free[i])
            res.append((i, a, b))
        R.free[w] = t
        return res, t

    def proj_tm(wsrc, hT, W, t_h, dst, e, *free):
        R = Ring.now
        w, tw = R.load(wsrc)
        t = None
        outs = []
        for n0 in range(0, W // 128, 4):
            n1 = min(W // 128, n0 + 4)
            i = bank()
            P.wait("pe", bank_free[i])
            for n in range(n0, n1):
                t = mms([(psum[:, i, 128 * (n - n0):128 * (n - n0) + 128], hT[:, k, 128 * n:128 * n + 128],
                          R.buf[:, w, k, :], k == 0, k == 7) for k in range(8)], tw, t_h)
            tc = copy(e, dst[:, n0:n1, :], psum[:, i, 0:128 * (n1 - n0)].rearrange("p (n c) -> p n c", c=128), t, *free)
            bank_free[i] = [tc]
            outs.append(tc)
        R.free[w] = t
        return outs

    def barrier():
        toks = [P.last(e) for e in ("pe", "act", "dve", "pool")]
        for e in P.q:
            P.wait(e, *toks)

    kit = Kit()
    kit.sb = sb
    kit.act = act
    kit.copy = copy
    kit.tt = tt
    kit.ts = ts
    kit.stt = stt
    kit.mms = mms
    kit.psum = psum
    kit.bank = bank
    kit.bank2 = bank2
    kit.bank_free = bank_free
    kit.C = C
    kit.Q = Q
    kit.ident = ident
    kit.ones = ones
    kit.blk = blk
    kit.modcs = modcs
    kit.ABs = ABs
    kit.Ring = Ring
    kit.transposes = transposes
    kit.rstd = rstd
    kit.spans = spans
    kit.proj_cm = proj_cm
    kit.proj_tm = proj_tm
    kit.barrier = barrier
    kit.t_con = t_con
    kit.t_par = t_par
    kit.modulation = modulation
    kit.normed = normed
    kit.sm = sm
    kit.ctx = ctx
    time_mix(nc, P, T, kit)
    diff_layer(nc, P, T, kit)
    second_block(nc, P, T, kit)


class Banks:

    def __init__(self):
        self.free = [[] for _ in range(8)]
        self.order = list(range(8))

    def __getitem__(self, i):
        return self.free[i]

    def __setitem__(self, i, toks):
        self.free[i] = toks
        self.order.append(i)

    def take(self):
        return self.order.pop(0)

    def take2(self):
        for i in self.order:
            j = i ^ 1
            if j in self.order:
                self.order.remove(i)
                self.order.remove(j)
                return min(i, j)
        raise RuntimeError("no two banks side by side")


def pace(*gens):
    left = [[0, n, g] for g, n in gens]
    while left:
        x = min(left, key=lambda x: (x[0] + 1) / x[1])
        x[0] += 1
        try:
            next(x[2])
        except StopIteration:
            left.remove(x)


def weave(*gens):
    gens = list(gens)
    while gens:
        for g in list(gens):
            try:
                next(g)
            except StopIteration:
                gens.remove(g)


class Kit:
    pass


def time_mix(nc, P, T, g_):
    sb, act, copy, tt, ts, stt, mms, psum = g_.sb, g_.act, g_.copy, g_.tt, g_.ts, g_.stt, g_.mms, g_.psum
    bank, bank_free, C, Q = g_.bank, g_.bank_free, g_.C, g_.Q
    ident, blk, modc, AB = g_.ident, g_.blk, g_.modcs[:, 0], g_.ABs[:, 0]
    transposes, rstd, spans, proj_cm, barrier = g_.transposes, g_.rstd, g_.spans, g_.proj_cm, g_.barrier
    t_con, t_par = g_.t_con, g_.t_par
    A = lambda k, s: AB[:, k, s:s + 1]
    B = lambda k, s: modc[:, k, s:s + 1]

    c = ExitStack()
    g_.Ring(c, "wa", 10)
    hT = sb(c, "hT", [8, NT])
    cx = ExitStack()
    xT = sb(cx, "xT0", [8, NT])
    t_x = P.dma("x", xT[:, :, :], T["x"], e="act")
    mods = {}
    weave(g_.modulation(0, mods))
    t_h = g_.normed(cx, xT, NT, hT, A, B, t_x, mods[0], "0", [(0, 256, 1), (256, 768, 0)])
    t_h = t_h + [P.last("act"), P.last("dve")]
    barrier()
    cx.close()
    lw2 = sb(c, "lw2", [4, 1024])
    w0b = sb(c, "w0b", [2, 1024])
    t_w2 = P.dma("lw2", lw2[:, :, :], T["lw2"])
    t_w0 = P.dma("w0b", w0b[:, :, :], T["w0b"])
    tl = sb(c, "tl", [NT])
    la = sb(c, "la", [NT])
    omu = sb(c, "omu", [2, 26])
    pads = [sb(c, f"pad{i}", [772]) for i in range(2)]
    sss = [sb(c, f"ss{i}", [772]) for i in range(2)]
    s7 = [sb(c, f"s7{i}", [7, NT]) for i in range(2)]
    kb = [sb(c, f"km{i}", [NT]) for i in range(2)]
    gbuf = [sb(c, f"gbuf{i}", [2, NT]) for i in range(2)]
    sqb = [sb(c, f"sqb{i}", [2, NT]) for i in range(1)] * 2
    sgb = [sb(c, f"sgb{i}", [1024]) for i in range(1)] * 2
    t_mu1 = ts("dve", omu[:, 0, :], Q("mu"), -1.0, 1.0, ALU.mult, ALU.add, t_par)
    t_mu2 = ts("dve", omu[:, 1, :], Q("mu"), 0.5, None, ALU.mult, None)
    t_zero = None
    for i in range(2):
        for cc in (0, 257, 770):
            t_zero = P.op("pool", lambda e, i=i, cc=cc: e.memset(pads[i][:, cc:cc + 1], 0.0))
    nmix = [0]
    padfree = [None, None]

    def mix(wsrc, mucol, dst, *free):
        i = nmix[0] % 2
        nmix[0] += 1
        pad, ss = pads[i], sss[i]
        res, t = proj_cm(wsrc, hT, NT, t_h)
        for (b, a, e_) in res:
            o = 1 if a == 0 else 2
            tp = copy("act", pad[:, a + o:e_ + o], psum[:, b, 0:e_ - a], t, t_zero, padfree[i])
            bank_free[b] = [tp]
        t1 = tt("dve", ss[:, 0:769], pad[:, 0:769], pad[:, 2:771], ALU.add, tp)
        last = None
        for a, e_, o in ((0, 256, 0), (256, 768, 1)):
            tu = act(dst[:, a:e_], pad[:, a + o + 1:e_ + o + 1], ACT.Copy, tp, t_mu1, *free,
                     scale=omu[:, 0, mucol:mucol + 1])
            last = stt(dst[:, a:e_], ss[:, a + o:e_ + o], omu[:, 1, mucol:mucol + 1], dst[:, a:e_],
                       ALU.mult, ALU.add, t1, tu, t_mu2)
        padfree[i] = last
        return last

    t_lw = mix(T["rw_in"][32], 24, tl)
    t_tl = act(tl[:, :], tl[:, :], ACT.Tanh, t_lw)
    t_la = mix(T["rw_in"][33], 25, la)
    stored = []
    sfree = [None, None]
    sgfree = [None, None]
    M_ = {}

    def project(gp):
        u = gp % 2
        f = sfree[u]
        X = M_[gp] = {}
        X["k"] = mix(T["rw_in"][8 + gp], 8 + gp, kb[u], f)
        yield
        X["r"] = mix(T["rw_in"][gp], gp, s7[u][:, 2, :], f)
        yield
        X["v"] = mix(T["rw_in"][16 + gp], 16 + gp, s7[u][:, 4, :], f)
        yield
        res, t = proj_cm(T["rw_in"][24 + gp], hT, NT, t_h)
        for (i, a, b) in res:
            t = act(gbuf[u][:, 0, a:b], psum[:, i, 0:b - a], ACT.Silu, t, f)
            bank_free[i] = [t]
        X["g"] = t
        yield

    def post(gp):
        u = gp % 2
        X = M_[gp]
        S7, k = s7[u], kb[u]
        sq, rr = sqb[u][:, 0, :], sqb[u][:, 1, :]
        col = Q("kk", gp, 1)
        t = ts("dve", S7[:, 3, :], k[:, :], col, None, ALU.mult, None, X["k"], sfree[u])
        tq = act(sq, S7[:, 3, :], ACT.Square, t, P.last("dve"), P.last("pool"))
        yield
        t = rstd([sq], spans(NT), rr, blk, 1e-12, 1.0, tq)
        t_kk = tt("dve", S7[:, 3, :], S7[:, 3, :], rr, ALU.mult, t)
        yield
        tb = {}
        for d in range(2):
            bd, kd = S7[:, 0 if d == 0 else 5, :], S7[:, 1 if d == 0 else 6, :]
            for a, b in spans(NT):
                i = bank()
                t = mms([(psum[:, i, 0:b - a], lw2[:, 2 + d, 128 * gp:128 * gp + 128], la[:, a:b], True, True)],
                        t_w2, t_la, bank_free[i])
                ta = act(bd[:, a:b], psum[:, i, 0:b - a], ACT.Sigmoid, t, sfree[u], bias=Q("a0", 8 * d + gp, 1))
                bank_free[i] = [ta]
            t = ts("dve", kd, bd, -1.0, Q("ka", gp, 1), ALU.add, ALU.mult, ta)
            t_kd = stt(kd, kd, 1.0, k[:, :], ALU.add, ALU.mult, t, X["k"])
            tb[d] = (t_kd, stt(bd, bd, -1.0, S7[:, 3, :], ALU.mult, ALU.mult, ta, t_kk))
        yield
        bon = sq
        t = tt("dve", bon, S7[:, 1, :], S7[:, 6, :], ALU.add, tb[0][0], tb[1][0])
        t = stt(bon, bon, Q("rk", gp, 1), S7[:, 2, :], ALU.mult, ALU.mult, t, X["r"])
        for a, b in spans(NT):
            i = bank()
            t1 = mms([(psum[:, i, 0:b - a], blk, bon[:, a:b], True, True)], t, bank_free[i])
            t1 = tt("dve", gbuf[u][:, 1, a:b], psum[:, i, 0:b - a], S7[:, 4, a:b], ALU.mult, t1, X["v"], sfree[u])
            bank_free[i] = [t1]
        w = [tb[0], tb[1]]
        w = [tb[0][1], tb[1][1], t1, X["g"], X["v"], X["r"]]
        td = []
        for n in range(6):
            td.append(P.dma(f"st{u}{n}", T["str"][gp, n], S7[:, :, 128 * n:128 * n + 128], *w, e="pool"))
        td.append(P.dma(f"sbg{u}", T["bg"][gp], gbuf[u][:, :, :], *w, e="pool"))
        sfree[u] = td + [t1, tb[0][1], tb[1][1]]
        stored.extend(td)
        yield

    nsg = [0]

    def decays():
        for d in range(2):
            for n in range(6):
                u = nsg[0] % 2
                nsg[0] += 1
                for z in range(2):
                    i = bank()
                    t = mms([(psum[:, i, :], tl[:, 128 * n:128 * n + 128], lw2[:, d, 512 * z:512 * z + 512],
                              True, True)], t_w2, t_tl, bank_free[i])
                    t = tt("dve", sgb[u][:, 512 * z:512 * z + 512], psum[:, i, :], w0b[:, d, 512 * z:512 * z + 512],
                           ALU.add, t, t_w0, sgfree[0])
                    bank_free[i] = [t]
                t = act(sgb[u][:, :], sgb[u][:, :], ACT.Sigmoid, t)
                t = P.dma("sgst", T["sg"][d, n], sgb[u][:, :], t, e="pool")
                sgfree[0] = t
                stored.append(t)
                yield

    weave(project(0))
    dg = decays()
    mg = g_.modulation(1, mods)
    for gp in range(8):
        fill = [(dg, 12), (mg, 25)] if gp == 0 else []
        if gp < 7:
            pace((post(gp), 4), (project(gp + 1), 4), *fill)
        else:
            weave(post(gp))
    P.t_mod = mods[1]
    barrier()
    stored = P.final(stored)
    for e in P.q:
        P.wait(e, stored)
    c.close()

    c = ExitStack()
    rc = sb(c, "rc", [NRC])
    t_rc = P.dma("rc", rc[:, :], T["rc"])
    TRI = lambda d: rc[:, 256 * d:256 * d + 256]
    MSK = lambda d: rc[:, 512 + 256 * d:512 + 256 * d + 256]
    LVL = lambda d, l: rc[:, 1024 + (6 * d + l) * 128:1024 + (6 * d + l + 1) * 128]
    NL = 3
    ld = sb(c, "ld", [NL, 2, 2, 5, 128])
    sgl = sb(c, "sgl", [NL, 2, 256])
    oTs = sb(c, "oT", [2, 2, NT])
    trs_ = sb(c, "tr", [2, 2, 1792])
    inv = c.enter_context(nc.sbuf_tensor("inv", [128, 2, 2048], F32R))
    idr = c.enter_context(nc.sbuf_tensor("idr", [128, 128], F32R))
    t_idr = copy("dve", idr[:, :], ident, t_con)
    S = sb(c, "S", [2, 2, 2, 128])
    keep = sb(c, "keep", [3, 2, 2560])
    pcs = sb(c, "pcs", [3, 2, 4])
    K2 = {}
    for z in range(3):
        for d in range(2):
            o = 0
            for nm, w in (("rho", 256), ("Lb", 512), ("Lk", 512), ("kt", 256), ("bt", 256), ("vt", 256),
                          ("W1", 256), ("W2", 256)):
                K2[z, nm, d] = keep[:, z, d, o:o + w]
                o += w
    Ut2 = sb(c, "Ut", [2, 2, 256])
    F_ = [0, 1, 2, 3, 4, 5]
    B_ = [1, 0, 5, 4, 3, 2]
    hl = [(j, p) for j in range(2) for p in range(2)]
    X2 = {}
    hs = lambda ap, h: ap[:, 128 * h:128 * h + 128]
    b2 = lambda ap: ap.rearrange("p (q t) -> p q t", q=2)
    v4 = lambda ap: ap.rearrange("p (h t) -> p h t", h=4)
    t_z = P.op("dve", lambda e: e.memset(S[:, :, :, :, :], 0.0))
    s_cur = {0: 0, 1: 0}
    t_s = {0: t_z, 1: t_z}
    t_o = {g: [] for g in range(4)}
    ofree = {0: None, 1: None}
    readers = {}

    def fetch(u):
        g, m = divmod(u, 6)
        tile = (F_[m], B_[m])
        w = u % NL
        X = X2[u] = {}
        for d in range(2):
            a = 0 if d == 0 else 2
            src = T["str"][2 * g:2 * g + 2, tile[d], :, a:a + 5, :].rearrange("q p n t -> p q n t")
            f = readers.get(u - NL)
            t1 = P.dma(f"ld{w}{d}", ld[:, w, d].rearrange("p q n t -> p q (n t)"),
                       src.rearrange("p q n t -> p q (n t)"), stored, f)
            t2 = P.dma(f"sl{w}{d}", sgl[:, w, d, :], T["sg"][d, tile[d], :, 256 * g:256 * g + 256], f)
            X[d] = {"t_ld": t1, "t_sg": t2}

    t_osp = []

    def prepare(u):
        g, m = divmod(u, 6)
        tile = (F_[m], B_[m])
        z = u % 3
        x = X2[u]
        w = u % NL
        pw = [P.last("pe"), P.last("dve"), P.last("act"), P.last("pool")]
        for d in range(2):
            X = x[d]
            X["tok"] = slice(128 * tile[d], 128 * tile[d] + 128)
            tr = trs_[:, u % 2]
            L5 = lambda nm, d=d: ld[:, w, d, :, {"b": 0, "kd": 1, "r": 2, "kk": 3, "v": 4}[nm] if d == 0 else
                                    {"r": 0, "kk": 1, "v": 2, "b": 3, "kd": 4}[nm], :]
            t_ld, t_sg = X["t_ld"], X["t_sg"]
            K_ = {nm: K2[z, nm, d] for nm in ("rho", "Lb", "Lk", "kt", "bt", "vt", "W1", "W2")}
            Pinv = at = tr[:, d, 0:256]
            AR = tr[:, d, 256:768].rearrange("p (q s t) -> p q s t", q=2, s=2)
            be, ka = tr[:, d, 768:1024], tr[:, d, 1024:1280]
            LKs = tr[:, d, 768:1280]
            LA = tr[:, d, 1280:1792]
            i = bank()
            t = mms([(psum[:, i, 256 * p:256 * p + 256], sgl[:, w, d, 128 * p:128 * p + 128], TRI(d),
                      True, True) for p in range(2)], t_sg, t_rc, bank_free[i])
            cum = psum[:, i, :].rearrange("p (q s t) -> p q s t", q=2, s=2)
            t1 = act(AR[:, :, 1, :], cum[:, :, 0, :], ACT.Exp, t, *pw)
            t2 = act(b2(Pinv), cum[:, :, 0, :], ACT.Exp, scale=-1.0)
            t3 = act(AR[:, :, 0, :], cum[:, :, 1, :], ACT.Exp)
            bank_free[i] = [t3]
            e0 = 63 if d == 0 else 0
            tpc = copy("pool", pcs[:, z, d, :].rearrange("p (q c) -> p q c", q=2), AR[:, :, 1, e0:128:64], t1, *pw)
            ta2 = tt("dve", AR[:, :, 0, :], AR[:, :, 0, :], L5("kk"), ALU.mult, t3, t_ld)
            ta1 = tt("dve", AR[:, :, 1, :], AR[:, :, 1, :], L5("r"), ALU.mult, t1, tpc, t_ld)
            tb = tt("pool", b2(be), b2(Pinv), L5("b"), ALU.mult, t2, t_ld, *pw)
            tk_ = tt("dve", b2(ka), b2(Pinv), L5("kd"), ALU.mult, t2, t_ld)
            X["tro"] = copy("pool", b2(K_["rho"]), AR[:, :, 1, :], ta1)
            yield
            i = bank()
            t = transposes([(psum[:, i, 128 * p:128 * p + 128], b2(be)[:, p, :]) for p in range(2)] +
                           [(psum[:, i, 256 + 128 * p:384 + 128 * p], b2(ka)[:, p, :]) for p in range(2)],
                           tb, tk_, bank_free[i])
            t4 = copy("act", K_["bt"], psum[:, i, 0:256], t)
            t5 = copy("act", K_["kt"], psum[:, i, 256:512])
            bank_free[i] = [t5]
            i = bank()
            t = transposes([(psum[:, i, 128 * p:128 * p + 128], AR[:, p, 0, :]) for p in range(2)] +
                           [(psum[:, i, 256 + 128 * p:384 + 128 * p], L5("v")[:, p, :]) for p in range(2)],
                           ta2, t_ld, bank_free[i])
            readers.setdefault(u, []).extend([t, ta1, ta2, tb, tk_])
            t6 = copy("act", at, psum[:, i, 0:256], t, tk_, tb)
            t7 = copy("act", K_["vt"], psum[:, i, 256:512])
            bank_free[i] = [t7]
            X.update(t7=t7, t6=t6)
            yield
            msk = MSK(d).rearrange("p (s t) -> p s t", s=2)
            got = []
            for which, src in ((0, be), (1, ka)):
                for j in range(2):
                    i = bank()
                    t = mms([(psum[:, i, 256 * p:256 * p + 256], b2(src)[64 * j:64 * j + 64, p, :],
                              AR[64 * j:64 * j + 64, p, :, :], True, True) for p in range(2)],
                            ta1, ta2, bank_free[i])
                    got.append((which, j, i, t))
            for which, j, i, t in got:
                pv = psum[:, i, :].rearrange("p (q s t) -> p q s t", q=2, s=2)
                strict = v4(LKs if which else LA)[:, 2 * j:2 * j + 2, :]
                incl = v4(K_["Lk" if which else "Lb"])[:, 2 * j:2 * j + 2, :]
                if which:
                    t = got[3][3]
                t = tt("dve", strict, pv[:, :, 0, :], msk[:, 0, :].unsqueeze(1).to_broadcast([128, 2, 128]),
                       ALU.mult, t)
                t_L = tt("dve", incl, pv[:, :, 1, :], msk[:, 1, :].unsqueeze(1).to_broadcast([128, 2, 128]),
                         ALU.mult)
                bank_free[i] = [t_L]
                if which == 0:
                    t_LA = t_L
            yield
            i = bank()
            t = mms([(psum[:, i, 64 * (2 * p + j):64 * (2 * p + j) + 64], hs(LKs, 2 * j + p),
                      K_["vt"][:, 64 * (2 * p + j):64 * (2 * p + j) + 64], True, True) for j, p in hl],
                    t_L, t7, bank_free[i])
            X["t_y0"] = copy("act", K_["W2"], psum[:, i, 0:256], t)
            bank_free[i] = [X["t_y0"]]
            X.update(LA=LA, at=at, K=K_, tpc=tpc, t_LA=t_LA)
            yield

    def invert(u):
        x = X2[u]
        pw = [P.last("pe"), P.last("dve"), P.last("act"), P.last("pool")]
        for d in range(2):
            X = x[d]
            D, E, Y, NTb = (inv[:, d, 512 * w:512 * w + 512] for w in range(4))
            LA, t_LA = X["LA"], X["t_LA"]
            lv = lambda l, d=d: LVL(d, l).unsqueeze(1).to_broadcast([128, 4, 128])
            idb = ident.unsqueeze(1).to_broadcast([128, 4, 128])
            t = tt("dve", v4(E), v4(LA), lv(0), ALU.mult, t_LA, *pw)
            X["t_e"] = tt("dve", v4(E), v4(E).bitcast(F32), idb, ALU.add, t)
            X["t_n"] = tt("pool", v4(NTb), v4(LA), lv(1), ALU.mult, t_LA, *pw)
            X.update(D=D, E=E, Y=Y, NTb=NTb, lv=lv)
        yield
        for d in range(2):
            X = x[d]
            i = bank()
            t = mms([(psum[:, i, 128 * h:128 * h + 128], hs(X["E"], h), idr[:, :], True, True) for h in range(4)],
                    X["t_e"], t_idr, bank_free[i])
            X["t_d"] = copy("act", X["D"], psum[:, i, :], t)
            bank_free[i] = [X["t_d"]]
        yield
        for l in range(1, 6):
            for d in range(2):
                X = x[d]
                i = bank()
                t = mms([(psum[:, i, 128 * h:128 * h + 128], hs(X["NTb"], h), hs(X["D"], h), True, True)
                         for h in range(4)], X["t_n"], X["t_d"], bank_free[i])
                X["ty"] = copy("act", X["Y"], psum[:, i, :], t)
                bank_free[i] = [X["ty"]]
                if l < 5:
                    X["t_n"] = tt("pool", v4(X["NTb"]), v4(X["LA"]), X["lv"](l + 1), ALU.mult, t)
            yield
            for d in range(2):
                X = x[d]
                i = bank()
                td = mms([(psum[:, i, 128 * h:128 * h + 128], hs(X["E"], h), hs(X["Y"], h), True, True)
                          for h in range(4)], X["ty"], X["t_e"], bank_free[i])
                if l < 5:
                    i2 = bank()
                    te = mms([(psum[:, i2, 128 * h:128 * h + 128], hs(X["Y"], h), hs(X["E"], h), True, True)
                              for h in range(4)], bank_free[i2])
                X["t_d"] = tt("dve", X["D"], X["D"].bitcast(F32), psum[:, i, :], ALU.add, td)
                bank_free[i] = [X["t_d"]]
                if l < 5:
                    X["t_e"] = tt("dve", X["E"], X["E"].bitcast(F32), psum[:, i2, :], ALU.add, te)
                    bank_free[i2] = [X["t_e"]]
            yield
        for d in range(2):
            X = x[d]
            i = bank()
            t = mms([(psum[:, i, 128 * h:128 * h + 128], hs(X["D"], h), idr[:, :], True, True)
                     for h in range(4)], X["t_d"], bank_free[i])
            X["t_e"] = copy("act", X["E"], psum[:, i, :], t)
            bank_free[i] = [X["t_e"]]
            i = bank()
            t = mms([(psum[:, i, 128 * h:128 * h + 128], hs(X["LA"], h), hs(X["D"], h).bitcast(F32), True, True)
                     for h in range(4)], bank_free[i])
            idb = ident.unsqueeze(1).to_broadcast([128, 4, 128])
            t1 = tt("pool", v4(X["D"]), idb, v4(X["D"]).bitcast(F32), ALU.subtract, t)
            X["ty"] = tt("dve", X["Y"], X["D"].bitcast(F32), psum[:, i, :], ALU.add, t1)
            bank_free[i] = [X["ty"]]
        yield
        for d in range(2):
            X = x[d]
            i = bank()
            t = mms([(psum[:, i, 128 * h:128 * h + 128], hs(X["Y"], h), hs(X["E"], h), True, True)
                     for h in range(4)], X["ty"], X["t_e"], bank_free[i])
            X["t_e"] = tt("dve", X["LA"], X["E"].bitcast(F32), psum[:, i, :], ALU.add, t)
            bank_free[i] = [X["t_e"]]
        yield
        for d in range(2):
            X = x[d]
            W1, W2 = X["K"]["W1"], X["K"]["W2"]
            i = bank()
            t = mms([(psum[:, i, 64 * (2 * p + j):64 * (2 * p + j) + 64], hs(X["LA"], 2 * j + p),
                      W2[:, 64 * (2 * p + j):64 * (2 * p + j) + 64], True, True) for j, p in hl],
                    X["t_e"], X["t_y0"], bank_free[i])
            X["t_w2"] = copy("act", W2, psum[:, i, 0:256], t)
            bank_free[i] = [X["t_w2"]]
            i = bank()
            t = mms([(psum[64 * j:64 * j + 64, i, 128 * p:128 * p + 128],
                      X["at"][:, 64 * (2 * p + j):64 * (2 * p + j) + 64], hs(X["LA"], 2 * j + p), True, True)
                     for j, p in hl], X["t6"], bank_free[i])
            X["t_w1"] = copy("act", W1, psum[:, i, 0:256], t)
            bank_free[i] = [X["t_w1"]]

    def chain(u):
        g, m = divmod(u, 6)
        tile = (F_[m], B_[m])
        z = u % 3
        x = X2[u]
        oT = oTs[:, g % 2]
        if m == 0 and g:
            for d in range(2):
                t_s[d] = P.op("dve", lambda e, d=d, s=s_cur[d]: e.memset(S[:, d, s], 0.0), P.last("pe"), t_s[d])
        K_ = {(nm, d): K2[z, nm, d] for nm in ("rho", "Lb", "Lk", "kt", "bt", "vt", "W1", "W2") for d in range(2)}
        Ut = Ut2[:, u % 2]
        for s in range(2):
            half = (s, 1 - s)
            iu = bank()
            P.wait("pe", bank_free[iu])
            for d in range(2):
                r0 = 64 * half[d]
                w1 = b2(K_["W1", d])
                t_u = mms([(psum[r0:r0 + 64, iu, 128 * p:128 * p + 128], w1[:, p, r0:r0 + 64],
                            S[:, d, s_cur[d], p, :], True, True) for p in range(2)], x[d]["t_w1"], t_s[d])
            for d in range(2):
                r0 = 64 * half[d]
                x[d]["t_u"] = tt("dve", Ut[r0:r0 + 64, d, :], psum[r0:r0 + 64, iu, 0:256],
                                 K_["W2", d][r0:r0 + 64, :], ALU.add, t_u, x[d]["t_w2"])
            bank_free[iu] = [x[1]["t_u"]]
            for d in range(2):
                r0 = 64 * half[d]
                if s == 0:
                    x[d]["io"] = bank()
                    P.wait("pe", bank_free[x[d]["io"]])
                io = x[d]["io"]
                x[d]["t_os"] = mms([(psum[:, io, 256 * s + 64 * p:256 * s + 64 * p + 64], S[:, d, s_cur[d], p, :],
                                     b2(K_["rho", d])[:, p, r0:r0 + 64], True, True) for p in range(2)],
                                   x[d]["tro"])
            yield
            for d in range(2):
                r0 = 64 * half[d]
                sc = s_cur[d]
                sn = 1 - sc
                i = bank()
                lst = []
                for p in range(2):
                    o_ = psum[:, i, 128 * p:128 * p + 128]
                    cs = slice(128 * p, 128 * p + 128)
                    lst += [(o_, K_["kt", d][r0:r0 + 64, cs], K_["vt", d][r0:r0 + 64, cs], True, False),
                            (o_, K_["bt", d][r0:r0 + 64, cs], Ut[r0:r0 + 64, d, cs], False, True)]
                ts_ = mms(lst, x[d]["t_u"], bank_free[i])
                pc = b2(pcs[:, z, d, :])[:, :, half[d]:half[d] + 1]
                for j in range(2):
                    q0 = 64 * j
                    src = psum[q0:q0 + 64, i, 0:256].rearrange("p (q v) -> p q v", q=2)[:, :, q0:q0 + 64]
                    so = S[q0:q0 + 64, d, sc, :, q0:q0 + 64]
                    sd = S[q0:q0 + 64, d, sn, :, q0:q0 + 64]
                    t = tt("dve", sd, src, so, ALU.add, ts_, t_s[d])
                    t_n2 = tt("dve", sd, sd, pc[q0:q0 + 64].to_broadcast([64, 2, 64]), ALU.mult, t, x[d]["tpc"])
                bank_free[i] = [t]
                t_s[d] = t_n2
                s_cur[d] = sn
            yield
        for d in range(2):
            X = x[d]
            i = bank()
            lst = []
            for j, p in hl:
                o_ = psum[64 * j:64 * j + 64, i, 128 * p:128 * p + 128]
                cs = slice(64 * (2 * p + j), 64 * (2 * p + j) + 64)
                lst += [(o_, K_["vt", d][:, cs], hs(K_["Lk", d], 2 * j + p), True, False),
                        (o_, Ut[:, d, cs], hs(K_["Lb", d], 2 * j + p), False, True)]
            t = mms(lst, X["t_u"], bank_free[i])
            first = (tile[d], d) in ((0, 0), (1, 1), (2, 0), (3, 0), (4, 1), (5, 1))
            od = oT[:, :, X["tok"]]
            src = psum[:, i, 0:256].rearrange("p (q t) -> p q t", q=2)
            if first:
                t1 = copy("act", od, src, t, ofree[g % 2])
            else:
                t1 = tt("dve", od, od, src, ALU.add, t, t_o[g])
            bank_free[i] = [t1]
            io = X["io"]
            for s in range(2):
                hf = s if d == 0 else 1 - s
                o2 = oT[:, :, 128 * tile[d] + 64 * hf:128 * tile[d] + 64 * hf + 64]
                t1 = tt("dve", o2, o2, psum[:, io, 256 * s:256 * s + 128].rearrange("p (q t) -> p q t", q=2),
                        ALU.add, t1, X["t_os"])
            bank_free[io] = [t1]
            t_o[g].append(t1)
            yield
        if m == 5:
            ofree[g % 2] = P.dma(f"os{g % 2}", T["o"][:, 2 * g:2 * g + 2, :], oT, t_o[g])
            t_osp.append(ofree[g % 2])

    fetch(0)
    fetch(1)
    weave(prepare(0))
    fetch(2)
    pace((invert(0), 15), (prepare(1), 8))
    for u in range(24):
        if u + 3 < 24:
            fetch(u + 3)
        parts = [(chain(u), 7)]
        if u + 1 < 24:
            parts.append((invert(u + 1), 15))
        if u + 2 < 24:
            parts.append((prepare(u + 2), 8))
        pace(*parts)
    barrier()
    for e in P.q:
        P.wait(e, t_osp)
    c.close()

    c = ExitStack()
    g_.Ring(c, "wo", 6)
    yT = sb(c, "yT", [8, NT])
    xT = sb(c, "xTb", [8, NT])
    t_xl = P.dma("xl", xT[:, :, :], T["x"], e="act")
    ol = [sb(c, f"ol{i}", [NT]) for i in range(4)]
    bgl = [sb(c, f"bgl{i}", [2, NT]) for i in range(4)]
    sq4 = [sb(c, f"sq4{i}", [2, NT]) for i in range(2)]
    t_y = []
    lfree = [None] * 4

    def readout(gp):
        u = gp % 4
        o, bg = yT[:, gp, :], bgl[u]
        to = P.dma(f"ol{u}", ol[u][:, :], T["o"][:, gp, :], lfree[u], e="act")
        tb = P.dma(f"bgl{u}", bg[:, :, :], T["bg"][gp], lfree[u], e="act")
        yield
        sq, rr = sq4[gp % 2][:, 0, :], sq4[gp % 2][:, 1, :]
        for a, b in spans(NT):
            i = bank()
            t = mms([(psum[:, i, 0:b - a], blk, ol[u][:, a:b], True, True)], to, bank_free[i])
            t = stt(o[:, a:b], psum[:, i, 0:b - a], -1.0 / 64, ol[u][:, a:b], ALU.mult, ALU.add, t)
            bank_free[i] = [t]
        yield
        tq = act(sq, o, ACT.Square, t, P.last("pool"), P.last("dve"))
        yield
        tr_ = rstd([sq], spans(NT), rr, blk, 64e-5, 64.0, tq)
        yield
        t = tt("dve", o, o, rr, ALU.mult, tr_)
        t = ts("dve", o, o, Q("gn_g", gp, 1), Q("gn_b", gp, 1), ALU.mult, ALU.add, t)
        t = tt("dve", o, o, bg[:, 1, :], ALU.add, tb, t)
        t = tt("dve", o, o, bg[:, 0, :], ALU.mult, t)
        lfree[u] = [t, P.last("pe")]
        t_y.append(t)

    weave(readout(0), readout(1))
    weave(readout(2), readout(3))
    weave(readout(4), readout(5))
    weave(readout(6), readout(7))
    for k in range(8):
        res, t = proj_cm(T["rw_out"][k], yT, NT, t_y)
        for (i, a, b) in res:
            s = 1 if a == 0 else 0
            tx = stt(xT[:, k, a:b], psum[:, i, 0:b - a], modc[:, 16 + k, s:s + 1], xT[:, k, a:b], ALU.mult, ALU.add,
                     t, t_xl)
            bank_free[i] = [tx]
    P.t_x1 = P.dma("xs", T["x1"], xT[:, :, :], tx)
    barrier()
    for e in P.q:
        P.wait(e, P.t_x1)
    c.close()


class Scratch:

    def __init__(self, sb, c, W, tag, n):
        self.sets = [(sb(c, f"sq{tag}{i}", [W]), sb(c, f"R{tag}{i}", [W]), sb(c, f"tm{tag}{i}", [512])) for i in range(n)]
        self.free = [None] * n
        self.k = 0

    def take(self):
        i = self.k % len(self.sets)
        self.k += 1
        return i


def norm_rope(g_, buf, W, gcol, sc, t, table=None, a0=0):
    u = sc.take()
    sq, R, tmp = sc.sets[u]
    tq = g_.act(sq[:, 0:W], buf[:, 0:W], ACT.Square, t, sc.free[u])
    yield None
    tr = g_.rstd([sq], g_.spans(W), R, g_.blk, 1e-6, 64.0, tq)
    yield None
    t = g_.stt(buf[:, 0:W], buf[:, 0:W], gcol, R[:, 0:W], ALU.mult, ALU.mult, tr)
    sc.free[u] = [t]
    if table is None:
        yield t
        return
    yield None
    rot, cos, sin, t_tab = table
    i = g_.bank()
    n = W - a0
    tm = g_.mms([(g_.psum[:, i, 0:n], rot, buf[:, a0:W], True, True)], t, t_tab, g_.bank_free[i])
    t1 = g_.tt("dve", tmp[:, 0:n], g_.psum[:, i, 0:n], sin, ALU.mult, tm)
    g_.bank_free[i] = [t1]
    t2 = g_.tt("pool", buf[:, a0:W], buf[:, a0:W], cos, ALU.mult, tm)
    t3 = g_.tt("dve", buf[:, a0:W], buf[:, a0:W], tmp[:, 0:n], ALU.add, t1, t2)
    sc.free[u] = [t, t3]
    yield t3


def diff_layer(nc, P, T, g_):
    sb, act, copy, tt, ts, stt, mms, psum = g_.sb, g_.act, g_.copy, g_.tt, g_.ts, g_.stt, g_.mms, g_.psum
    bank, bank2, bank_free, C, Q = g_.bank, g_.bank2, g_.bank_free, g_.C, g_.Q
    modc, AB = g_.modcs[:, 1], g_.ABs[:, 1]
    barrier, proj_cm, proj_tm, transposes = g_.barrier, g_.proj_cm, g_.proj_tm, g_.transposes
    x2 = sb(g_.ctx, "x2", [8, 512])
    c = ExitStack()
    hT = sb(c, "hT1", [8, NT])
    yT = sb(c, "yT1", [8, 512])
    ac = sb(c, "ac", [NAC])
    t_ac = P.dma("ac", ac[:, :], T["ac"])
    g_.Ring(c, "wd", 5)
    t_ab = P.t_mod
    cx = ExitStack()
    xT = sb(cx, "xT1", [8, NT])
    t_x = P.dma("x1l", xT[:, :, :], T["x1"], P.t_x1)
    A = lambda k, s: AB[:, k, s:s + 1]
    B = lambda k, s: modc[:, k, s:s + 1]
    t_h = g_.normed(cx, xT, NT, hT, A, B, t_x, t_ab, "1", [(0, 256, 1), (256, 768, 0)])
    t_h = t_h + [P.last("act"), P.last("dve")]
    barrier()
    cx.close()
    sm = g_.sm
    lv = Q("lam")
    t1 = tt("dve", sm[:, 0:64], lv[:, 0:64], lv[:, 64:128], ALU.mult, g_.t_par)
    t1 = P.op("dve", lambda e: e.reduce_sum(sm[:, 64:65], sm[:, 0:64], AX.X), t1)
    t2 = tt("dve", sm[:, 0:64], lv[:, 128:192], lv[:, 192:256], ALU.mult, t1)
    t2 = P.op("dve", lambda e: e.reduce_sum(sm[:, 65:66], sm[:, 0:64], AX.X), t2)
    t3 = act(sm[:, 64:66], sm[:, 64:66], ACT.Exp, t2)
    t3 = tt("dve", sm[:, 66:67], sm[:, 65:66], sm[:, 64:65], ALU.subtract, t3)
    t_lam = ts("dve", sm[:, 67:68], sm[:, 66:67], -LAM_INIT, None, ALU.add, None, t3)
    t_sl = ts("dve", sm[:, 68:69], Q("subln"), 1.0 - LAM_INIT, None, ALU.mult, None)
    nlam = sm[:, 67:68]
    subl = sm[:, 68:69]

    def two(name, cols):
        return [sb(c, f"{name}{i}", cols) for i in range(2)]

    qb, kb, vb, gb = two("qb", [512]), two("kb", [NT]), two("vb", [6, 128]), two("gb", [512])
    sc = Scratch(sb, c, NT, "a", 3)
    NP_ = 3
    p0 = [sb(c, f"p0{i}", [NT]) for i in range(NP_)]
    p1 = [sb(c, f"p1{i}", [NT]) for i in range(NP_)]
    aT = two("aT", [6, 512])
    st = [sb(c, f"st{i}", [8]) for i in range(NP_)]
    cos, sin = ac[:, 512:1024], ac[:, 1280:1792]
    table = (ac[:, 0:128], cos, sin, t_ac)
    hl = hT[:, :, 256:768]
    fin = {0: None, 1: None}
    t_y = []
    npair = [0]
    pfree = [None] * NP_
    ready = {}

    def project(h):
        b = h % 2
        q, k, v, gg = qb[b], kb[b], vb[b], gb[b]
        f = fin[b]
        res, t = proj_cm(T["da_in"][h], hl, 512, t_h)
        tq = copy("act", q[:, :], psum[:, res[0][0], :], t, f)
        bank_free[res[0][0]] = [tq]
        yield
        res, t = proj_cm(T["da_in"][8 + h], hT, NT, t_h)
        for (i, a0, a1) in res:
            tk = copy("act", k[:, a0:a1], psum[:, i, 0:a1 - a0], t, f)
            bank_free[i] = [tk]
        yield
        gq = norm_rope(g_, q, 512, Q("qn"), sc, tq, table)
        gk = norm_rope(g_, k, NT, Q("kn"), sc, tk, table, 256)
        next(gq)
        tg = None
        v_done = []
        for n0, n1 in ((0, 4), (4, 6)):
            pass
        tv = proj_tm(T["da_in"][16 + h], hT, NT, t_h, v, "act", f)
        next(gk)
        yield
        next(gq)
        next(gk)
        res, t = proj_cm(T["da_in"][24 + h], hl, 512, t_h)
        tg = act(gg[:, :], psum[:, res[0][0], :], ACT.Silu, t, f)
        bank_free[res[0][0]] = [tg]
        yield
        next(gq)
        next(gk)
        yield
        tq = next(gq)
        tk = next(gk)
        yield
        ready[h] = (tq, tk, tv, tg)

    def attend(h):
        b = h % 2
        q, k, v, gg = qb[b], kb[b], vb[b], gb[b]
        tq, tk, tv, tg = ready[h]
        t_at = []
        S = {}

        def scores(qt):
            u = npair[0] % NP_
            npair[0] += 1
            s_ = st[u]
            pr = (p0[u], p1[u])
            te = []
            for cc in range(2):
                i = bank2()
                t = mms([(psum[:, i + (a0 // 512), 0:a1 - a0], q[64 * cc:64 * cc + 64, 128 * qt:128 * qt + 128],
                          k[64 * cc:64 * cc + 64, a0:a1], True, True) for a0, a1 in ((0, 512), (512, 768))],
                        tq, tk, bank_free[i], bank_free[i + 1])
                sp_ = psum[:, i:i + 2, :].rearrange("p a n -> p (a n)")[:, 0:768]
                t = P.op("dve", lambda e, sp_=sp_, cc=cc, s_=s_: e.reduce_max(s_[:, cc:cc + 1], sp_, AX.X), t, pfree[u])
                t = ts("dve", s_[:, cc:cc + 1], s_[:, cc:cc + 1], -0.125, None, ALU.mult, None, t)
                t = act(pr[cc][:, :], sp_, ACT.Exp, t, pfree[u], scale=0.125, bias=s_[:, cc:cc + 1],
                        accum=s_[:, 2 + cc:3 + cc])
                bank_free[i] = [t]
                bank_free[i + 1] = [t]
                te.append(t)
            S[qt] = (u, te)

        def combine(qt):
            u, te = S[qt]
            s_ = st[u]
            pr = (p0[u], p1[u])
            t = P.op("dve", lambda e, s_=s_: e.reciprocal(s_[:, 4:6], s_[:, 2:4]), te)
            t2 = ts("dve", s_[:, 5:6], s_[:, 5:6], nlam, None, ALU.mult, None, t, t_lam)
            ta = ts("dve", pr[1][:, :], pr[1][:, :], s_[:, 5:6], None, ALU.mult, None, t2)
            ta = stt(pr[0][:, :], pr[0][:, :], s_[:, 4:5], pr[1][:, :], ALU.mult, ALU.add, ta)
            for n0, n1 in ((0, 4), (4, 6)):
                i = bank()
                t = transposes([(psum[:, i, 128 * (n - n0):128 * (n - n0) + 128], pr[0][:, 128 * n:128 * n + 128])
                                for n in range(n0, n1)], ta, bank_free[i])
                t2 = copy("dve" if n0 else "act", aT[b][:, n0:n1, 128 * qt:128 * qt + 128],
                          psum[:, i, 0:128 * (n1 - n0)].rearrange("p (n c) -> p n c", c=128), t, fin[b])
                bank_free[i] = [t2]
                t_at.append(t2)
            pfree[u] = [t, ta]

        scores(0)
        yield
        for qt in range(4):
            if qt < 3:
                scores(qt + 1)
                yield
            combine(qt)
            yield
        i = bank()
        t_pv = mms([(psum[:, i, :], v[:, n, :], aT[b][:, n, :], n == 0, n == 5) for n in range(6)],
                   t_at, tv, bank_free[i])
        t = copy("act", yT[:, h, :], psum[:, i, :], t_pv)
        bank_free[i] = [t]
        u = sc.take()
        sq, R, _ = sc.sets[u]
        tq2 = act(sq[:, 0:512], yT[:, h, :], ACT.Square, t, sc.free[u])
        yield
        tr = g_.rstd([sq], [(0, 512)], R, g_.ones, 1e-5, 128.0, tq2)
        t = stt(yT[:, h, :], yT[:, h, :], subl, R[:, 0:512], ALU.mult, ALU.mult, tr, t_sl)
        sc.free[u] = [t]
        t = tt("pool", yT[:, h, :], yT[:, h, :], gg[:, :], ALU.mult, t, tg)
        fin[b] = [t_pv, t]
        t_y.append(t)

    weave(project(0))
    for h in range(8):
        if h < 7:
            weave(attend(h), project(h + 1))
        else:
            weave(attend(h))
    barrier()
    t_xl = P.dma("x1m", x2[:, :, :], T["x1"][:, :, 256:768])
    for k in range(8):
        res, t = proj_cm(T["da_out"][k], yT, 512, t_y)
        i = res[0][0]
        tx = stt(x2[:, k, :], psum[:, i, :], modc[:, 16 + k, 0:1], x2[:, k, :], ALU.mult, ALU.add, t, t_xl)
        bank_free[i] = [tx]
    P.x2, P.t_x2 = x2, tx
    barrier()
    c.close()


def second_block(nc, P, T, g_):
    sb, act, copy, tt, ts, stt, mms, psum = g_.sb, g_.act, g_.copy, g_.tt, g_.ts, g_.stt, g_.mms, g_.psum
    bank, bank2, bank_free, C, Q = g_.bank, g_.bank2, g_.bank_free, g_.C, g_.Q
    barrier, proj_cm, proj_tm, transposes = g_.barrier, g_.proj_cm, g_.proj_tm, g_.transposes
    x2, t_x = P.x2, P.t_x2
    c = g_.ctx
    g_.Ring(c, "we", 8)
    bc = sb(c, "bc", [NBC])
    t_bc = P.dma("bc", bc[:, :], T["bc"])
    mem = sb(c, "mem", [8, 256])
    t_mem = P.dma("mem", mem[:, :, :], T["mem"])
    hT = sb(c, "hT2", [8, 512])
    hm = sb(c, "hm2", [8, 256])
    yT = sb(c, "yT2", [8, 512])

    def two(name, cols):
        return [sb(c, f"{name}{i}", cols) for i in range(2)]

    qb, kb, vb, gb = two("qc", [512]), two("kc", [512]), two("vc", [4, 128]), two("gc", [512])
    sc = Scratch(sb, c, 512, "c", 3)
    NP_ = 4
    pr = [sb(c, f"pc{i}", [512]) for i in range(NP_)]
    aT = [sb(c, f"aTc{i}", [4, 512]) for i in range(3)]
    st = [sb(c, f"stc{i}", [8]) for i in range(NP_)]
    table = (bc[:, 0:128], bc[:, 128:640], bc[:, 640:1152], t_bc)
    fin = {0: None, 1: None}
    pfree = [None] * NP_
    afree = [None] * 3
    n_ = [0, 0]
    ready = {}

    def project(l, pi, t_h, t_m):
        kind = 0 if pi < 3 else (1 if pi < 6 else 2)
        b = pi % 2
        q, k, v, gg = qb[b], kb[b], vb[b], gb[b]
        f = fin[b]
        if kind < 2:
            base = 12 * kind + (pi - 3 * kind)
            wq, wk, wv, wg = (T["w_in2"][l, base + 3 * z] for z in range(4))
            nk, src, th2, tab = 512, hT, t_h, table
        else:
            r = pi - 6
            wq, wg = T["w_in2"][l, 24 + r], T["w_in2"][l, 26 + r]
            wk, wv = T["w_mkv"][l, r], T["w_mkv"][l, 2 + r]
            nk, src, th2, tab = 256, hm, t_m, None
        res, t = proj_cm(wq, hT, 512, t_h)
        tq = copy("act", q[:, :], psum[:, res[0][0], :], t, f)
        bank_free[res[0][0]] = [tq]
        yield
        res, t = proj_cm(wk, src, nk, th2)
        tk = copy("act", k[:, 0:nk], psum[:, res[0][0], 0:nk], t, f)
        bank_free[res[0][0]] = [tk]
        yield
        gq = norm_rope(g_, q, 512, Q("qkg", 6 * l + 2 * kind, 1), sc, tq, tab)
        gk = norm_rope(g_, k, nk, Q("qkg", 6 * l + 2 * kind + 1, 1), sc, tk, tab)
        next(gq)
        tv = proj_tm(wv, src, nk, th2, v, "act", f)
        next(gk)
        yield
        next(gq)
        next(gk)
        res, t = proj_cm(wg, hT, 512, t_h)
        tg = act(gg[:, :], psum[:, res[0][0], :], ACT.Silu, t, f)
        bank_free[res[0][0]] = [tg]
        yield
        tq, tk = next(gq), next(gk)
        yield
        if tab:
            tq, tk = next(gq), next(gk)
        ready[pi] = (tq, tk, tv, tg)

    def attend(pi):
        kind = 0 if pi < 3 else (1 if pi < 6 else 2)
        b = pi % 2
        q, k, v, gg = qb[b], kb[b], vb[b], gb[b]
        tq, tk, tv, tg = ready[pi]
        io = bank()
        P.wait("pe", bank_free[io])
        t_at = {0: [], 1: []}
        a_ = {}
        S = {}
        for j in range(2):
            a_[j] = n_[0] % 3
            n_[0] += 1

        def scores(j, qt):
            u = n_[1] % NP_
            n_[1] += 1
            s_, pp = st[u], pr[u]
            n = 128 * (qt + 1) if kind < 2 else 256
            i = bank()
            t = mms([(psum[:, i, 0:n], q[64 * j:64 * j + 64, 128 * qt:128 * qt + 128],
                      k[64 * j:64 * j + 64, 0:n], True, True)], tq, tk, bank_free[i])
            if kind < 2:
                o = (1152 if kind == 0 else 1664) + 384 - 128 * qt
                t = P.op("dve", lambda e: e.tensor_tensor_reduce(
                    out=pp[:, 0:n], in0=psum[:, i, 0:n], in1=bc[:, o:o + n], scale=1.0, scalar=-3.0e38,
                    op0=ALU.add, op1=ALU.max, accum_out=s_[:, 0:1]), t, pfree[u], t_bc)
                bank_free[i] = [t]
                ein = pp[:, 0:n]
            else:
                t = P.op("dve", lambda e: e.reduce_max(s_[:, 0:1], psum[:, i, 0:n], AX.X), t, pfree[u])
                ein = psum[:, i, 0:n]
            t = ts("dve", s_[:, 1:2], s_[:, 0:1], -0.125, None, ALU.mult, None, t)
            t = act(pp[:, 0:n], ein, ACT.Exp, t, scale=0.125, bias=s_[:, 1:2], accum=s_[:, 2:3])
            if kind == 2:
                bank_free[i] = [t]
            S[j, qt] = (u, n, t)

        def finish(j, qt):
            u, n, t = S[j, qt]
            s_, pp = st[u], pr[u]
            t = P.op("dve", lambda e: e.reciprocal(s_[:, 3:4], s_[:, 2:3]), t)
            ta = ts("dve", pp[:, 0:n], pp[:, 0:n], s_[:, 3:4], None, ALU.mult, None, t)
            i = bank()
            t = transposes([(psum[:, i, 128 * z:128 * z + 128], pp[:, 128 * z:128 * z + 128])
                            for z in range(n // 128)], ta, bank_free[i])
            pfree[u] = [t]
            t2 = copy("act" if qt % 2 else "dve", aT[a_[j]][:, 0:n // 128, 128 * qt:128 * qt + 128],
                      psum[:, i, 0:n].rearrange("p (n c) -> p n c", c=128), t, afree[a_[j]])
            bank_free[i] = [t2]
            t_at[j].append(t2)

        tpv = []

        def values(j):
            nkt = 4 if kind < 2 else 2
            lst = []
            for z in range(nkt):
                q0 = 128 * z if kind < 2 else 0
                lst.append((psum[64 * j:64 * j + 64, io, q0:512], v[:, z, 64 * j:64 * j + 64],
                            aT[a_[j]][:, z, q0:512], z == 0, z == nkt - 1))
            t = mms(lst, t_at[j], tv, skip=True)
            afree[a_[j]] = [t]
            tpv.append(t)

        order = [(j, qt) for j in range(2) for qt in range(4)]
        scores(*order[0])
        scores(*order[1])
        yield
        for z, (j, qt) in enumerate(order):
            if z + 2 < 8:
                scores(*order[z + 2])
            finish(j, qt)
            yield
            if z == 5:
                values(0)
        values(1)
        t = tt("dve", yT[:, pi, :], psum[:, io, :], gg[:, :], ALU.mult, tpv, tg)
        bank_free[io] = [t]
        fin[b] = [tpv[-1], t]
        t_y.append(t)

    for l in range(2):
        cl = ExitStack()
        A = lambda k, s: Q("ng2", 8 * l + k, 1)
        Am = lambda k, s: Q("mng2", 8 * l + k, 1)
        g_.normed(cl, mem, 256, hm, Am, None, t_mem, None, f"m{l}", [(0, 256, 0)], P.last("pe"))
        t_m = [P.last("dve"), P.last("act")]
        g_.normed(cl, x2, 512, hT, A, None, t_x, None, f"n{l}", [(0, 512, 0)], P.last("pe"))
        t_h = [P.last("dve"), P.last("act")]
        t_y = []
        weave(project(l, 0, t_h, t_m))
        for pi in range(8):
            if pi < 7:
                weave(attend(pi), project(l, pi + 1, t_h, t_m))
            else:
                weave(attend(pi))
        for k in range(8):
            res, t = proj_cm(T["w_out2"][l, k], yT, 512, t_y)
            i = res[0][0]
            tx = tt("dve", x2[:, k, :], psum[:, i, :], x2[:, k, :], ALU.add, t)
            bank_free[i] = [tx]
        t_x = tx
        cl.close()
        P.wait("act", P.last("pe"), P.last("dve"))
        P.wait("dve", P.last("pe"), P.last("act"))
    t = P.dma("out", T["out"], x2[:, :, :], t_x)
    P.wait("sp", t)


def kernel(**inputs):
    import numpy as _np
    import concourse.bacc as _bacc
    from concourse import mybir as _mybir
    from concourse.bass_utils import run_bass_kernel_spmd as _run

    I = {k: _np.asarray(v) for k, v in inputs.items()}

    def cm(a):
        return a.T.reshape(8, 128, -1).transpose(1, 0, 2)

    def wb(w):
        n = w.shape[-1] // 128
        lead = w.shape[:-2]
        k = len(lead)
        a = w.reshape(*lead, 8, 128, n, 128)
        return _np.ascontiguousarray(a.transpose(*range(k), k + 2, k + 1, k, k + 3))

    def cols(v):
        return v.reshape(-1, 128).T

    con, rc, ac, bc = constants()
    par = _np.zeros((128, NPAR), _np.float32)

    def put(name, a):
        o, w = PCOLS[name]
        par[:, o:o + w] = a.reshape(128, w)

    put("cs", _np.stack([cols(I["c"][0]), cols(I["c_ctx"])], axis=2))
    put("ada_b", _np.concatenate([cols(I["ada_b"][l]) for l in range(2)], axis=1))
    put("norm_g", _np.concatenate([cols(I["norm_g"][l]) for l in range(2)], axis=1))
    put("mu", cols(I["rw_mu"][0]))
    put("kk", cols(I["rw_kk"][0]))
    put("ka", cols(I["rw_ka"][0]))
    put("rk", cols(I["rw_rk"][0].reshape(-1)))
    put("gn_g", cols(I["rw_gn_g"][0]))
    put("gn_b", cols(I["rw_gn_b"][0]))
    put("a0", _np.concatenate([cols(I["rw_a0"][0, d]) for d in range(2)], axis=1))
    two = lambda v: _np.tile(v, 2)[:, None]
    put("qn", two(I["da_qn"][0]))
    put("kn", two(I["da_kn"][0]))
    put("subln", I["da_subln"][0][:, None])
    put("ng2", _np.concatenate([cols(I["norm_g_2"][l]) for l in range(2)], axis=1))
    put("mng2", _np.concatenate([cols(I["mem_norm_g_2"][l]) for l in range(2)], axis=1))
    put("qkg", _np.concatenate([two(I["qk_g_2"][l, i]) for l in range(2) for i in range(6)], axis=1))
    put("lam", _np.broadcast_to(I["da_lam"][0].reshape(1, 256), (128, 256)))
    lw2 = _np.zeros((128, 4, 1024), _np.float32)
    w0b = _np.zeros((128, 2, 1024), _np.float32)
    for d in range(2):
        lw2[64 * d:64 * d + 64, d] = I["rw_w2"][0, d]
        lw2[64 * d:64 * d + 64, 2 + d] = I["rw_a2"][0, d]
        w0b[:, d] = I["rw_w0"][0, d][None]
    w2 = I["w_in_2"]
    arrays = {
        "x": cm(_np.concatenate([I["ctx"][0], I["x"][0]], axis=0)),
        "mem": cm(I["mem_2"][0]),
        "con": con, "rc": rc, "ac": ac, "bc": bc, "par": par, "lw2": lw2, "w0b": w0b,
        "ada": wb(I["ada_w"]),
        "rw_in": wb(I["rw_in"][0]), "rw_out": wb(I["rw_out"][0]),
        "da_in": wb(I["da_in"][0]), "da_out": wb(I["da_out"][0]),
        "w_in2": wb(w2), "w_out2": wb(I["w_out_2"]), "w_mkv": wb(I["w_mem_kv_2"]),
    }
    nc = _bacc.Bacc("TRN2", target_bir_lowering=False, num_devices=1)
    T, feed = {}, {}
    for k, a in arrays.items():
        a = _np.ascontiguousarray(a)
        feed["in_" + k] = a
        T[k] = nc.dram_tensor("in_" + k, a.shape, _mybir.dt.float32, kind="ExternalInput").ap()
    for k, shape in (("str", (8, 6, 128, 7, 128)), ("bg", (8, 128, 2, 768)), ("sg", (2, 6, 128, 1024)),
                     ("o", (128, 8, 768))):
        T[k] = nc.dram_tensor("s_" + k + "_dram", shape, _mybir.dt.float32, kind="Internal").ap()
    T["x1"] = nc.dram_tensor("x1s", (128, 8, 768), _mybir.dt.float32, kind="Internal").ap()
    T["out"] = nc.dram_tensor("out_x", (128, 8, 512), _mybir.dt.float32, kind="ExternalOutput").ap()
    build(nc, T)
    r = _run(nc, [feed], core_ids=[0])
    o = r.results[0]["out_x"]
    return _np.ascontiguousarray(_np.asarray(o).transpose(2, 1, 0).reshape(1, 512, 1024))
```

```python
from contextlib import ExitStack
import math

import numpy as np

import concourse.bass as bass
from concourse import mybir

ALU = mybir.AluOpType
ACT = mybir.ActivationFunctionType
F32 = mybir.dt.float32
F32R = mybir.dt.float32r
AX = mybir.AxisListType

NCTX, NLAT, NT = 256, 512, 768
NEG = -1.0e30
DECAY = math.exp(-0.5)
LAM_INIT = 0.8 - 0.6 * math.exp(-0.3)

PCOLS = {}
_n = 0
for _name, _w in (("cs", 16), ("ada_b", 48), ("norm_g", 16), ("mu", 26), ("kk", 8), ("ka", 8), ("rk", 8),
                  ("gn_g", 8), ("gn_b", 8), ("a0", 16), ("qn", 1), ("kn", 1), ("subln", 1), ("ng2", 16),
                  ("mng2", 16), ("qkg", 12), ("lam", 256)):
    PCOLS[_name] = (_n, _w)
    _n += _w
NPAR = _n

CCOLS = {}
_n = 0
for _name, _w in (("ident", 128), ("ones", 128), ("blk", 128), ("eps", 8)):
    CCOLS[_name] = (_n, _w)
    _n += _w
NCON = _n
RCOLS = {"tri": (0, 512), "msk": (512, 512), "lvl": (1024, 2 * 6 * 128)}
NRC = 1024 + 1536
ACOLS = {"rot1": (0, 128), "rot2": (128, 128), "cos1": (256, 768), "sin1": (1024, 768)}
NAC = 1792
BCOLS = {"rot2": (0, 128), "cos2": (128, 512), "sin2": (640, 512), "mw1": (1152, 512), "mw2": (1664, 512)}
NBC = 2176


def constants():
    f = np.float32
    con = np.zeros((128, NCON), f)
    con[:, 0:128] = np.eye(128)
    con[:, 128:256] = 1.0
    i = np.arange(128)
    con[:, 256:384] = (i[:, None] // 64 == i[None] // 64)
    con[:, 384:392] = np.array([1e-6, 1e-5, 64e-5, 1e-12, 0, 0, 0, 0])[None]
    rc = np.zeros((128, NRC), f)
    j, t = i[:, None], i[None, :]
    same = (j // 64) == (t // 64)
    for d in range(2):
        incl = same & ((j <= t) if d == 0 else (j >= t))
        strict = same & ((j < t) if d == 0 else (j > t))
        rc[:, 256 * d:256 * d + 128] = -DECAY * incl
        rc[:, 256 * d + 128:256 * d + 256] = -DECAY * strict
        rc[:, 512 + 256 * d:512 + 256 * d + 128] = strict
        rc[:, 512 + 256 * d + 128:512 + 256 * d + 256] = incl
        for l in range(6):
            s = 1 << l
            b = (j // (2 * s)) == (t // (2 * s))
            jo, to = (j // s) % 2, (t // s) % 2
            m = b & ((jo == 0) & (to == 1) if d == 0 else (jo == 1) & (to == 0))
            rc[:, 1024 + (6 * d + l) * 128:1024 + (6 * d + l + 1) * 128] = m
    ac = np.zeros((128, NAC), f)
    inv = (np.float32(10000.0) ** (-np.arange(16, dtype=f) / f(16))).astype(f)
    tok = np.arange(512)
    rows, cols = (tok // 64).astype(f), (tok % 64).astype(f)
    ac[:, 256:1024] = 1.0
    for p in range(128):
        c = p % 64
        ax, half, fr = c // 32, (c // 16) % 2, c % 16
        ang = ((rows if ax == 0 else cols) * inv[fr]).astype(f)
        ac[p, 256 + 256:256 + 768] = np.cos(ang)
        ac[p, 1024 + 256:1024 + 768] = np.sin(ang)
        partner = p + 16 if half == 0 else p - 16
        ac[partner, p] = -1.0 if half == 0 else 1.0
    bc = np.zeros((128, NBC), f)
    inv = (np.float32(10000.0) ** (-np.arange(32, dtype=f) / f(32))).astype(f)
    for p in range(128):
        c = p % 64
        half, fr = c // 32, c % 32
        ang = (tok.astype(f) * inv[fr]).astype(f)
        bc[p, 128:640] = np.cos(ang)
        bc[p, 640:1152] = np.sin(ang)
        partner = p + 32 if half == 0 else p - 32
        bc[partner, p] = -1.0 if half == 0 else 1.0
    u = np.arange(512)
    dist = i[:, None] - (u[None] - 384)
    bc[:, 1152:1664] = np.where(dist >= 0, 0.0, NEG)
    mult = (dist <= 128).astype(f) + (dist % 4 == 0) + (dist % 16 == 0)
    ok = (dist >= 0) & (mult > 0)
    bc[:, 1664:2176] = np.where(ok, 8.0 * np.log(np.maximum(mult, 1.0)), NEG)
    return con, rc, ac, bc


class Prog:

    def __init__(self, nc, ctx):
        self.nc, self.ctx = nc, ctx
        self.q = {e: [] for e in ("pe", "act", "dve", "pool", "sp")}
        self.sem = {e: ctx.enter_context(nc.semaphore("s_" + e)) for e in self.q}
        self.n = {e: 0 for e in self.q}
        self.seen = {e: {} for e in self.q}
        self.slots = {}

    def wait(self, e, *toks):
        for t in toks:
            if t is None:
                continue
            if isinstance(t, list):
                self.wait(e, *t)
                continue
            s, v = t
            if self.seen[e].get(id(s), 0) < v:
                self.seen[e][id(s)] = v
                self.q[e].append(lambda eng, s=s, v=v: eng.wait_ge(s, v))

    def op(self, e, fn, *toks):
        self.wait(e, *toks)
        self.n[e] += 1
        s = self.sem[e]
        self.q[e].append(lambda eng: fn(eng).then_inc(s, 1))
        return (s, self.n[e])

    def quiet(self, e, fn, *toks):
        self.wait(e, *toks)
        self.q[e].append(fn)

    def dma(self, slot, dst, src, *toks, e="sp"):
        self.wait(e, *toks)
        if slot not in self.slots:
            self.slots[slot] = [self.ctx.enter_context(self.nc.semaphore("d_" + slot)), 0]
        r = self.slots[slot]
        r[1] += 16
        self.q[e].append(lambda eng, s=r[0]: eng.dma_start(dst, src).then_inc(s, 16))
        return (r[0], r[1])

    def last(self, e):
        return (self.sem[e], self.n[e]) if self.n[e] else None

    def final(self, toks):
        best = {}
        for s, v in toks:
            best[id(s)] = max(best.get(id(s), (s, 0)), (s, v), key=lambda t: t[1])
        return list(best.values())

    def play(self, e, eng):
        for f in self.q[e]:
            f(eng)


def build(nc, T):
    with ExitStack() as ctx:
        P = Prog(nc, ctx)
        body(nc, ctx, P, T)
        block = ctx.enter_context(nc.Block())

        @block.sync
        def _(e):
            P.play("sp", e)

        @block.gpsimd
        def _(e):
            P.play("pool", e)

        @block.scalar
        def _(e):
            P.play("act", e)

        @block.vector
        def _(e):
            P.play("dve", e)

        @block.tensor
        def _(e):
            P.play("pe", e)


def body(nc, ctx, P, T):
    def sb(c, name, cols):
        return c.enter_context(nc.sbuf_tensor(name, [128] + list(cols), F32))

    def pe(fn, *t):
        return P.op("pe", fn, *t)

    tables = [""]

    def act(out, in_, f, *t, scale=1.0, bias=0.0, accum=None):
        want = {ACT.Exp: "el", ACT.Ln: "el", ACT.Silu: "silu", ACT.Sigmoid: "sig", ACT.Tanh: "tanh"}.get(f)
        if want and want != tables[0]:
            tables[0] = want
            if want == "el":
                P.quiet("act", lambda e: e.preload_act_table_set("natural_log_exp_and_others"))
        if accum is None:
            return P.op("act", lambda e: e.activation(out, in_, f, bias=bias, scale=scale), *t)
        return P.op("act", lambda e: e.activation(out, in_, f, bias=bias, scale=scale, accum_out=accum), *t)

    def copy(e, out, in_, *t):
        if e == "act":
            return P.op("act", lambda g: g.activation(out, in_, ACT.Copy), *t)
        return P.op(e, lambda g: g.tensor_copy(out, in_), *t)

    def tt(e, out, a, b, o, *t):
        return P.op(e, lambda g: g.tensor_tensor(out, a, b, o), *t)

    def ts(e, out, a, s1, s2, o0, o1, *t):
        if o1 is None:
            return P.op(e, lambda g: g.tensor_scalar(out, a, s1, None, o0), *t)
        return P.op(e, lambda g: g.tensor_scalar(out, a, s1, s2, o0, o1), *t)

    def stt(out, a, s, b, o0, o1, *t):
        return P.op("dve", lambda g: g.scalar_tensor_tensor(out=out, in0=a, scalar=s, in1=b, op0=o0, op1=o1), *t)

    psum = ctx.enter_context(nc.psum_tensor("ps", [128, 8, 512], F32))
    bank_free = Banks()
    bank, bank2 = bank_free.take, bank_free.take2

    def mms(lst, *toks, skip=False):
        P.wait("pe", *toks)
        for k, (o, l, r, st, sp_) in enumerate(lst):
            f = lambda e, o=o, l=l, r=r, st=st, sp_=sp_: e.matmul(o, l, r, start=st, stop=sp_, skip_group_check=skip)
            if k == len(lst) - 1:
                return P.op("pe", f)
            P.quiet("pe", f)

    con = sb(ctx, "con", [NCON])
    par = sb(ctx, "par", [NPAR])
    t_con = P.dma("con", con[:, :], T["con"])
    t_par = P.dma("par", par[:, :], T["par"])
    P.t_in = [t_con, t_par]

    def C(name, a=0, n=None):
        o, w = CCOLS[name]
        return con[:, o + a:o + (w if n is None else a + n)]

    def Q(name, a=0, n=None):
        o, w = PCOLS[name]
        return par[:, o + a:o + (w if n is None else a + n)]

    ident, ones, blk = C("ident"), C("ones"), C("blk")
    EPS = {v: C("eps", k, 1) for k, v in enumerate((1e-6, 1e-5, 64e-5, 1e-12))}

    def transposes(lst, *toks):
        P.wait("pe", *toks)
        for k, (o, i) in enumerate(lst):
            f = lambda e, o=o, i=i: e.transpose(o, i, ident)
            if k == len(lst) - 1:
                return P.op("pe", f)
            P.quiet("pe", f)

    def sbr(c, name, cols):
        return c.enter_context(nc.sbuf_tensor(name, [128] + list(cols), F32R))

    def halves(out, src, eh, el, *toks):
        hi, lo = out
        t1 = copy(eh, hi, src, *toks)
        return [t1, tt(el, lo, src, hi.bitcast(F32), ALU.subtract, t1)]

    class Ring:

        def __init__(self, c, name, n, buf=None):
            self.buf, self.name, self.n, self.k = sb(c, name, [n, 8, 128]) if buf is None else buf, name, n, 0
            self.free = [[P.last(e) for e in ("pe", "act", "dve", "pool")]] * n

        def load(self, src):
            i = self.k % self.n
            self.k += 1
            return i, P.dma(f"{self.name}{i}", self.buf[:, i, :, :], src, self.free[i])

    class Halves:
        now = None

        def __init__(self, c, name, raw, n, plan, ahead=1, fill=True):
            self.raw, self.plan = Ring(c, name, raw), plan
            self.hi, self.lo = sbr(c, name + "h", [n, 8, 128]), sbr(c, name + "l", [n, 8, 128])
            self.n, self.ahead, self.k, self.made, self.loads, self.tok = n, ahead, 0, 0, [], {}
            self.free = [[P.last(e) for e in ("pe", "act", "dve", "pool")]] * n
            Halves.now = self
            if fill:
                self.fill()

        def fill(self):
            while len(self.loads) < min(len(self.plan), self.made + self.raw.n):
                self.loads.append(self.raw.load(self.plan[len(self.loads)]))

        def split(self, upto):
            while self.made < min(len(self.plan), upto):
                r, t = self.loads[self.made]
                i = self.made % self.n
                src = self.raw.buf[:, r, :, :]
                ts_ = halves((self.hi[:, i, :, :], self.lo[:, i, :, :]), src, "act", "pool", t, self.free[i])
                self.raw.free[r] = ts_
                self.tok[i] = ts_
                self.made += 1
                self.fill()

        def take(self):
            self.split(self.k + 1 + self.ahead)
            i = self.k % self.n
            self.k += 1
            return i, self.hi[:, i], self.lo[:, i], self.tok[i]

    sm = sb(ctx, "sm", [160])
    modcs = sb(ctx, "modc", [2, 24, 2])
    s0 = sb(ctx, "s0", [8, 2])
    ABs = sb(ctx, "AB", [2, 8, 2])
    t_cs = act(s0[:, :, :], Q("cs").rearrange("p (k s) -> p k s", s=2), ACT.Silu, t_par)

    def modulation(layer, done, at):
        modc, AB = modcs[:, layer], ABs[:, layer]
        P.wait("pe", t_cs, t_con)
        ab = Q("ada_b", 24 * layer, 24).unsqueeze(2).to_broadcast([128, 24, 2])
        free = [None, None]
        out = []
        for c in range(6):
            R, mrow = at(c)
            i = bank()
            for kk in range(4):
                w, tw = R.load(T["ada"][layer, c, kk].rearrange("p a (b n) -> p (a b) n", b=4))
                rows = R.buf[:, w, :, :].rearrange("p (a b) n -> p a (b n)", a=2)
                t = mms([(psum[0:2, i, :], s0[:, 2 * kk + e, :], rows[:, e, :], kk + e == 0, kk + e == 4)
                         for e in range(2)], tw, bank_free[i])
                R.free[w] = t
                yield
            tr = copy("act", mrow[0:2, c % 2, :], psum[0:2, i, :], t, free[c % 2])
            bank_free[i] = [tr]
            yield
            i = bank()
            t = mms([(psum[:, i, 2 * m:2 * m + 2], mrow[0:2, c % 2, 128 * m:128 * m + 128], ident[0:2, 0:2], True, True)
                     for m in range(4)], tr, bank_free[i])
            free[c % 2] = t
            t1 = tt("dve", modc[:, 4 * c:4 * c + 4, :], psum[:, i, 0:8].rearrange("p (m s) -> p m s", s=2),
                    ab[:, 4 * c:4 * c + 4, :], ALU.add, t, t_par)
            bank_free[i] = [t1]
            out.append(t1)
            yield
        t2 = ts("dve", AB, modc[:, 8:16, :], 1.0, None, ALU.add, None, out)
        g = Q("norm_g", 8 * layer, 8).unsqueeze(2).to_broadcast([128, 8, 2])
        done[layer] = tt("dve", AB, AB, g, ALU.mult, t2)

    def rstd(src_sq, widths, R, lhs, eps, n, t_sq):
        out = []
        for (a, b) in widths:
            i = bank()
            t = mms([(psum[:, i, 0:b - a], lhs, src_sq[:, a:b], True, True)], t_sq, bank_free[i], t_con)
            out.append(rstd_of(i, R[:, a:b], src_sq[:, a:b], eps, n, t))
        return out

    def rstd_of(i, r, M, eps, n, t):
        m = psum[:, i, 0:r.shape[-1]]
        t1 = act(r, m, ACT.Ln, t, scale=1.0 / n, bias=EPS[eps])
        t2 = act(r, r, ACT.Exp, t1, scale=-0.5)
        t3 = ts("dve", M, m, 0.5 / n, 0.5 * eps, ALU.mult, ALU.add, t1)
        bank_free[i] = [t3]
        t4 = tt("pool", M, M, r, ALU.mult, t2, t3)
        t5 = tt("pool", M, M, r, ALU.mult, t4)
        return P.op("dve", lambda e: e.scalar_tensor_tensor(out=r, in0=M, scalar=1.5, in1=r, op0=ALU.subtract,
                                                            op1=ALU.mult, reverse0=True), t5)

    def spans(W):
        return [(0, 256), (256, 768)] if W == 768 else ([(0, 512)] if W == 512 else [(0, 256)])

    def normed(c, xT, W, tag, hT, A, B, streams, tk, n=3, free=None, own=False):
        hi, lo = hT
        rows = [sb(c, f"row{i}" + tag, [W]) for i in range(n)]
        R_ = sb(c, "R" + tag, [W])
        rfree = [None] * n
        banks = [(bank(), a, b) for a, b in spans(W)]
        tq = {}
        for k in range(9):
            if k < 8:
                tq[k] = act(rows[k % n][:, :], xT[:, k, :], ACT.Square, tk[k], rfree[k % n])
            if k:
                r = rows[(k - 1) % n]
                for i, a, b in banks:
                    t = mms([(psum[:, i, 0:b - a], ones, r[:, a:b], k == 1, k == 8)], tq[k - 1], t_con, bank_free[i])
                rfree[(k - 1) % n] = t
            if k < 8:
                yield
        tr = [rstd_of(i, R_[:, a:b], rows[-1][:, a:b], 1e-6, 1024.0, t) for i, a, b in banks]
        rfree = [[f, tr] for f in rfree]
        tb, th, out = {}, {}, []

        def place(k):
            return xT[:, k, :] if own else rows[k % n][:, :]

        def low(k):
            out.append(tt("pool" if k % 2 else "dve", lo[:, k, 0:W], place(k), hi[:, k, 0:W].bitcast(F32),
                          ALU.subtract, th[k], free))
            rfree[k % n] = out[-1]

        for k in range(10):
            if k < 8:
                r = place(k)
                tb[k] = [stt(r[:, a:b], xT[:, k, a:b], A(k, s), R_[:, a:b], ALU.mult, ALU.mult, tk["ab"],
                             tr if own else rfree[k % n], tk["out"][k] if "out" in tk else None)
                         for a, b, s in streams]
            if 0 < k < 9:
                th[k - 1] = copy("act", hi[:, k - 1, 0:W], place(k - 1), tb[k - 1], free)
            if k < 8 and B is not None:
                tb[k] = [act(r[:, a:b], r[:, a:b], ACT.Identity, t, bias=B(k, s))
                         for t, (a, b, s) in zip(tb[k], streams)]
            if k > 1:
                low(k - 2)
        tk["h"] = out

    def product(hT, W, t_h, sink, o=0):
        hi, lo = hT
        Hv = Halves.now
        n, wh, wl, tw = Hv.take()
        last = []
        for a, b in spans(W):
            i = bank()
            P.wait("pe", tw, bank_free[i])
            z = psum[:, i, 0:b - a]
            for k in range(8):
                x, y = hi[:, k, o + a:o + b], lo[:, k, o + a:o + b]
                t = mms([(z, wh[:, k, :], x, k == 0, False), (z, wh[:, k, :], y, False, False),
                         (z, wl[:, k, :], x, False, k == 7)], t_h[k])
                if b - a > 256 and k == 3:
                    yield
            sink(i, a, b, t)
            Hv.free[n] = [t]
            yield

    def barrier():
        toks = [P.last(e) for e in ("pe", "act", "dve", "pool")]
        for e in P.q:
            P.wait(e, *toks)

    kit = Kit()
    kit.sb = sb
    kit.act = act
    kit.copy = copy
    kit.tt = tt
    kit.ts = ts
    kit.stt = stt
    kit.mms = mms
    kit.psum = psum
    kit.bank = bank
    kit.bank2 = bank2
    kit.bank_free = bank_free
    kit.C = C
    kit.Q = Q
    kit.ident = ident
    kit.ones = ones
    kit.blk = blk
    kit.modcs = modcs
    kit.ABs = ABs
    kit.Ring = Ring
    kit.transposes = transposes
    kit.rstd = rstd
    kit.spans = spans
    kit.product = product
    kit.Halves = Halves
    kit.halves = halves
    kit.sbr = sbr
    kit.barrier = barrier
    kit.t_con = t_con
    kit.t_par = t_par
    kit.modulation = modulation
    kit.normed = normed
    kit.sm = sm
    kit.ctx = ctx
    time_mix(nc, P, T, kit)
    diff_layer(nc, P, T, kit)
    second_block(nc, P, T, kit)


class Banks:

    def __init__(self):
        self.free = [[] for _ in range(8)]
        self.order = list(range(8))

    def __getitem__(self, i):
        return self.free[i]

    def __setitem__(self, i, toks):
        self.free[i] = toks
        self.order.append(i)

    def take(self):
        return self.order.pop(0)

    def take2(self):
        for i in self.order:
            j = i ^ 1
            if j in self.order:
                self.order.remove(i)
                self.order.remove(j)
                return min(i, j)
        raise RuntimeError("no two banks side by side")


def pace(*gens):
    left = [[0, n, g] for g, n in gens]
    while left:
        x = min(left, key=lambda x: (x[0] + 1) / x[1])
        x[0] += 1
        try:
            next(x[2])
        except StopIteration:
            left.remove(x)


def weave(*gens):
    gens = list(gens)
    while gens:
        for g in list(gens):
            try:
                next(g)
            except StopIteration:
                gens.remove(g)


def some(gen, n):
    for _ in range(n):
        if next(gen, 1):
            return
        yield


class Kit:
    pass


def time_mix(nc, P, T, g_):
    sb, act, copy, tt, ts, stt, mms, psum = g_.sb, g_.act, g_.copy, g_.tt, g_.ts, g_.stt, g_.mms, g_.psum
    bank, bank_free, C, Q = g_.bank, g_.bank_free, g_.C, g_.Q
    ident, blk, modc, AB = g_.ident, g_.blk, g_.modcs[:, 0], g_.ABs[:, 0]
    transposes, rstd, spans, product, barrier = g_.transposes, g_.rstd, g_.spans, g_.product, g_.barrier
    t_con, t_par = g_.t_con, g_.t_par
    A = lambda k, s: AB[:, k, s:s + 1]
    B = lambda k, s: modc[:, k, s:s + 1]

    c = ExitStack()
    hT = (g_.sbr(c, "hTh", [8, NT]), g_.sbr(c, "hTl", [8, NT]))
    plan = [T["rw_in"][32], T["rw_in"][33]]
    for gp in range(8):
        plan += [T["rw_in"][z + gp] for z in (8, 0, 16, 24)]
    hv = g_.Halves(c, "wa", 3, 2, plan, fill=False)
    cx = ExitStack()
    xT = sb(cx, "xT0", [8, NT])
    t_x = [P.dma(f"x{k}", xT[:, k, :], T["x"][:, k, :], e="act") for k in range(8)]
    mods = {}
    tk = dict(enumerate(t_x))
    nm = g_.normed(cx, xT, NT, "0", hT, A, B, [(0, 256, 1), (256, 768, 0)], tk, own=True)
    ring, mrow = g_.Ring(cx, "wm", 16), sb(cx, "mrow0", [2, 512])

    def sums():
        for k in range(8):
            next(nm)
            yield

    weave(g_.modulation(0, mods, lambda c: (ring, mrow)), sums())
    tk["ab"] = mods[0]
    hv.fill()
    hv.split(2)
    weave(nm)
    t_h = tk["h"]
    barrier()
    cx.close()
    lw2 = sb(c, "lw2", [4, 1024])
    w0b = sb(c, "w0b", [2, 1024])
    t_w2 = P.dma("lw2", lw2[:, :, :], T["lw2"])
    t_w0 = P.dma("w0b", w0b[:, :, :], T["w0b"])
    tl = sb(c, "tl", [NT])
    la = sb(c, "la", [NT])
    omu = sb(c, "omu", [2, 26])
    pads = [sb(c, f"pad{i}", [772]) for i in range(2)]
    sss = [sb(c, f"ss{i}", [772]) for i in range(2)]
    s7 = [sb(c, f"s7{i}", [7, NT]) for i in range(2)]
    kb = [sb(c, f"km{i}", [NT]) for i in range(2)]
    gbuf = [sb(c, f"gbuf{i}", [2, NT]) for i in range(2)]
    sqb = [sb(c, f"sqb{i}", [2, NT]) for i in range(1)] * 2
    sgb = [sb(c, f"sgb{i}", [1024]) for i in range(2)]
    t_mu1 = ts("dve", omu[:, 0, :], Q("mu"), -1.0, 1.0, ALU.mult, ALU.add, t_par)
    t_mu2 = ts("dve", omu[:, 1, :], Q("mu"), 0.5, None, ALU.mult, None)
    t_zero = None
    for i in range(2):
        for cc in (0, 257, 770):
            t_zero = P.op("pool", lambda e, i=i, cc=cc: e.memset(pads[i][:, cc:cc + 1], 0.0))
    nmix = [0]
    padfree = [None, None]

    def mix(mucol, dst, done, key, *free):
        i = nmix[0] % 2
        nmix[0] += 1
        pad, ss = pads[i], sss[i]
        tp = []

        def sink(b, a, e_, t):
            o = 1 if a == 0 else 2
            tp.append(copy("act", pad[:, a + o:e_ + o], psum[:, b, 0:e_ - a], t, t_zero, padfree[i]))
            bank_free[b] = [tp[-1]]

        yield from product(hT, NT, t_h, sink)
        t1 = tt("dve", ss[:, 0:769], pad[:, 0:769], pad[:, 2:771], ALU.add, tp)
        last = None
        for a, e_, o in ((0, 256, 0), (256, 768, 1)):
            tu = act(dst[:, a:e_], pad[:, a + o + 1:e_ + o + 1], ACT.Copy, tp, t_mu1, *free,
                     scale=omu[:, 0, mucol:mucol + 1])
            last = stt(dst[:, a:e_], ss[:, a + o:e_ + o], omu[:, 1, mucol:mucol + 1], dst[:, a:e_],
                       ALU.mult, ALU.add, t1, tu, t_mu2)
        padfree[i] = last
        done[key] = last

    L_ = {}
    weave(mix(24, tl, L_, "w"))
    t_tl = act(tl[:, :], tl[:, :], ACT.Tanh, L_["w"])
    weave(mix(25, la, L_, "a"))
    t_la = L_["a"]
    stored = []
    sfree = [None, None]
    sgfree = [None, None]
    M_ = {}

    def project(gp):
        u = gp % 2
        f = sfree[u]
        X = M_[gp] = {}
        yield from mix(8 + gp, kb[u], X, "k", f)
        yield from mix(gp, s7[u][:, 2, :], X, "r", f)
        yield from mix(16 + gp, s7[u][:, 4, :], X, "v", f)

        def sink(i, a, b, t):
            X["g"] = act(gbuf[u][:, 0, a:b], psum[:, i, 0:b - a], ACT.Silu, t, f)
            bank_free[i] = [X["g"]]

        yield from product(hT, NT, t_h, sink)

    def post(gp):
        u = gp % 2
        X = M_[gp]
        S7, k = s7[u], kb[u]
        sq, rr = sqb[u][:, 0, :], sqb[u][:, 1, :]
        col = Q("kk", gp, 1)
        t = ts("dve", S7[:, 3, :], k[:, :], col, None, ALU.mult, None, X["k"], sfree[u])
        tq = act(sq, S7[:, 3, :], ACT.Square, t, P.last("dve"), P.last("pool"))
        yield
        t = rstd(sq, spans(NT), rr, blk, 1e-12, 1.0, tq)
        t_kk = tt("dve", S7[:, 3, :], S7[:, 3, :], rr, ALU.mult, t)
        yield
        tb = {}
        for d in range(2):
            bd, kd = S7[:, 0 if d == 0 else 5, :], S7[:, 1 if d == 0 else 6, :]
            for a, b in spans(NT):
                i = bank()
                t = mms([(psum[:, i, 0:b - a], lw2[:, 2 + d, 128 * gp:128 * gp + 128], la[:, a:b], True, True)],
                        t_w2, t_la, bank_free[i])
                ta = act(bd[:, a:b], psum[:, i, 0:b - a], ACT.Sigmoid, t, sfree[u], bias=Q("a0", 8 * d + gp, 1))
                bank_free[i] = [ta]
            t = ts("dve", kd, bd, -1.0, Q("ka", gp, 1), ALU.add, ALU.mult, ta)
            t_kd = stt(kd, kd, 1.0, k[:, :], ALU.add, ALU.mult, t, X["k"])
            tb[d] = (t_kd, stt(bd, bd, -1.0, S7[:, 3, :], ALU.mult, ALU.mult, ta, t_kk))
            yield
        bon = sq
        t = tt("dve", bon, S7[:, 1, :], S7[:, 6, :], ALU.add, tb[0][0], tb[1][0])
        t = stt(bon, bon, Q("rk", gp, 1), S7[:, 2, :], ALU.mult, ALU.mult, t, X["r"])
        yield
        for a, b in spans(NT):
            i = bank()
            t1 = mms([(psum[:, i, 0:b - a], blk, bon[:, a:b], True, True)], t, bank_free[i])
            t1 = tt("dve", gbuf[u][:, 1, a:b], psum[:, i, 0:b - a], S7[:, 4, a:b], ALU.mult, t1, X["v"], sfree[u])
            bank_free[i] = [t1]
        w = [tb[0][1], tb[1][1], t1, X["g"], X["v"], X["r"]]
        td = []
        for n in range(6):
            td.append(P.dma(f"st{u}{n}", T["str"][gp, n], S7[:, :, 128 * n:128 * n + 128], *w, e="pool"))
        td.append(P.dma(f"sbg{u}", T["bg"][gp], gbuf[u][:, :, :], *w, e="pool"))
        sfree[u] = td + [t1, tb[0][1], tb[1][1]]
        stored.extend(td)
        yield

    nsg = [0]

    def decays():
        for d in range(2):
            for n in range(6):
                u = nsg[0] % 2
                nsg[0] += 1
                for z in range(2):
                    i = bank()
                    t = mms([(psum[:, i, :], tl[:, 128 * n:128 * n + 128], lw2[:, d, 512 * z:512 * z + 512],
                              True, True)], t_w2, t_tl, bank_free[i])
                    t = tt("dve", sgb[u][:, 512 * z:512 * z + 512], psum[:, i, :], w0b[:, d, 512 * z:512 * z + 512],
                           ALU.add, t, t_w0, sgfree[u])
                    bank_free[i] = [t]
                t = act(sgb[u][:, :], sgb[u][:, :], ACT.Sigmoid, t)
                t = P.dma(f"sgst{u}", T["sg"][d, n], sgb[u][:, :], t, e="pool")
                sgfree[u] = t
                stored.append(t)
                yield

    weave(project(0))
    dg = decays()
    for gp in range(8):
        if gp < 7:
            fill = [(some(dg, 6), 6)] if gp == 1 else []
            pace((post(gp), 7), (project(gp + 1), 12), *fill)
        else:
            pace((post(gp), 7), (dg, 6))
    barrier()
    stored = P.final(stored)
    for e in ("act", "dve", "pool", "sp"):
        P.wait(e, stored)
    c.close()

    c = ExitStack()
    rc = sb(c, "rc", [NRC])
    t_rc = P.dma("rc", rc[:, :], T["rc"])
    TRI = lambda d: rc[:, 256 * d:256 * d + 256]
    MSK = lambda d: rc[:, 512 + 256 * d:512 + 256 * d + 256]
    LVL = lambda d, l: rc[:, 1024 + (6 * d + l) * 128:1024 + (6 * d + l + 1) * 128]
    NL = 3
    ld = sb(c, "ld", [NL, 2, 2, 5, 128])
    sgl = sb(c, "sgl", [NL, 2, 256])
    oTs = sb(c, "oT", [2, 2, NT])
    trs_ = sb(c, "tr", [2, 2, 1792])
    inv = c.enter_context(nc.sbuf_tensor("inv", [128, 2, 2048], F32R))
    idr = c.enter_context(nc.sbuf_tensor("idr", [128, 128], F32R))
    t_idr = copy("dve", idr[:, :], ident, t_con)
    S = sb(c, "S", [2, 2, 2, 128])
    keep = sb(c, "keep", [3, 2, 2560])
    pcs = sb(c, "pcs", [3, 2, 4])
    K2 = {}
    for z in range(3):
        for d in range(2):
            o = 0
            for nm, w in (("rho", 256), ("Lb", 512), ("Lk", 512), ("kt", 256), ("bt", 256), ("vt", 256),
                          ("W1", 256), ("W2", 256)):
                K2[z, nm, d] = keep[:, z, d, o:o + w]
                o += w
    Ut2 = sb(c, "Ut", [2, 2, 256])
    F_ = [0, 1, 2, 3, 4, 5]
    B_ = [1, 0, 5, 4, 3, 2]
    hl = [(j, p) for j in range(2) for p in range(2)]
    X2 = {}
    hs = lambda ap, h: ap[:, 128 * h:128 * h + 128]
    b2 = lambda ap: ap.rearrange("p (q t) -> p q t", q=2)
    v4 = lambda ap: ap.rearrange("p (h t) -> p h t", h=4)
    t_z = P.op("dve", lambda e: e.memset(S[:, :, :, :, :], 0.0))
    s_cur = {0: 0, 1: 0}
    t_s = {0: t_z, 1: t_z}
    t_o = {g: [] for g in range(4)}
    ofree = {0: None, 1: None}
    readers = {}

    def fetch(u):
        g, m = divmod(u, 6)
        tile = (F_[m], B_[m])
        w = u % NL
        X = X2[u] = {}
        for d in range(2):
            a = 0 if d == 0 else 2
            src = T["str"][2 * g:2 * g + 2, tile[d], :, a:a + 5, :].rearrange("q p n t -> p q n t")
            f = readers.get(u - NL)
            t1 = P.dma(f"ld{w}{d}", ld[:, w, d].rearrange("p q n t -> p q (n t)"),
                       src.rearrange("p q n t -> p q (n t)"), stored, f)
            t2 = P.dma(f"sl{w}{d}", sgl[:, w, d, :], T["sg"][d, tile[d], :, 256 * g:256 * g + 256], f)
            X[d] = {"t_ld": t1, "t_sg": t2}


    def prepare(u):
        g, m = divmod(u, 6)
        tile = (F_[m], B_[m])
        z = u % 3
        x = X2[u]
        w = u % NL
        pw = [P.last("pe"), P.last("dve"), P.last("act"), P.last("pool")]
        for d in range(2):
            X = x[d]
            X["tok"] = slice(128 * tile[d], 128 * tile[d] + 128)
            tr = trs_[:, u % 2]
            L5 = lambda nm, d=d: ld[:, w, d, :, {"b": 0, "kd": 1, "r": 2, "kk": 3, "v": 4}[nm] if d == 0 else
                                    {"r": 0, "kk": 1, "v": 2, "b": 3, "kd": 4}[nm], :]
            t_ld, t_sg = X["t_ld"], X["t_sg"]
            K_ = {nm: K2[z, nm, d] for nm in ("rho", "Lb", "Lk", "kt", "bt", "vt", "W1", "W2")}
            Pinv = at = tr[:, d, 0:256]
            AR = tr[:, d, 256:768].rearrange("p (q s t) -> p q s t", q=2, s=2)
            be, ka = tr[:, d, 768:1024], tr[:, d, 1024:1280]
            LKs = tr[:, d, 768:1280]
            LA = tr[:, d, 1280:1792]
            i = bank()
            t = mms([(psum[:, i, 256 * p:256 * p + 256], sgl[:, w, d, 128 * p:128 * p + 128], TRI(d),
                      True, True) for p in range(2)], t_sg, t_rc, bank_free[i])
            cum = psum[:, i, :].rearrange("p (q s t) -> p q s t", q=2, s=2)
            t1 = act(AR[:, :, 1, :], cum[:, :, 0, :], ACT.Exp, t, *pw)
            t2 = act(b2(Pinv), cum[:, :, 0, :], ACT.Exp, scale=-1.0)
            t3 = act(AR[:, :, 0, :], cum[:, :, 1, :], ACT.Exp)
            bank_free[i] = [t3]
            e0 = 63 if d == 0 else 0
            tpc = copy("pool", pcs[:, z, d, :].rearrange("p (q c) -> p q c", q=2), AR[:, :, 1, e0:128:64], t1, *pw)
            ta2 = tt("dve", AR[:, :, 0, :], AR[:, :, 0, :], L5("kk"), ALU.mult, t3, t_ld)
            ta1 = tt("dve", AR[:, :, 1, :], AR[:, :, 1, :], L5("r"), ALU.mult, t1, tpc, t_ld)
            tb = tt("pool", b2(be), b2(Pinv), L5("b"), ALU.mult, t2, t_ld, *pw)
            tk_ = tt("dve", b2(ka), b2(Pinv), L5("kd"), ALU.mult, t2, t_ld)
            X["tro"] = copy("pool", b2(K_["rho"]), AR[:, :, 1, :], ta1)
            yield
            i = bank()
            t = transposes([(psum[:, i, 128 * p:128 * p + 128], b2(be)[:, p, :]) for p in range(2)] +
                           [(psum[:, i, 256 + 128 * p:384 + 128 * p], b2(ka)[:, p, :]) for p in range(2)],
                           tb, tk_, bank_free[i])
            t4 = copy("act", K_["bt"], psum[:, i, 0:256], t)
            t5 = copy("act", K_["kt"], psum[:, i, 256:512])
            bank_free[i] = [t5]
            i = bank()
            t = transposes([(psum[:, i, 128 * p:128 * p + 128], AR[:, p, 0, :]) for p in range(2)] +
                           [(psum[:, i, 256 + 128 * p:384 + 128 * p], L5("v")[:, p, :]) for p in range(2)],
                           ta2, t_ld, bank_free[i])
            readers.setdefault(u, []).extend([t, ta1, ta2, tb, tk_])
            t6 = copy("act", at, psum[:, i, 0:256], t, tk_, tb)
            t7 = copy("act", K_["vt"], psum[:, i, 256:512])
            bank_free[i] = [t7]
            X.update(t7=t7, t6=t6)
            yield
            msk = MSK(d).rearrange("p (s t) -> p s t", s=2)
            got = []
            for which, src in ((0, be), (1, ka)):
                for j in range(2):
                    i = bank()
                    t = mms([(psum[:, i, 256 * p:256 * p + 256], b2(src)[64 * j:64 * j + 64, p, :],
                              AR[64 * j:64 * j + 64, p, :, :], True, True) for p in range(2)],
                            ta1, ta2, bank_free[i])
                    got.append((which, j, i, t))
            for which, j, i, t in got:
                pv = psum[:, i, :].rearrange("p (q s t) -> p q s t", q=2, s=2)
                strict = v4(LKs if which else LA)[:, 2 * j:2 * j + 2, :]
                incl = v4(K_["Lk" if which else "Lb"])[:, 2 * j:2 * j + 2, :]
                if which:
                    t = got[3][3]
                t = tt("dve", strict, pv[:, :, 0, :], msk[:, 0, :].unsqueeze(1).to_broadcast([128, 2, 128]),
                       ALU.mult, t)
                t_L = tt("dve", incl, pv[:, :, 1, :], msk[:, 1, :].unsqueeze(1).to_broadcast([128, 2, 128]),
                         ALU.mult)
                bank_free[i] = [t_L]
                if which == 0:
                    t_LA = t_L
            yield
            i = bank()
            t = mms([(psum[:, i, 64 * (2 * p + j):64 * (2 * p + j) + 64], hs(LKs, 2 * j + p),
                      K_["vt"][:, 64 * (2 * p + j):64 * (2 * p + j) + 64], True, True) for j, p in hl],
                    t_L, t7, bank_free[i])
            X["t_y0"] = copy("act", K_["W2"], psum[:, i, 0:256], t)
            bank_free[i] = [X["t_y0"]]
            X.update(LA=LA, at=at, K=K_, tpc=tpc, t_LA=t_LA)
            yield

    def invert(u):
        x = X2[u]
        pw = [P.last("pe"), P.last("dve"), P.last("act"), P.last("pool")]
        for d in range(2):
            X = x[d]
            D, E, Y, NTb = (inv[:, d, 512 * w:512 * w + 512] for w in range(4))
            LA, t_LA = X["LA"], X["t_LA"]
            lv = lambda l, d=d: LVL(d, l).unsqueeze(1).to_broadcast([128, 4, 128])
            idb = ident.unsqueeze(1).to_broadcast([128, 4, 128])
            t = tt("dve", v4(E), v4(LA), lv(0), ALU.mult, t_LA, *pw)
            X["t_e"] = tt("dve", v4(E), v4(E).bitcast(F32), idb, ALU.add, t)
            X["t_n"] = tt("pool", v4(NTb), v4(LA), lv(1), ALU.mult, t_LA, *pw)
            X.update(D=D, E=E, Y=Y, NTb=NTb, lv=lv)
        yield
        for d in range(2):
            X = x[d]
            i = bank()
            t = mms([(psum[:, i, 128 * h:128 * h + 128], hs(X["E"], h), idr[:, :], True, True) for h in range(4)],
                    X["t_e"], t_idr, bank_free[i])
            X["t_d"] = copy("act", X["D"], psum[:, i, :], t)
            bank_free[i] = [X["t_d"]]
        yield
        for l in range(1, 6):
            for d in range(2):
                X = x[d]
                i = bank()
                t = mms([(psum[:, i, 128 * h:128 * h + 128], hs(X["NTb"], h), hs(X["D"], h), True, True)
                         for h in range(4)], X["t_n"], X["t_d"], bank_free[i])
                X["ty"] = copy("act", X["Y"], psum[:, i, :], t)
                bank_free[i] = [X["ty"]]
                if l < 5:
                    X["t_n"] = tt("pool", v4(X["NTb"]), v4(X["LA"]), X["lv"](l + 1), ALU.mult, t)
            yield
            for d in range(2):
                X = x[d]
                i = bank()
                td = mms([(psum[:, i, 128 * h:128 * h + 128], hs(X["E"], h), hs(X["Y"], h), True, True)
                          for h in range(4)], X["ty"], X["t_e"], bank_free[i])
                if l < 5:
                    i2 = bank()
                    te = mms([(psum[:, i2, 128 * h:128 * h + 128], hs(X["Y"], h), hs(X["E"], h), True, True)
                              for h in range(4)], bank_free[i2])
                X["t_d"] = tt("dve", X["D"], X["D"].bitcast(F32), psum[:, i, :], ALU.add, td)
                bank_free[i] = [X["t_d"]]
                if l < 5:
                    X["t_e"] = tt("dve", X["E"], X["E"].bitcast(F32), psum[:, i2, :], ALU.add, te)
                    bank_free[i2] = [X["t_e"]]
            yield
        for d in range(2):
            X = x[d]
            i = bank()
            t = mms([(psum[:, i, 128 * h:128 * h + 128], hs(X["D"], h), idr[:, :], True, True)
                     for h in range(4)], X["t_d"], bank_free[i])
            X["t_e"] = copy("act", X["E"], psum[:, i, :], t)
            bank_free[i] = [X["t_e"]]
            i = bank()
            t = mms([(psum[:, i, 128 * h:128 * h + 128], hs(X["LA"], h), hs(X["D"], h).bitcast(F32), True, True)
                     for h in range(4)], bank_free[i])
            idb = ident.unsqueeze(1).to_broadcast([128, 4, 128])
            t1 = tt("pool", v4(X["D"]), idb, v4(X["D"]).bitcast(F32), ALU.subtract, t)
            X["ty"] = tt("dve", X["Y"], X["D"].bitcast(F32), psum[:, i, :], ALU.add, t1)
            bank_free[i] = [X["ty"]]
        yield
        for d in range(2):
            X = x[d]
            i = bank()
            t = mms([(psum[:, i, 128 * h:128 * h + 128], hs(X["Y"], h), hs(X["E"], h), True, True)
                     for h in range(4)], X["ty"], X["t_e"], bank_free[i])
            X["t_e"] = tt("dve", X["LA"], X["E"].bitcast(F32), psum[:, i, :], ALU.add, t)
            bank_free[i] = [X["t_e"]]
        yield
        for d in range(2):
            X = x[d]
            W1, W2 = X["K"]["W1"], X["K"]["W2"]
            i = bank()
            t = mms([(psum[:, i, 64 * (2 * p + j):64 * (2 * p + j) + 64], hs(X["LA"], 2 * j + p),
                      W2[:, 64 * (2 * p + j):64 * (2 * p + j) + 64], True, True) for j, p in hl],
                    X["t_e"], X["t_y0"], bank_free[i])
            X["t_w2"] = copy("act", W2, psum[:, i, 0:256], t)
            bank_free[i] = [X["t_w2"]]
            i = bank()
            t = mms([(psum[64 * j:64 * j + 64, i, 128 * p:128 * p + 128],
                      X["at"][:, 64 * (2 * p + j):64 * (2 * p + j) + 64], hs(X["LA"], 2 * j + p), True, True)
                     for j, p in hl], X["t6"], bank_free[i])
            X["t_w1"] = copy("act", W1, psum[:, i, 0:256], t)
            bank_free[i] = [X["t_w1"]]

    def chain(u):
        g, m = divmod(u, 6)
        tile = (F_[m], B_[m])
        z = u % 3
        x = X2[u]
        oT = oTs[:, g % 2]
        if m == 0 and g:
            for d in range(2):
                t_s[d] = P.op("dve", lambda e, d=d, s=s_cur[d]: e.memset(S[:, d, s], 0.0), P.last("pe"), t_s[d])
        K_ = {(nm, d): K2[z, nm, d] for nm in ("rho", "Lb", "Lk", "kt", "bt", "vt", "W1", "W2") for d in range(2)}
        Ut = Ut2[:, u % 2]
        for s in range(2):
            half = (s, 1 - s)
            iu = bank()
            P.wait("pe", bank_free[iu])
            for d in range(2):
                r0 = 64 * half[d]
                w1 = b2(K_["W1", d])
                t_u = mms([(psum[r0:r0 + 64, iu, 128 * p:128 * p + 128], w1[:, p, r0:r0 + 64],
                            S[:, d, s_cur[d], p, :], True, True) for p in range(2)], x[d]["t_w1"], t_s[d])
            for d in range(2):
                r0 = 64 * half[d]
                x[d]["t_u"] = tt("dve", Ut[r0:r0 + 64, d, :], psum[r0:r0 + 64, iu, 0:256],
                                 K_["W2", d][r0:r0 + 64, :], ALU.add, t_u, x[d]["t_w2"])
            bank_free[iu] = [x[1]["t_u"]]
            for d in range(2):
                r0 = 64 * half[d]
                if s == 0:
                    x[d]["io"] = bank()
                    P.wait("pe", bank_free[x[d]["io"]])
                io = x[d]["io"]
                x[d]["t_os"] = mms([(psum[:, io, 256 * s + 64 * p:256 * s + 64 * p + 64], S[:, d, s_cur[d], p, :],
                                     b2(K_["rho", d])[:, p, r0:r0 + 64], True, True) for p in range(2)],
                                   x[d]["tro"])
            yield
            for d in range(2):
                r0 = 64 * half[d]
                sc = s_cur[d]
                sn = 1 - sc
                i = bank()
                lst = []
                for p in range(2):
                    o_ = psum[:, i, 128 * p:128 * p + 128]
                    cs = slice(128 * p, 128 * p + 128)
                    lst += [(o_, K_["kt", d][r0:r0 + 64, cs], K_["vt", d][r0:r0 + 64, cs], True, False),
                            (o_, K_["bt", d][r0:r0 + 64, cs], Ut[r0:r0 + 64, d, cs], False, True)]
                ts_ = mms(lst, x[d]["t_u"], bank_free[i])
                pc = b2(pcs[:, z, d, :])[:, :, half[d]:half[d] + 1]
                for j in range(2):
                    q0 = 64 * j
                    src = psum[q0:q0 + 64, i, 0:256].rearrange("p (q v) -> p q v", q=2)[:, :, q0:q0 + 64]
                    so = S[q0:q0 + 64, d, sc, :, q0:q0 + 64]
                    sd = S[q0:q0 + 64, d, sn, :, q0:q0 + 64]
                    t = tt("dve", sd, src, so, ALU.add, ts_, t_s[d])
                    t_n2 = tt("dve", sd, sd, pc[q0:q0 + 64].to_broadcast([64, 2, 64]), ALU.mult, t, x[d]["tpc"])
                bank_free[i] = [t]
                t_s[d] = t_n2
                s_cur[d] = sn
            yield
        for d in range(2):
            X = x[d]
            i = bank()
            lst = []
            for j, p in hl:
                o_ = psum[64 * j:64 * j + 64, i, 128 * p:128 * p + 128]
                cs = slice(64 * (2 * p + j), 64 * (2 * p + j) + 64)
                lst += [(o_, K_["vt", d][:, cs], hs(K_["Lk", d], 2 * j + p), True, False),
                        (o_, Ut[:, d, cs], hs(K_["Lb", d], 2 * j + p), False, True)]
            t = mms(lst, X["t_u"], bank_free[i])
            first = (tile[d], d) in ((0, 0), (1, 1), (2, 0), (3, 0), (4, 1), (5, 1))
            od = oT[:, :, X["tok"]]
            src = psum[:, i, 0:256].rearrange("p (q t) -> p q t", q=2)
            if first:
                t1 = copy("act", od, src, t, ofree[g % 2])
            else:
                t1 = tt("dve", od, od, src, ALU.add, t, t_o[g])
            bank_free[i] = [t1]
            io = X["io"]
            for s in range(2):
                hf = s if d == 0 else 1 - s
                o2 = oT[:, :, 128 * tile[d] + 64 * hf:128 * tile[d] + 64 * hf + 64]
                t1 = tt("dve", o2, o2, psum[:, io, 256 * s:256 * s + 128].rearrange("p (q t) -> p q t", q=2),
                        ALU.add, t1, X["t_os"])
            bank_free[io] = [t1]
            t_o[g].append(t1)
            yield

    bgl = sb(c, "bgl", [2, 2, NT])
    ros = sb(c, "ro", [2, 3, NT])
    t_yst = []
    frees = [[None, None], [None, None]]

    def readout(gp):
        g = gp // 2
        w = gp % 2
        lfree = frees[w]
        o, sq, rr = (ros[:, w, z, :] for z in range(3))
        src = oTs[:, g % 2, gp % 2, :]
        tb = P.dma(f"bgl{w}", bgl[:, w, :, :], T["bg"][gp], lfree[0])
        for a, b in spans(NT):
            i = bank()
            t = mms([(psum[:, i, 0:b - a], blk, src[:, a:b], True, True)], t_o[g], bank_free[i])
            t = stt(o[:, a:b], psum[:, i, 0:b - a], -1.0 / 64, src[:, a:b], ALU.mult, ALU.add, t, lfree[1])
            bank_free[i] = [t]
        ofree.setdefault(g % 2, [])
        ofree[g % 2] = (ofree[g % 2] or []) + [t]
        yield
        tq = act(sq, o, ACT.Square, t, lfree[0])
        yield
        tr_ = rstd(sq, spans(NT), rr, blk, 64e-5, 64.0, tq)
        yield
        t = tt("dve", o, o, rr, ALU.mult, tr_)
        t = ts("dve", o, o, Q("gn_g", gp, 1), Q("gn_b", gp, 1), ALU.mult, ALU.add, t)
        yield
        t = tt("pool", o, o, bgl[:, w, 1, :], ALU.add, tb, t)
        t = tt("pool", o, o, bgl[:, w, 0, :], ALU.mult, t)
        lfree[0] = t
        lfree[1] = P.dma(f"ys{w}", T["y"][:, gp, :], o, t, e="pool")
        t_yst.append(lfree[1])

    fetch(0)
    fetch(1)
    weave(prepare(0))
    fetch(2)
    pace((invert(0), 15), (prepare(1), 8))
    for u in range(24):
        if u + 3 < 24:
            fetch(u + 3)
        parts = [(chain(u), 7)]
        if u + 1 < 24:
            parts.append((invert(u + 1), 15))
        if u + 2 < 24:
            parts.append((prepare(u + 2), 8))
        g, m = divmod(u, 6)
        if g and m in (1, 3):
            parts.append((readout(2 * (g - 1) + m // 2), 6))
        pace(*parts)
    old = keep[:, 0].rearrange("p d n -> p (d n)")
    ring = g_.Ring(c, "wm1", 4, old[:, 0:4096].rearrange("p (n k w) -> p n k w", n=4, k=8))
    mrow = old[:, 4096:5120].rearrange("p (n w) -> p n w", n=2)
    place = [(ring, mrow)]
    mg = g_.modulation(1, mods, lambda c: place[-1])

    pace((readout(6), 5), (readout(7), 5), (some(mg, 18), 18))
    barrier()
    for e in ("act", "dve", "pool", "sp"):
        P.wait(e, P.final(t_yst))
    c.close()

    P.x2 = sb(g_.ctx, "x2", [8, 512])
    plan = [T["rw_out"][k] for k in range(8)]
    for h in range(8):
        plan += [T["da_in"][z + h] for z in (0, 8, 16, 24)]
    plan += [T["da_out"][k] for k in range(8)]
    for l in range(2):
        for pi in range(8):
            kind = min(pi // 3, 2)
            if kind < 2:
                plan += [T["w_in2"][l, 12 * kind + pi - 3 * kind + 3 * z] for z in range(4)]
            else:
                r = pi - 6
                plan += [T["w_in2"][l, 24 + r], T["w_mkv"][l, r], T["w_mkv"][l, 2 + r], T["w_in2"][l, 26 + r]]
        plan += [T["w_out2"][l, k] for k in range(8)]
    hv = g_.Halves(g_.ctx, "wb", 3, 2, plan)
    P.c = ExitStack()
    ring, mrow = g_.Ring(P.c, "wm2", 11), sb(P.c, "mrow2", [2, 512])
    place.append((ring, mrow))
    P.c.close()
    P.h1 = (g_.sbr(P.c, "hT1h", [8, NT]), g_.sbr(P.c, "hT1l", [8, NT]))
    c = ExitStack()
    yr = [sb(c, f"yr{i}", [NT]) for i in range(4)]
    yT = (g_.sbr(c, "yTh", [8, NT]), g_.sbr(c, "yTl", [8, NT]))
    xT = sb(c, "xTb", [8, NT])
    yfree = [None] * 4

    def load_y(k):
        return P.dma(f"yl{k % 4}", yr[k % 4][:, :], T["y"][:, k, :], yfree[k % 4], e="pool")

    t_y = []
    for k in range(8):
        t = load_y(k)
        yfree[k % 4] = g_.halves((yT[0][:, k, :], yT[1][:, k, :]), yr[k % 4][:, :], "act", "dve", t)
        t_y.append(yfree[k % 4])
    weave(mg)
    t_xl = P.dma("xl", xT[:, :, :], T["x"])
    tk = {"ab": mods[1]}
    A1 = lambda k, s: g_.ABs[:, 1][:, k, s:s + 1]
    B1 = lambda k, s: g_.modcs[:, 1][:, k, s:s + 1]
    hv.split(2)
    nm = g_.normed(c, xT, NT, "1", P.h1, A1, B1, [(0, 256, 1), (256, 768, 0)], tk, n=2, own=True)
    P.t_x1 = tk["out"] = []
    for k in range(8):
        def sink(i, a, b, t):
            s = 1 if a == 0 else 0
            stt(xT[:, k, a:b], psum[:, i, 0:b - a], modc[:, 16 + k, s:s + 1], xT[:, k, a:b], ALU.mult, ALU.add,
                t, t_xl)
            bank_free[i] = [P.last("dve")]
        weave(product(yT, NT, t_y, sink))
        tx = tk[k] = P.last("dve")
        P.t_x1.append(P.dma(f"xs{k}", T["x1"][:, k, :], xT[:, k, :], tx, e="pool"))
        if k:
            next(nm)
    weave(nm)
    P.t_h1 = tk["h"]
    barrier()
    for e in P.q:
        P.wait(e, P.t_x1)
    c.close()


class Scratch:

    def __init__(self, sb, c, W, tag, n):
        self.sets = [(sb(c, f"sq{tag}{i}", [W]), sb(c, f"R{tag}{i}", [W]), sb(c, f"tm{tag}{i}", [512])) for i in range(n)]
        self.free = [None] * n
        self.k = 0

    def take(self):
        i = self.k % len(self.sets)
        self.k += 1
        return i


def norm_rope(g_, buf, W, gcol, sc, t, table=None, a0=0):
    u = sc.take()
    sq, R, tmp = sc.sets[u]
    tq = g_.act(sq[:, 0:W], buf[:, 0:W], ACT.Square, t, sc.free[u])
    yield None
    tr = g_.rstd(sq, g_.spans(W), R, g_.blk, 1e-6, 64.0, tq)
    yield None
    t = g_.stt(buf[:, 0:W], buf[:, 0:W], gcol, R[:, 0:W], ALU.mult, ALU.mult, tr)
    sc.free[u] = [t]
    if table is None:
        yield t
        return
    yield None
    rot, cos, sin, t_tab = table
    i = g_.bank()
    n = W - a0
    tm = g_.mms([(g_.psum[:, i, 0:n], rot, buf[:, a0:W], True, True)], t, t_tab, g_.bank_free[i])
    t1 = g_.tt("dve", tmp[:, 0:n], g_.psum[:, i, 0:n], sin, ALU.mult, tm)
    g_.bank_free[i] = [t1]
    t2 = g_.tt("pool", buf[:, a0:W], buf[:, a0:W], cos, ALU.mult, tm)
    t3 = g_.tt("dve", buf[:, a0:W], buf[:, a0:W], tmp[:, 0:n], ALU.add, t1, t2)
    sc.free[u] = [t, t3]
    yield t3


def tokens(g_, src, dst, n, t, *free):
    out = []
    for n0 in range(0, n, 4):
        n1 = min(n, n0 + 4)
        i = g_.bank()
        tm = g_.transposes([(g_.psum[:, i, 128 * (z - n0):128 * (z - n0) + 128], src[:, 128 * z:128 * z + 128])
                            for z in range(n0, n1)], t, g_.bank_free[i])
        out.append(g_.copy("dve", dst[:, n0:n1, :],
                           g_.psum[:, i, 0:128 * (n1 - n0)].rearrange("p (n c) -> p n c", c=128), tm, *free))
        g_.bank_free[i] = [out[-1]]
    return out


def diff_layer(nc, P, T, g_):
    sb, act, copy, tt, ts, stt, mms, psum = g_.sb, g_.act, g_.copy, g_.tt, g_.ts, g_.stt, g_.mms, g_.psum
    bank, bank2, bank_free, C, Q = g_.bank, g_.bank2, g_.bank_free, g_.C, g_.Q
    modc = g_.modcs[:, 1]
    barrier, product, transposes = g_.barrier, g_.product, g_.transposes
    x2, c, hT, t_h = P.x2, P.c, P.h1, P.t_h1
    yT = x2
    ac = sb(c, "ac", [NAC])
    t_ac = P.dma("ac", ac[:, :], T["ac"])
    sm = g_.sm
    lv = Q("lam")
    t1 = tt("dve", sm[:, 0:64], lv[:, 0:64], lv[:, 64:128], ALU.mult, g_.t_par)
    t1 = P.op("dve", lambda e: e.reduce_sum(sm[:, 64:65], sm[:, 0:64], AX.X), t1)
    t2 = tt("dve", sm[:, 0:64], lv[:, 128:192], lv[:, 192:256], ALU.mult, t1)
    t2 = P.op("dve", lambda e: e.reduce_sum(sm[:, 65:66], sm[:, 0:64], AX.X), t2)
    t3 = act(sm[:, 64:66], sm[:, 64:66], ACT.Exp, t2)
    t3 = tt("dve", sm[:, 66:67], sm[:, 65:66], sm[:, 64:65], ALU.subtract, t3)
    t_lam = ts("dve", sm[:, 67:68], sm[:, 66:67], -LAM_INIT, None, ALU.add, None, t3)
    t_sl = ts("dve", sm[:, 68:69], Q("subln"), 1.0 - LAM_INIT, None, ALU.mult, None)
    nlam = sm[:, 67:68]
    subl = sm[:, 68:69]

    def two(name, cols):
        return [sb(c, f"{name}{i}", cols) for i in range(2)]

    qb, kb, vb, gb = two("qb", [512]), two("kb", [NT]), two("vb", [6, 128]), two("gb", [512])
    sc = Scratch(sb, c, NT, "a", 2)
    NP_ = 3
    p0 = [sb(c, f"p0{i}", [NT]) for i in range(NP_)]
    p1 = [sb(c, f"p1{i}", [NT]) for i in range(NP_)]
    aT = two("aT", [6, 512])
    st = [sb(c, f"st{i}", [8]) for i in range(NP_)]
    cos, sin = ac[:, 512:1024], ac[:, 1280:1792]
    table = (ac[:, 0:128], cos, sin, t_ac)
    vt = sb(c, "vt1", [NT])
    fin = {0: None, 1: None}
    t_y = []
    npair = [0]
    pfree = [None] * NP_
    ready = {}
    vtf = [None]

    def project(h):
        b = h % 2
        q, k, v, gg = qb[b], kb[b], vb[b], gb[b]
        f = fin[b]
        X = {}

        def into(key, dst):
            def sink(i, a, b, t):
                X.setdefault(key, []).append(copy("act", dst[:, a:b], psum[:, i, 0:b - a], t, f, vtf[0]))
                bank_free[i] = [X[key][-1]]
            return sink

        def gate(i, a, b, t):
            X["g"] = act(gg[:, :], psum[:, i, :], ACT.Silu, t, f)
            bank_free[i] = [X["g"]]

        yield from product(hT, 512, t_h, into("q", q), 256)
        gq = norm_rope(g_, q, 512, Q("qn"), sc, X["q"], table)
        next(gq)
        pk = product(hT, NT, t_h, into("k", k))
        yield next(pk)
        next(gq)
        yield next(pk)
        next(gq)
        yield next(pk)
        weave(pk)
        gk = norm_rope(g_, k, NT, Q("kn"), sc, X["k"], table, 256)
        tq = next(gq)
        next(gk)
        pv = product(hT, NT, t_h, into("v", vt))
        yield next(pv)
        next(gk)
        yield next(pv)
        next(gk)
        yield next(pv)
        weave(pv)
        tk = next(gk)
        pg = product(hT, 512, t_h, gate, 256)
        yield next(pg)
        tv = tokens(g_, vt, v, 6, X["v"], f)
        vtf[0] = P.last("pe")
        yield next(pg)
        weave(pg)
        ready[h] = (tq, tk, tv, X["g"])

    def attend(h):
        b = h % 2
        q, k, v, gg = qb[b], kb[b], vb[b], gb[b]
        tq, tk, tv, tg = ready[h]
        t_at = []
        S = {}

        def scores(qt):
            u = npair[0] % NP_
            npair[0] += 1
            s_ = st[u]
            pr = (p0[u], p1[u])
            te = []
            for cc in range(2):
                i = bank2()
                t = mms([(psum[:, i + (a0 // 512), 0:a1 - a0], q[64 * cc:64 * cc + 64, 128 * qt:128 * qt + 128],
                          k[64 * cc:64 * cc + 64, a0:a1], True, True) for a0, a1 in ((0, 512), (512, 768))],
                        tq, tk, bank_free[i], bank_free[i + 1])
                sp_ = psum[:, i:i + 2, :].rearrange("p a n -> p (a n)")[:, 0:768]
                t = P.op("dve", lambda e, sp_=sp_, cc=cc, s_=s_: e.reduce_max(s_[:, cc:cc + 1], sp_, AX.X), t, pfree[u])
                t = ts("dve", s_[:, cc:cc + 1], s_[:, cc:cc + 1], -0.125, None, ALU.mult, None, t)
                t = act(pr[cc][:, :], sp_, ACT.Exp, t, pfree[u], scale=0.125, bias=s_[:, cc:cc + 1],
                        accum=s_[:, 2 + cc:3 + cc])
                bank_free[i] = [t]
                bank_free[i + 1] = [t]
                te.append(t)
            S[qt] = (u, te)

        def differ(qt):
            u, te = S[qt]
            s_ = st[u]
            pr = (p0[u], p1[u])
            t = P.op("dve", lambda e, s_=s_: e.reciprocal(s_[:, 4:6], s_[:, 2:4]), te)
            t2 = ts("dve", s_[:, 5:6], s_[:, 5:6], nlam, None, ALU.mult, None, t, t_lam)
            ta = ts("dve", pr[1][:, :], pr[1][:, :], s_[:, 5:6], None, ALU.mult, None, t2)
            S[qt] = u, stt(pr[0][:, :], pr[0][:, :], s_[:, 4:5], pr[1][:, :], ALU.mult, ALU.add, ta)

        def combine(qt):
            u, ta = S[qt]
            pr = (p0[u], p1[u])
            for n0, n1 in ((0, 4), (4, 6)):
                i = bank()
                t = transposes([(psum[:, i, 128 * (n - n0):128 * (n - n0) + 128], pr[0][:, 128 * n:128 * n + 128])
                                for n in range(n0, n1)], ta, bank_free[i])
                t2 = copy("dve" if n0 else "act", aT[b][:, n0:n1, 128 * qt:128 * qt + 128],
                          psum[:, i, 0:128 * (n1 - n0)].rearrange("p (n c) -> p n c", c=128), t, fin[b])
                bank_free[i] = [t2]
                t_at.append(t2)
            pfree[u] = [t, ta]

        scores(0)
        yield
        scores(1)
        yield
        for qt in range(4):
            differ(qt)
            if qt < 2:
                scores(qt + 2)
            yield
            combine(qt)
            yield
        i = bank()
        t_pv = mms([(psum[:, i, :], v[:, n, :], aT[b][:, n, :], n == 0, n == 5) for n in range(6)],
                   t_at, tv, bank_free[i])
        t = copy("act", yT[:, h, :], psum[:, i, :], t_pv)
        bank_free[i] = [t]
        u = sc.take()
        sq, R, _ = sc.sets[u]
        tq2 = act(sq[:, 0:512], yT[:, h, :], ACT.Square, t, sc.free[u])
        yield
        tr = g_.rstd(sq, [(0, 512)], R, g_.ones, 1e-5, 128.0, tq2)
        t = stt(yT[:, h, :], yT[:, h, :], subl, R[:, 0:512], ALU.mult, ALU.mult, tr, t_sl)
        sc.free[u] = [t]
        t = tt("pool", yT[:, h, :], yT[:, h, :], gg[:, :], ALU.mult, t, tg)
        fin[b] = [t_pv, t]
        t_y.append(t)

    th_y = []

    def split(h):
        th_y.append(g_.halves((hT[0][:, h, 0:512], hT[1][:, h, 0:512]), yT[:, h, :], "act", "pool", t_y[h],
                              P.last("pe")))

    def splits():
        for h in range(7):
            yield
            split(h)

    weave(project(0))
    for h in range(8):
        if h < 7:
            pace((attend(h), 11), (project(h + 1), 10))
        else:
            weave(attend(h), splits())
    split(7)
    t_xl = P.dma("x1m", x2[:, :, :], T["x1"][:, :, 256:768], th_y)
    for k in range(8):
        def sink(i, a, b, t):
            stt(x2[:, k, :], psum[:, i, :], modc[:, 16 + k, 0:1], x2[:, k, :], ALU.mult, ALU.add, t, t_xl)
            bank_free[i] = [P.last("dve")]
        weave(product(hT, 512, th_y, sink))
    tx = P.last("dve")
    P.x2, P.t_x2 = x2, tx
    barrier()
    c.close()


def second_block(nc, P, T, g_):
    sb, act, copy, tt, ts, stt, mms, psum = g_.sb, g_.act, g_.copy, g_.tt, g_.ts, g_.stt, g_.mms, g_.psum
    bank, bank2, bank_free, C, Q = g_.bank, g_.bank2, g_.bank_free, g_.C, g_.Q
    barrier, product, transposes = g_.barrier, g_.product, g_.transposes
    x2, t_x = P.x2, P.t_x2
    c = g_.ctx
    bc = sb(c, "bc", [NBC])
    t_bc = P.dma("bc", bc[:, :], T["bc"])
    hT = (g_.sbr(c, "hT2h", [8, 512]), g_.sbr(c, "hT2l", [8, 512]))
    hm = (g_.sbr(c, "hm2h", [8, 256]), g_.sbr(c, "hm2l", [8, 256]))
    yT = (g_.sbr(c, "yT2h", [8, 512]), g_.sbr(c, "yT2l", [8, 512]))
    yo = [sb(c, f"yo2{i}", [512]) for i in range(1)] * 2
    yfree = [None, None]
    vt = sb(c, "vt2", [512])
    vtf = [None]

    def two(name, cols):
        return [sb(c, f"{name}{i}", cols) for i in range(2)]

    qb, kb, vb, gb = two("qc", [512]), two("kc", [512]), two("vc", [4, 128]), two("gc", [512])
    sc = Scratch(sb, c, 512, "c", 3)
    NP_ = 4
    pr = [sb(c, f"pc{i}", [512]) for i in range(NP_)]
    st = [sb(c, f"stc{i}", [8]) for i in range(NP_)]
    table = (bc[:, 0:128], bc[:, 128:640], bc[:, 640:1152], t_bc)
    fin = {0: None, 1: None}
    pfree = [None] * NP_
    afree = [None] * 3
    n_ = [0, 0]
    ready = {}

    def project(l, pi, t_h, t_m):
        kind = 0 if pi < 3 else (1 if pi < 6 else 2)
        b = pi % 2
        q, k, v, gg = qb[b], kb[b], vb[b], gb[b]
        f = fin[b]
        nk, src, th2, tab = (512, hT, t_h, table) if kind < 2 else (256, hm, t_m, None)
        X = {}

        def into(key, dst):
            def sink(i, a, b, t):
                X[key] = copy("act", dst[:, a:b], psum[:, i, 0:b - a], t, f, vtf[0])
                bank_free[i] = [X[key]]
            return sink

        def gate(i, a, b, t):
            X["g"] = act(gg[:, :], psum[:, i, :], ACT.Silu, t, f)
            bank_free[i] = [X["g"]]

        yield from product(hT, 512, t_h, into("q", q))
        gq = norm_rope(g_, q, 512, Q("qkg", 6 * l + 2 * kind, 1), sc, X["q"], tab)
        next(gq)
        pk = product(src, nk, th2, into("k", k))
        yield next(pk)
        tq = next(gq)
        yield next(pk, None)
        tq = next(gq)
        weave(pk)
        gk = norm_rope(g_, k, nk, Q("qkg", 6 * l + 2 * kind + 1, 1), sc, X["k"], tab)
        next(gk)
        pv = product(src, nk, th2, into("v", vt))
        yield next(pv)
        if tab:
            tq = next(gq)
        next(gk)
        yield next(pv, None)
        weave(pv)
        tk = next(gk)
        pg = product(hT, 512, t_h, gate)
        yield next(pg)
        if tab:
            tk = next(gk)
        tv = tokens(g_, vt, v, nk // 128, X["v"], f)
        vtf[0] = P.last("pe")
        yield next(pg)
        weave(pg)
        ready[pi] = (tq, tk, tv, X["g"])

    def attend(pi):
        kind = 0 if pi < 3 else (1 if pi < 6 else 2)
        b = pi % 2
        q, k, v, gg = qb[b], kb[b], vb[b], gb[b]
        tq, tk, tv, tg = ready[pi]
        io = bank()
        P.wait("pe", bank_free[io])
        t_at = {0: [], 1: []}
        a_ = {}
        S = {}
        for j in range(2):
            a_[j] = n_[0] % 3
            n_[0] += 1

        def scores(j, qt):
            u = n_[1] % NP_
            n_[1] += 1
            s_, pp = st[u], pr[u]
            n = 128 * (qt + 1) if kind < 2 else 256
            i = bank()
            t = mms([(psum[:, i, 0:n], q[64 * j:64 * j + 64, 128 * qt:128 * qt + 128],
                      k[64 * j:64 * j + 64, 0:n], True, True)], tq, tk, bank_free[i])
            if kind < 2:
                o = (1152 if kind == 0 else 1664) + 384 - 128 * qt
                t = P.op("dve", lambda e: e.tensor_tensor_reduce(
                    out=pp[:, 0:n], in0=psum[:, i, 0:n], in1=bc[:, o:o + n], scale=1.0, scalar=-3.0e38,
                    op0=ALU.add, op1=ALU.max, accum_out=s_[:, 0:1]), t, pfree[u], t_bc)
                bank_free[i] = [t]
                ein = pp[:, 0:n]
            else:
                t = P.op("dve", lambda e: e.reduce_max(s_[:, 0:1], psum[:, i, 0:n], AX.X), t, pfree[u])
                ein = psum[:, i, 0:n]
            t = ts("dve", s_[:, 1:2], s_[:, 0:1], -0.125, None, ALU.mult, None, t)
            t = act(pp[:, 0:n], ein, ACT.Exp, t, scale=0.125, bias=s_[:, 1:2], accum=s_[:, 2:3])
            if kind == 2:
                bank_free[i] = [t]
            S[j, qt] = (u, n, t)

        def scale(j, qt):
            u, n, t = S[j, qt]
            s_, pp = st[u], pr[u]
            t = P.op("dve", lambda e: e.reciprocal(s_[:, 3:4], s_[:, 2:3]), t)
            S[j, qt] = u, n, ts("dve", pp[:, 0:n], pp[:, 0:n], s_[:, 3:4], None, ALU.mult, None, t)

        def finish(j, qt):
            u, n, ta = S[j, qt]
            pp = pr[u]
            i = bank()
            t = transposes([(psum[:, i, 128 * z:128 * z + 128], pp[:, 128 * z:128 * z + 128])
                            for z in range(n // 128)], ta, bank_free[i])
            pfree[u] = [t]
            t2 = copy("act" if qt % 2 else "dve", aT[a_[j]][:, 0:n // 128, 128 * qt:128 * qt + 128],
                      psum[:, i, 0:n].rearrange("p (n c) -> p n c", c=128), t, afree[a_[j]])
            bank_free[i] = [t2]
            t_at[j].append(t2)

        tpv = []

        def values(j):
            nkt = 4 if kind < 2 else 2
            lst = []
            for z in range(nkt):
                q0 = 128 * z if kind < 2 else 0
                lst.append((psum[64 * j:64 * j + 64, io, q0:512], v[:, z, 64 * j:64 * j + 64],
                            aT[a_[j]][:, z, q0:512], z == 0, z == nkt - 1))
            t = mms(lst, t_at[j], tv, skip=True)
            afree[a_[j]] = [t]
            tpv.append(t)

        order = [(j, qt) for j in range(2) for qt in range(4)]
        scores(*order[0])
        scores(*order[1])
        yield
        for z, (j, qt) in enumerate(order):
            scale(j, qt)
            if z + 2 < 8:
                scores(*order[z + 2])
            if z:
                finish(*order[z - 1])
            yield
            if z == 5:
                values(0)
        finish(*order[7])
        yield
        values(1)
        y = yo[pi % 2]
        t = tt("dve", y[:, :], psum[:, io, :], gg[:, :], ALU.mult, tpv, tg, yfree[0])
        bank_free[io] = [t]
        fin[b] = [tpv[-1], t]
        yfree[0] = g_.halves((yT[0][:, pi, :], yT[1][:, pi, :]), y[:, :], "act", "pool", t, t_out)
        t_y.append(yfree[0])

    t_out = [None]

    def turn():
        for e in ("act", "dve", "pool"):
            P.wait(e, P.last("pe"), P.last("dve"), P.last("act"), P.last("pool"))

    cl = ExitStack()
    kx = {k: t_x for k in range(8)}
    kx["ab"] = None
    nx = g_.normed(cl, x2, 512, "n0", hT, lambda k, s: Q("ng2", k, 1), None, [(0, 512, 0)], kx)
    for l in range(2):
        Am = lambda k, s: Q("mng2", 8 * l + k, 1)
        mem = sb(cl, f"mem{l}", [8, 256])
        t_mem = P.dma("mem", mem[:, :, :], T["mem"], *[P.last(e) for e in ("pe", "act", "dve", "pool")])
        km = {k: t_mem for k in range(8)}
        km["ab"] = None
        weave(nx, g_.normed(cl, mem, 256, f"m{l}", hm, Am, None, [(0, 256, 0)], km, free=P.last("pe")))
        t_h, t_m = kx["h"], km["h"]
        cl.close()
        turn()
        cl = ExitStack()
        aT = [sb(cl, f"aTc{l}{i}", [4, 512]) for i in range(3)]
        t_y = []
        weave(project(l, 0, t_h, t_m))
        for pi in range(8):
            if pi < 7:
                pace((attend(pi), 10), (project(l, pi + 1, t_h, t_m), 8))
            else:
                weave(attend(pi))
        cl.close()
        turn()
        cl = ExitStack()
        if l == 0:
            kx = {"ab": None}
            nx = g_.normed(cl, x2, 512, "n1", hT, lambda k, s: Q("ng2", 8 + k, 1), None, [(0, 512, 0)], kx,
                           free=P.last("pe"))
        t_o = []
        for k in range(8):
            def sink(i, a, b, t):
                kx[k] = tt("dve", x2[:, k, :], psum[:, i, :], x2[:, k, :], ALU.add, t)
                bank_free[i] = [kx[k]]
                if l:
                    t_o.append(P.dma(f"out{k}", T["out"][:, k, :], x2[:, k, :], kx[k]))
            weave(product(yT, 512, t_y, sink))
            if l == 0 and k:
                next(nx)
        t_out[0] = P.last("pe")
    cl.close()
    P.wait("sp", t_o)


def kernel(**inputs):
    import numpy as _np
    import concourse.bacc as _bacc
    from concourse import mybir as _mybir
    from concourse.bass_utils import run_bass_kernel_spmd as _run

    I = {k: _np.asarray(v) for k, v in inputs.items()}

    def cm(a):
        return a.T.reshape(8, 128, -1).transpose(1, 0, 2)

    def wb(w):
        n = w.shape[-1] // 128
        lead = w.shape[:-2]
        k = len(lead)
        a = w.reshape(*lead, 8, 128, n, 128)
        return _np.ascontiguousarray(a.transpose(*range(k), k + 2, k + 1, k, k + 3))

    def cols(v):
        return v.reshape(-1, 128).T

    con, rc, ac, bc = constants()
    par = _np.zeros((128, NPAR), _np.float32)

    def put(name, a):
        o, w = PCOLS[name]
        par[:, o:o + w] = a.reshape(128, w)

    put("cs", _np.stack([cols(I["c"][0]), cols(I["c_ctx"])], axis=2))
    put("ada_b", _np.concatenate([cols(I["ada_b"][l]) for l in range(2)], axis=1))
    put("norm_g", _np.concatenate([cols(I["norm_g"][l]) for l in range(2)], axis=1))
    put("mu", cols(I["rw_mu"][0]))
    put("kk", cols(I["rw_kk"][0]))
    put("ka", cols(I["rw_ka"][0]))
    put("rk", cols(I["rw_rk"][0].reshape(-1)))
    put("gn_g", cols(I["rw_gn_g"][0]))
    put("gn_b", cols(I["rw_gn_b"][0]))
    put("a0", _np.concatenate([cols(I["rw_a0"][0, d]) for d in range(2)], axis=1))
    two = lambda v: _np.tile(v, 2)[:, None]
    put("qn", two(I["da_qn"][0]))
    put("kn", two(I["da_kn"][0]))
    put("subln", I["da_subln"][0][:, None])
    put("ng2", _np.concatenate([cols(I["norm_g_2"][l]) for l in range(2)], axis=1))
    put("mng2", _np.concatenate([cols(I["mem_norm_g_2"][l]) for l in range(2)], axis=1))
    put("qkg", _np.concatenate([two(I["qk_g_2"][l, i]) for l in range(2) for i in range(6)], axis=1))
    put("lam", _np.broadcast_to(I["da_lam"][0].reshape(1, 256), (128, 256)))
    lw2 = _np.zeros((128, 4, 1024), _np.float32)
    w0b = _np.zeros((128, 2, 1024), _np.float32)
    for d in range(2):
        lw2[64 * d:64 * d + 64, d] = I["rw_w2"][0, d]
        lw2[64 * d:64 * d + 64, 2 + d] = I["rw_a2"][0, d]
        w0b[:, d] = I["rw_w0"][0, d][None]
    w2 = I["w_in_2"]
    arrays = {
        "x": cm(_np.concatenate([I["ctx"][0], I["x"][0]], axis=0)),
        "mem": cm(I["mem_2"][0]),
        "con": con, "rc": rc, "ac": ac, "bc": bc, "par": par, "lw2": lw2, "w0b": w0b,
        "ada": _np.ascontiguousarray(I["ada_w"].reshape(2, 4, 2, 128, 6, 512).transpose(0, 4, 1, 3, 2, 5)),
        "rw_in": wb(I["rw_in"][0]), "rw_out": wb(I["rw_out"][0]),
        "da_in": wb(I["da_in"][0]), "da_out": wb(I["da_out"][0]),
        "w_in2": wb(w2), "w_out2": wb(I["w_out_2"]), "w_mkv": wb(I["w_mem_kv_2"]),
    }
    nc = _bacc.Bacc("TRN2", target_bir_lowering=False, num_devices=1)
    T, feed = {}, {}
    for k, a in arrays.items():
        a = _np.ascontiguousarray(a)
        feed["in_" + k] = a
        T[k] = nc.dram_tensor("in_" + k, a.shape, _mybir.dt.float32, kind="ExternalInput").ap()
    for k, shape in (("str", (8, 6, 128, 7, 128)), ("bg", (8, 128, 2, 768)), ("sg", (2, 6, 128, 1024)),
                     ("y", (128, 8, 768))):
        T[k] = nc.dram_tensor("s_" + k + "_dram", shape, _mybir.dt.float32, kind="Internal").ap()
    T["x1"] = nc.dram_tensor("x1s", (128, 8, 768), _mybir.dt.float32, kind="Internal").ap()
    T["out"] = nc.dram_tensor("out_x", (128, 8, 512), _mybir.dt.float32, kind="ExternalOutput").ap()
    build(nc, T)
    r = _run(nc, [feed], core_ids=[0])
    o = r.results[0]["out_x"]
    return _np.ascontiguousarray(_np.asarray(o).transpose(2, 1, 0).reshape(1, 512, 1024))
```
